# Optimizing a Trainium2 kernel written in Bass

```python
import math
import jax, jax.numpy as jnp
from jax import lax
import numpy as np

D_MODEL = 1024
BATCH = 1
SEQ = 512
DEPTH = 1
DEC_BATCH = 1
DEC_SEQ = 512
PAST_LEN = 128

N_HEADS = 8
N_KV_HEADS = 2
Q_GROUP = N_HEADS // N_KV_HEADS
HEAD_DIM = 64
WINDOW = 128
ATTN_BLOCK = 128
ATTN_WIDTH = N_HEADS * HEAD_DIM
KV_WIDTH = N_KV_HEADS * HEAD_DIM
N_FOURIER_GROUPS = 8
FOURIER_GROUP_DIM = 64
FOURIER_WIDTH = N_FOURIER_GROUPS * FOURIER_GROUP_DIM
N_BRANCHES = 2
IN_WIDTH = FOURIER_WIDTH + ATTN_WIDTH + 2 * KV_WIDTH + N_BRANCHES * D_MODEL
PEER_HEADS = 8
PEER_NKEYS = 128
PEER_N_EXPERTS = PEER_NKEYS * PEER_NKEYS
PEER_TOPK = 16
PEER_KEY_DIM = 128
PEER_CHUNK = 128
PLE_DIM = 256
DEEPNORM_ALPHA = (2 * DEPTH) ** 0.25
DEEPNORM_BETA = (8 * DEPTH) ** -0.25
LN_EPS = 1e-5
NEG_INF = -1e30

kernel_name = 'hybrid_fnet_swa_peer_encoder'

def layer_norm(x, g, b):
    xf = x.astype(jnp.float32)
    mu = jnp.mean(xf, axis=-1, keepdims=True)
    var = jnp.mean(jnp.square(xf - mu), axis=-1, keepdims=True)
    y = (xf - mu) * lax.rsqrt(var + LN_EPS) * g.astype(jnp.float32) + b.astype(jnp.float32)
    return y.astype(x.dtype)

def alibi_slopes():
    h = jnp.arange(1, N_HEADS + 1, dtype=jnp.float32)
    return jnp.exp2(-8.0 * h / N_HEADS)

def fourier_mix(f):
    B, S, _ = f.shape
    fg = f.reshape(B, S, N_FOURIER_GROUPS, FOURIER_GROUP_DIM).astype(jnp.float32)
    out = jnp.fft.fftn(fg, axes=(1, 3), norm='ortho').real
    return out.reshape(B, S, FOURIER_WIDTH).astype(f.dtype)

def window_attention(q, k, v, sink):
    B, S, _ = q.shape
    nb = S // ATTN_BLOCK
    f32 = jnp.float32
    qb = q.reshape(B, nb, ATTN_BLOCK, N_KV_HEADS, Q_GROUP, HEAD_DIM).astype(f32)

    def neighbours(t):
        tp = jnp.pad(t.reshape(B, S, N_KV_HEADS, HEAD_DIM).astype(f32),
                     ((0, 0), (ATTN_BLOCK, ATTN_BLOCK), (0, 0), (0, 0)))
        tp = tp.reshape(B, nb + 2, ATTN_BLOCK, N_KV_HEADS, HEAD_DIM)
        return jnp.concatenate([tp[:, :-2], tp[:, 1:-1], tp[:, 2:]], axis=2)

    kb = neighbours(k)
    vb = neighbours(v)
    s = jnp.einsum('bnqkgd,bnskd->bnkgqs', qb, kb) * (HEAD_DIM ** -0.5)
    qi = jnp.arange(ATTN_BLOCK)
    kj = jnp.arange(3 * ATTN_BLOCK)
    rel = qi[:, None] + ATTN_BLOCK - kj[None, :]
    kpos = (jnp.arange(nb)[:, None] - 1) * ATTN_BLOCK + kj[None, :]
    valid = (jnp.abs(rel) <= WINDOW)[None] & ((kpos >= 0) & (kpos < S))[:, None, :]
    slopes = alibi_slopes().reshape(N_KV_HEADS, Q_GROUP)
    bias = -slopes[:, :, None, None] * jnp.abs(rel).astype(f32)[None, None]
    bias = jnp.where(valid[:, None, None], bias[None], NEG_INF)
    s = s + bias[None]
    sk = sink.astype(f32).reshape(N_KV_HEADS, Q_GROUP)[None, None, :, :, None]
    m = jnp.maximum(jnp.max(s, axis=-1), sk)
    pr = jnp.exp(s - m[..., None])
    denom = jnp.sum(pr, axis=-1) + jnp.exp(sk - m)
    o = jnp.einsum('bnkgqs,bnskd->bnkgqd', pr, vb) / denom[..., None]
    return o.transpose(0, 1, 4, 2, 3, 5).reshape(B, S, ATTN_WIDTH).astype(q.dtype)

def peer(x, w_q, keys, u, v):
    B, S, D = x.shape
    f32 = jnp.float32
    xt = x.reshape(-1, PEER_CHUNK, D)

    def chunk(xc):
        C = xc.shape[0]
        qh = (xc @ w_q).reshape(C, PEER_HEADS, 2, PEER_KEY_DIM).astype(f32)
        sc = jnp.einsum('chpd,hpnd->chpn', qh, keys.astype(f32))
        s1, i1 = lax.top_k(sc[:, :, 0], PEER_TOPK)
        s2, i2 = lax.top_k(sc[:, :, 1], PEER_TOPK)
        cand = (s1[..., :, None] + s2[..., None, :]).reshape(C, PEER_HEADS, PEER_TOPK * PEER_TOPK)
        cidx = (i1[..., :, None] * PEER_NKEYS + i2[..., None, :]).reshape(C, PEER_HEADS, PEER_TOPK * PEER_TOPK)
        fs, fi = lax.top_k(cand, PEER_TOPK)
        eidx = jnp.take_along_axis(cidx, fi, axis=-1)
        gate = jax.nn.softmax(fs, axis=-1)
        ue = u[eidx].astype(f32)
        act = jax.nn.gelu(jnp.einsum('cd,chkd->chk', xc.astype(f32), ue), approximate=False)
        ve = v[eidx].astype(f32)
        return jnp.einsum('chk,chkd->cd', gate * act, ve).astype(x.dtype)

    return lax.map(chunk, xt).reshape(B, S, D)

def encoder_layer(x, p, w_in, sink, w_fo, w_ao, w_out, ln1_g, ln1_b,
                  pq, pkeys, pu, pv, ple_wg, ple_wp, ln2_g, ln2_b):
    h = x @ w_in
    o0 = FOURIER_WIDTH
    o1 = o0 + ATTN_WIDTH
    o2 = o1 + KV_WIDTH
    o3 = o2 + KV_WIDTH
    f_in, q, k, v, g = h[..., :o0], h[..., o0:o1], h[..., o1:o2], h[..., o2:o3], h[..., o3:]
    f_branch = fourier_mix(f_in) @ w_fo
    a_branch = window_attention(q, k, v, sink) @ w_ao
    gates = jax.nn.sigmoid(g.astype(jnp.float32)).astype(x.dtype)
    merged = gates[..., :D_MODEL] * f_branch + gates[..., D_MODEL:] * a_branch
    x = layer_norm(DEEPNORM_ALPHA * x + merged @ w_out, ln1_g, ln1_b)
    cm = peer(x, pq, pkeys, pu, pv)
    ple = jax.nn.sigmoid((x @ ple_wg).astype(jnp.float32)).astype(x.dtype) * (p @ ple_wp)
    return layer_norm(DEEPNORM_ALPHA * x + cm + ple, ln2_g, ln2_b)

def trunk(x, p_all, emb_ln_g, emb_ln_b, w_in, attn_sink, w_fourier_out, w_attn_out, w_out,
          ln1_g, ln1_b, peer_w_q, peer_keys, peer_u, peer_v, ple_w_gate, ple_w_proj, ln2_g, ln2_b):
    x = layer_norm(x, emb_ln_g, emb_ln_b)
    for i in range(DEPTH):
        x = encoder_layer(x, p_all[i], w_in[i], attn_sink[i], w_fourier_out[i], w_attn_out[i],
                          w_out[i], ln1_g[i], ln1_b[i], peer_w_q[i], peer_keys[i], peer_u[i],
                          peer_v[i], ple_w_gate[i], ple_w_proj[i], ln2_g[i], ln2_b[i])
    return x

def setup_inputs(seed: int = 0) -> dict:
    key = jax.random.key(seed)
    ks = jax.random.split(key, 24)
    f32 = jnp.float32

    def nrm(k, shape, scale):
        return jax.random.normal(k, shape, f32) * scale

    return {
        'x_prompt': nrm(ks[0], (BATCH, SEQ, D_MODEL), 1.0),
        'x_sample': nrm(ks[1], (DEC_BATCH, DEC_SEQ, D_MODEL), 1.0),
        'p_prompt': nrm(ks[2], (DEPTH, BATCH, SEQ, PLE_DIM), 1.0),
        'p_sample': nrm(ks[3], (DEPTH, DEC_BATCH, DEC_SEQ, PLE_DIM), 1.0),
        'emb_ln_g': 1.0 + nrm(ks[4], (D_MODEL,), 0.02),
        'emb_ln_b': nrm(ks[5], (D_MODEL,), 0.02),
        'w_in': nrm(ks[6], (DEPTH, D_MODEL, IN_WIDTH), D_MODEL ** -0.5),
        'attn_sink': nrm(ks[7], (DEPTH, N_HEADS), 1.0),
        'w_fourier_out': nrm(ks[8], (DEPTH, FOURIER_WIDTH, D_MODEL), FOURIER_WIDTH ** -0.5),
        'w_attn_out': nrm(ks[9], (DEPTH, ATTN_WIDTH, D_MODEL), ATTN_WIDTH ** -0.5),
        'w_out': nrm(ks[10], (DEPTH, D_MODEL, D_MODEL), DEEPNORM_BETA * D_MODEL ** -0.5),
        'ln1_g': 1.0 + nrm(ks[11], (DEPTH, D_MODEL), 0.02),
        'ln1_b': nrm(ks[12], (DEPTH, D_MODEL), 0.02),
        'peer_w_q': nrm(ks[13], (DEPTH, D_MODEL, PEER_HEADS * 2 * PEER_KEY_DIM), D_MODEL ** -0.5),
        'peer_keys': nrm(ks[14], (DEPTH, PEER_HEADS, 2, PEER_NKEYS, PEER_KEY_DIM), PEER_KEY_DIM ** -0.5),
        'peer_u': nrm(ks[15], (DEPTH, PEER_N_EXPERTS, D_MODEL), D_MODEL ** -0.5),
        'peer_v': nrm(ks[16], (DEPTH, PEER_N_EXPERTS, D_MODEL), DEEPNORM_BETA),
        'ple_w_gate': nrm(ks[17], (DEPTH, D_MODEL, D_MODEL), D_MODEL ** -0.5),
        'ple_w_proj': nrm(ks[18], (DEPTH, PLE_DIM, D_MODEL), DEEPNORM_BETA * PLE_DIM ** -0.5),
        'ln2_g': 1.0 + nrm(ks[19], (DEPTH, D_MODEL), 0.02),
        'ln2_b': nrm(ks[20], (DEPTH, D_MODEL), 0.02),
    }

def reference(x_prompt, x_sample, p_prompt, p_sample, emb_ln_g, emb_ln_b, w_in, attn_sink,
              w_fourier_out, w_attn_out, w_out, ln1_g, ln1_b, peer_w_q, peer_keys, peer_u,
              peer_v, ple_w_gate, ple_w_proj, ln2_g, ln2_b):
    y_prompt = trunk(x_prompt, p_prompt, emb_ln_g, emb_ln_b, w_in, attn_sink, w_fourier_out,
                     w_attn_out, w_out, ln1_g, ln1_b, peer_w_q, peer_keys, peer_u, peer_v,
                     ple_w_gate, ple_w_proj, ln2_g, ln2_b)
    y_sample = trunk(x_sample, p_sample, emb_ln_g, emb_ln_b, w_in, attn_sink, w_fourier_out,
                     w_attn_out, w_out, ln1_g, ln1_b, peer_w_q, peer_keys, peer_u, peer_v,
                     ple_w_gate, ple_w_proj, ln2_g, ln2_b)
    return (y_prompt, y_sample)


_drawn_inputs = setup_inputs


def setup_inputs(seed=0):
    import zlib

    import numpy as np

    out = dict(_drawn_inputs(seed))
    spreads = {}
    factors = {'attn_sink': 6.114, 'ln2_g': 2.835, 'ln2_b': 2.949}
    for name, (base, spread) in spreads.items():
        noise = np.random.default_rng([zlib.crc32(name.encode()), seed]).standard_normal(out[name].shape)
        drawn = base * np.exp(spread * noise) if base else spread * noise
        out[name] = __import__('jax').numpy.asarray(drawn.astype(out[name].dtype))
    for name, factor in factors.items():
        out[name] = (out[name] * factor).astype(out[name].dtype)
    return out
```

```python
from contextlib import ExitStack

import concourse.bass as bass
from concourse import mybir

F32 = mybir.dt.float32
F32R = mybir.dt.float32r
BF16 = mybir.dt.bfloat16
U32 = mybir.dt.uint32
ALU = mybir.AluOpType
ACT = mybir.ActivationFunctionType
AX_X = mybir.AxisListType.X

P = 128
SEQS = 2
T = 512
NT = T // P
D = 1024
KD = D // P
HEADS, KV_HEADS, HEAD_DIM = 8, 2, 64
Q_GROUP = HEADS // KV_HEADS
WINDOW = 128
FOURIER = 512
FT = FOURIER // P
GROUP_DIM = 64
PEER_HEADS, NKEYS, TOPK = 8, 128, 16
SIDES = 2 * PEER_HEADS
HK = PEER_HEADS * TOPK
PLE = 256
ALPHA = 2 ** 0.25
LN_EPS = 1e-5
NEG_INF = -1e30
LOWEST = -3.0e38

FQK_TILES = FT + FT + KV_HEADS
V_TILE = FQK_TILES
MERGE_AT = V_TILE + 1
OUT_AT = MERGE_AT + 3 * KD
QUERY_AT = OUT_AT + KD
PLE_AT = QUERY_AT + SIDES
LAYER_TILES = PLE_AT + 2 * (KD // 2 + 1)
EXPERT_TILES = NKEYS
STREAM = LAYER_TILES + EXPERT_TILES

GROUP = 4
GROUPS = EXPERT_TILES // GROUP
OUTS = NT * 2

UNITS = NT * KV_HEADS
BATCH = 8
BATCHES = P // BATCH


def key_tiles(blk):
    return [b for b in (blk - 1, blk, blk + 1) if 0 <= b < NT]


def encoder(nc, x, p_t, weights, u_t, v_rows, keys_t, sink, emb_g, emb_b, ln1_g, ln1_b, ln2_g, ln2_b,
            identity, key_iota, group_dft, token_dft, attn_bias, out):
    ln_params = [(emb_g, emb_b), (ln1_g, ln1_b), (ln2_g, ln2_b)]
    with ExitStack() as ctx:
        def sb(name, shape, dt=F32, scope=ctx):
            return scope.enter_context(nc.sbuf_tensor(name, shape, dt))

        def sem(name):
            return ctx.enter_context(nc.semaphore(name))

        g_dram = nc.dram_tensor("g_dram", (SEQS, NKEYS, P, T), F32, kind="Internal").ap()

        ident = sb("ident", [P, P])
        iota_bf = sb("iota_bf", [P, P], BF16)
        iota = sb("iota", [P, P])
        sinks = sb("sinks", [P, HEADS])
        resid = sb("resid", [P, NT, D])
        ln_gb = sb("ln_gb", [P, 2, D])
        w_raw = sb("w_raw", [P, 2, D])
        w_hi = sb("w_hi", [P, 2, D], F32R)
        w_lo = sb("w_lo", [P, 2, D], F32R)
        xt_hi = sb("xt_hi", [P, KD, T], F32R)
        xt_lo = sb("xt_lo", [P, KD, T], F32R)
        bn = sb("bn", [P, NT, 2, 6])
        mv = sb("mv", [P, NT, 2])
        var_eps = sb("var_eps", [P, NT])
        std = sb("std", [P, NT])
        rstd = sb("rstd", [P, NT])

        with ExitStack() as mix:
            fm_hi = sb("fm_hi", [P, FT, T], F32R, mix)
            fm_lo = sb("fm_lo", [P, FT, T], F32R, mix)
            o_hi = sb("o_hi", [P, FT, T], F32R, mix)
            o_lo = sb("o_lo", [P, FT, T], F32R, mix)
            with ExitStack() as four:
                pq = sb("pq", [P, NT, 2, FOURIER], F32, four)
                dft = sb("dft", [P, 2, NT, T], F32, four)
            m_hi = sb("m_hi", [P, KD, T], F32R, mix)
            m_lo = sb("m_lo", [P, KD, T], F32R, mix)
            gdft = sb("gdft", [P, 2 * P], F32, mix)
            with ExitStack() as att:
                fqk = sb("fqk", [P, FQK_TILES, T], F32, att)
                v_dup = sb("v_dup", [P, NT, KV_HEADS, 2, HEAD_DIM], F32, att)
                bias = sb("bias", [P, HEADS, 3 * P], F32, att)
                probs = sb("probs", [P, 2, Q_GROUP, 3 * P], F32, att)
                probs_t = sb("probs_t", [P, 3, Q_GROUP * P], F32, att)
                row_max = sb("row_max", [P, 2, Q_GROUP], F32, att)
                neg_max = sb("neg_max", [P, 2, Q_GROUP], F32, att)
                sink_ex = sb("sink_ex", [P, 2, Q_GROUP], F32, att)
                row_sum = sb("row_sum", [P, 2, Q_GROUP], F32, att)
                row_inv = sb("row_inv", [P, 2, Q_GROUP], F32, att)
            with ExitStack() as mrg:
                sig = sb("sig", [P, 2, 2, T], F32, mrg)
                gated = sb("gated", [P, 2, 2, T], F32, mrg)
                merged = sb("merged", [P, 2, T], F32, mrg)

        with ExitStack() as route:
            all_t = sb("all_t", [P, 3, T], F32, route)
            part = sb("part", [P, T], F32, route)
            gate_parts = sb("gate_parts", [P, 3, T], F32, route)
            gate_bf = sb("gate_bf", [P, 3, T], BF16, route)
            with ExitStack() as choice:
                score = sb("score", [P, NT, SIDES, NKEYS], F32, choice)
                with ExitStack() as query:
                    keys = sb("keys", [P, SIDES, NKEYS], F32, query)
                    q_t = sb("q_t", [P, 2, T], F32, query)
                    pt_raw = sb("pt_raw", [P, 2, T], F32, query)
                    pt_hi = sb("pt_hi", [P, 2, T], F32R, query)
                    pt_lo = sb("pt_lo", [P, 2, T], F32R, query)
                    sig_p = sb("sig_p", [P, NT, T], F32, query)
                    ple_t = sb("ple_t", [P, NT, T], F32, query)
                with ExitStack() as pick:
                    tile_sc = sb("tile_sc", [P, SIDES, NKEYS], F32, pick)
                    rest_sc = sb("rest_sc", [P, SIDES, NKEYS], F32, pick)
                    pair_sc = sb("pair_sc", [P, PEER_HEADS, TOPK * TOPK], F32, pick)
                    chosen = sb("chosen", [P, 3, HK], F32, pick)
                    top_v = sb("top_v", [P, SIDES, TOPK], F32, pick)
                    top_i = sb("top_i", [P, SIDES, TOPK], U32, pick)
                    top_f = sb("top_f", [P, SIDES, TOPK], F32, pick)
                    fin_v = sb("fin_v", [P, PEER_HEADS, TOPK], F32, pick)
                    fin_i = sb("fin_i", [P, HK], U32, pick)
                    pos_i = sb("pos_i", [P, 2, HK], U32, pick)
                    pos_f = sb("pos_f", [P, 2, HK], F32, pick)
                    gate_x = sb("gate_x", [P, PEER_HEADS, TOPK], F32, pick)
                    gate_e = sb("gate_e", [P, PEER_HEADS, TOPK], F32, pick)
                    gate_s = sb("gate_s", [P, PEER_HEADS], F32, pick)
                    gate_r = sb("gate_r", [P, PEER_HEADS], F32, pick)
            with ExitStack() as spread:
                g_tile = sb("g_tile", [P, NKEYS, P], F32, spread)
                onehot = sb("onehot", [P, 2, BATCH, 4, P], BF16, spread)
                cols = sb("cols", [P, 2, 5, BATCH], F32, spread)

        with ExitStack() as dense:
            vw_raw = sb("vw_raw", [P, 2, D], F32, dense)
            vw_hi = sb("vw_hi", [P, 2, GROUP, D], F32R, dense)
            vw_lo = sb("vw_lo", [P, 2, GROUP, D], F32R, dense)
            a_hi = sb("a_hi", [P, 2, GROUP, T], F32R, dense)
            a_lo = sb("a_lo", [P, 2, GROUP, T], F32R, dense)
            g_in = sb("g_in", [P, 2, T], F32, dense)
            act_t = sb("act_t", [P, 2, T], F32, dense)
            ga = sb("ga", [P, 2, T], F32, dense)
        ps = ctx.enter_context(nc.psum_tensor("ps", [P, 8, T], F32))

        consts_in, mix_in, keys_in, pt_in = sem("consts_in"), sem("mix_in"), sem("keys_in"), sem("pt_in")
        x_in = [sem(f"x_in{tt}") for tt in range(NT)]
        gb_in = sem("gb_in")
        stored = [sem(f"stored{tt}") for tt in range(NT)]
        w_in = [sem(f"w_in{k}") for k in range(2)]
        w_hi_made = sem("w_hi_made")
        w_lo_made = sem("w_lo_made")
        w_used = sem("w_used")
        var_made, std_made, ln_done, scaled = sem("var_made"), sem("std_made"), sem("ln_done"), sem("scaled")
        xt_ps, xt_hi_made, xt_lo_made = sem("xt_ps"), sem("xt_hi_made"), sem("xt_lo_made")
        fqk_copied = sem("fqk_copied")
        v_copied = sem("v_copied")
        pq_ps, pq_copied, fm_ps, fm_hi_made, fm_lo_made = (
            sem("pq_ps"), sem("pq_copied"), sem("fm_ps"), sem("fm_hi_made"), sem("fm_lo_made"))
        sc_ps, sc_copied, max_made, exp_made, probs_made = (
            sem("sc_ps"), sem("sc_copied"), sem("max_made"), sem("exp_made"), sem("probs_made"))
        pt_ps, pt_copied, o_ps, o_hi_made, o_lo_made = (
            sem("pt_ps"), sem("pt_copied"), sem("o_ps"), sem("o_hi_made"), sem("o_lo_made"))
        sig_made, merged_made, m_hi_made = sem("sig_made"), sem("merged_made"), sem("m_hi_made")
        m_lo_made = sem("m_lo_made")
        mixed = sem("mixed")
        q_copied = sem("q_copied")
        key_ps = sem("key_ps")
        key_copied = sem("key_copied")
        pt_hi_made, pt_lo_made, sig_p_made, ple_added = (
            sem("pt_hi_made"), sem("pt_lo_made"), sem("sig_p_made"), sem("ple_added"))
        tile_copied, tile_done = sem("tile_copied"), sem("tile_done")
        gate_x_made, gate_e_made, chosen_made = sem("gate_x_made"), sem("gate_e_made"), sem("chosen_made")
        chosen_ps, chosen_copied = sem("chosen_ps"), sem("chosen_copied")
        onehot_made = sem("onehot_made")
        onehot_used = sem("onehot_used")
        g_copied = sem("g_copied")
        g_stored = sem("g_stored")
        act_made = sem("act_made")
        ga_made = sem("ga_made")
        a_hi_made, a_lo_made = sem("a_hi_made"), sem("a_lo_made")
        g_in_sem = [sem(f"g_in{k}") for k in range(2)]
        v_in = [sem(f"v_in{k}") for k in range(2)]
        v_hi_made = sem("v_hi_made")
        v_lo_made = sem("v_lo_made")
        outs_ps = sem("outs_ps")
        outs_added = sem("outs_added")

        block = ctx.enter_context(nc.Block())

        def cols_of(tt):
            return slice(tt * P, (tt + 1) * P)

        def slot_free(m):
            return m + 1

        def made(m):
            return m + 3

        def landed(m, slot):
            return 8 * (m - slot) + 16

        @block.sync
        def _(sp):
            def load_w(m, slot, source):
                sp.wait_ge(w_lo_made, slot_free(m))
                sp.dma_start(w_raw[:, slot, :], source).then_inc(w_in[slot], 16)

            def load_layer(s, first, last):
                pairs = (last - first) // 2
                with sp.Fori(0, pairs) as i:
                    for j in range(2):
                        m = s * STREAM + first + j
                        load_w(2 * i + m, m % 2, weights[bass.ds(2 * i + first + j, 1), :, :].rearrange("a p n -> (a p) n"))
                if (last - first) % 2:
                    m = s * STREAM + last - 1
                    load_w(m, m % 2, weights[last - 1])

            def load_ln(s, which):
                use = 3 * s + which
                if use:
                    sp.wait_ge(ln_done, NT * use)
                g, b = ln_params[which]
                for k, row in enumerate((g, b)):
                    sp.dma_start(ln_gb[:, k, :], row.rearrange("(a n) -> a n", a=1).to_broadcast([P, D])).then_inc(gb_in, 16)

            def load_u(s, n, slot):
                load_w(s * STREAM + LAYER_TILES + n, slot, u_t[bass.ds(n, 1), :, :].rearrange("a p n -> (a p) n"))

            def load_gates(s, n, slot):
                sp.wait_ge(ga_made, s * EXPERT_TILES + n + 1)
                sp.dma_start(g_in[:, slot, :], g_dram[s, bass.ds(n, 1), :, :].rearrange("a p n -> (a p) n")).then_inc(g_in_sem[slot], 16)

            def load_v(s, n, slot):
                sp.wait_ge(v_lo_made, s * EXPERT_TILES + n + 1)
                sp.dma_start(vw_raw[:, slot, :], v_rows[bass.ds(n * P, P), :]).then_inc(v_in[slot], 16)

            sp.dma_start(ident[:], identity).then_inc(consts_in, 16)
            sp.dma_start(iota[:], key_iota).then_inc(consts_in, 16)
            sp.dma_start(sinks[:], sink.to_broadcast([P, HEADS])).then_inc(consts_in, 16)
            for s in range(SEQS):
                base = s * STREAM
                for tt in range(NT):
                    if s:
                        sp.wait_ge(stored[tt], 16 * s)
                    sp.dma_start(resid[:, tt, :], x[s, cols_of(tt), :]).then_inc(x_in[tt], 16)
                load_ln(s, 0)
                load_layer(s, 1 if s else 0, 4)
                if s:
                    sp.wait_ge(outs_added, 4 + s * OUTS * GROUPS)
                sp.dma_start(gdft[:], group_dft).then_inc(mix_in, 16)
                sp.dma_start(dft[:], token_dft.rearrange("c (t p) n -> p c t n", p=P)).then_inc(mix_in, 16)
                sp.dma_start(bias[:], attn_bias).then_inc(mix_in, 16)
                load_layer(s, 4, MERGE_AT)
                load_ln(s, 1)
                load_layer(s, MERGE_AT, QUERY_AT + 2)
                sp.wait_ge(w_used, made(base + QUERY_AT - 1))
                sp.wait_ge(m_lo_made, 2 + KD * (s + 1))
                sp.dma_start(keys[:], keys_t).then_inc(keys_in, 16)
                sp.dma_start(pt_raw[:], p_t[s]).then_inc(pt_in, 16)
                load_layer(s, QUERY_AT + 2, LAYER_TILES)
                load_u(s, 0, (base + LAYER_TILES) % 2)
                load_ln(s, 2)
                for tt in range(NT):
                    sp.wait_ge(g_copied, 4 + 2 * BATCHES * (s * NT + tt + 1))
                    sp.dma_start(g_dram[s, :, :, cols_of(tt)].rearrange("i j t -> j i t"), g_tile[:]).then_inc(g_stored, 16)
                sp.wait_ge(g_stored, 16 * NT * (s + 1))
                def load_group(g, last=False):
                    for e in range(GROUP):
                        n = g * GROUP + e
                        load_gates(s, n, e % 2)
                        if not last or e < GROUP - 1:
                            load_u(s, n + 1, (base + LAYER_TILES + e + 1) % 2)
                        elif s + 1 < SEQS:
                            load_w(base + STREAM, (base + STREAM) % 2, weights[0])
                    for e in range(GROUP):
                        load_v(s, g * GROUP + e, e % 2)
                with sp.Fori(0, GROUPS - 1) as g:
                    load_group(g)
                load_group(GROUPS - 1, last=True)
                for tt in range(NT):
                    sp.wait_ge(ln_done, NT * (3 * s + 2) + tt + 1)
                    sp.dma_start(out[s, cols_of(tt), :], resid[:, tt, :]).then_inc(stored[tt], 16)
            for tt in range(NT):
                sp.wait_ge(stored[tt], 16 * SEQS)

        @block.scalar
        def _(act):
            act.sem_inc(fqk_copied, 2)
            act.sem_inc(q_copied, 2)
            act.sem_inc(g_copied, 4)
            act.sem_inc(act_made, 2)

            def split_w(m, slot):
                act.wait_ge(w_in[slot], landed(m, slot))
                act.wait_ge(w_used, slot_free(m))
                act.activation(w_hi[:, slot, :], w_raw[:, slot, :], ACT.Copy).then_inc(w_hi_made, 1)

            def norm(use):
                act.wait_ge(var_made, use + 1)
                act.activation(std[:], var_eps[:], ACT.Sqrt).then_inc(std_made, 1)

            def turn(use):
                for n in range(2 * NT):
                    act.wait_ge(xt_ps, 2 * NT * use + n + 1)
                    act.activation(xt_hi[:, 4 * (n % 2):4 * (n % 2) + 4, cols_of(n // 2)],
                                   ps[:, n % 4, :].rearrange("p (k t) -> p k t", k=4), ACT.Copy).then_inc(xt_hi_made, 1)

            for s in range(SEQS):
                base = s * STREAM
                if s == 0:
                    split_w(0, 0)
                norm(3 * s)
                turn(2 * s)
                with act.Fori(0, FQK_TILES // 2) as i:
                    for j in range(2):
                        m = base + j
                        split_w(2 * i + m + 1, (m + 1) % 2)
                        act.wait_ge(w_used, made(2 * i + m))
                        act.activation(fqk[:, bass.ds(2 * i + j, 1), :].rearrange("p a t -> p (a t)"), ps[:, 4 + j, :], ACT.Copy).then_inc(fqk_copied, 1)
                split_w(base + V_TILE + 1, (base + V_TILE + 1) % 2)
                for n in range(2 * NT):
                    tt, ch = n // 2, n % 2
                    act.wait_ge(pq_ps, 2 * NT * s + n + 1)
                    act.activation(pq[:, tt, :, 256 * ch:256 * ch + 256].rearrange("p q (c f) -> p c q f", c=2),
                                   ps[:, n % 4, :].rearrange("p (c q f) -> p c q f", c=2, q=2), ACT.Copy).then_inc(pq_copied, 1)
                for c in range(FT):
                    act.wait_ge(fm_ps, FT * s + c + 1)
                    act.activation(fm_hi[:, c, :], ps[:, 4 + c % 2, :], ACT.Copy).then_inc(fm_hi_made, 1)

                def exps(u):
                    w = P * len(key_tiles(u // 2))
                    act.wait_ge(max_made, UNITS * s + u + 1)
                    for h in range(Q_GROUP):
                        act.activation(probs[:, u % 2, h, 0:w], probs[:, u % 2, h, 0:w], ACT.Exp,
                                       bias=neg_max[:, u % 2, h:h + 1], accum_out=row_sum[:, u % 2, h:h + 1])
                    act.activation(sink_ex[:, u % 2, :], sink_ex[:, u % 2, :], ACT.Exp).then_inc(exp_made, 1)

                def outputs_hi(u):
                    g, blk = u % 2, u // 2
                    act.wait_ge(o_ps, UNITS * s + u + 1)
                    for half in range(2):
                        rows = slice(64 * half, 64 * half + 64)
                        act.activation(o_hi[rows, 2 * g:2 * g + 2, cols_of(blk)],
                                       ps[rows, 7, :].rearrange("p (a b q) -> p a b q", a=2, b=2)[:, :, half, :], ACT.Copy).then_inc(o_hi_made, 1)

                exps(0)
                for u in range(UNITS):
                    if u + 1 < UNITS:
                        exps(u + 1)
                    act.wait_ge(pt_ps, UNITS * s + u + 1)
                    if u:
                        act.wait_ge(o_ps, UNITS * s + u)
                    nk = len(key_tiles(u // 2))
                    for k in range(nk):
                        a = act.activation(probs_t[:, k, :], ps[:, 4 + k, :], ACT.Copy)
                    a.then_inc(pt_copied, 1)
                    outputs_hi(u)

                with act.Fori(0, KD // 2) as i:
                    for j in range(2):
                        m = base + MERGE_AT + 3 * j
                        for gate in range(2):
                            split_w(6 * i + m + gate + 1, (m + gate + 1) % 2)
                            act.wait_ge(w_used, made(6 * i + m + gate))
                            if gate == 0:
                                act.wait_ge(m_lo_made, s * KD + 2 * i + j + 1)
                            act.activation(sig[:, j, gate, :], ps[:, 4 * j + gate, :], ACT.Sigmoid).then_inc(sig_made, 1)
                        split_w(6 * i + m + 3, (m + 3) % 2)
                        act.wait_ge(merged_made, s * KD + 2 * i + j + 1)
                        act.activation(m_hi[:, bass.ds(2 * i + j, 1), :].rearrange("p a t -> p (a t)"), merged[:, j, :], ACT.Copy).then_inc(m_hi_made, 1)
                for m in range(base + OUT_AT, base + QUERY_AT):
                    split_w(m + 1, (m + 1) % 2)
                norm(3 * s + 1)
                turn(2 * s + 1)

                def query(n, j):
                    m = base + QUERY_AT + j
                    split_w(m + 1 + n, (m + 1) % 2)
                    act.wait_ge(w_used, made(m + n))
                    act.wait_ge(key_ps, SIDES * s + n + j + 1)
                    act.activation(q_t[:, j, :], ps[:, 4 + j, :], ACT.Copy).then_inc(q_copied, 1)
                act.wait_ge(keys_in, 16 * (s + 1))
                with act.Fori(0, SIDES // 2) as i:
                    for j in range(2):
                        query(2 * i, j)
                act.wait_ge(pt_in, 16 * (s + 1))
                act.activation(pt_hi[:], pt_raw[:], ACT.Copy).then_inc(pt_hi_made, 1)
                for half in range(2):
                    m = base + PLE_AT + 5 * half
                    for k in range(5):
                        split_w(m + k + 1, (m + k + 1) % 2)
                        if k == 3:
                            act.wait_ge(w_used, made(m + k))
                            if half:
                                act.wait_ge(ple_added, 2 * s + half)
                            act.activation(sig_p[:], ps[:, 0:4, :], ACT.Sigmoid).then_inc(sig_p_made, 1)
                for tt in range(NT):
                    if tt:
                        act.wait_ge(tile_done, NT * s + tt)
                    act.wait_ge(key_copied, 2 + SIDES * (s + 1))
                    if tt == 0:
                        act.wait_ge(ple_added, 2 * (s + 1))
                    act.activation(tile_sc[:], score[:, tt, :, :], ACT.Copy).then_inc(tile_copied, 1)
                    act.wait_ge(gate_x_made, NT * s + tt + 1)
                    act.activation(gate_e[:], gate_x[:], ACT.Exp).then_inc(gate_e_made, 1)
                for tt in range(NT):
                    if tt:
                        act.wait_ge(g_stored, 16 * (NT * s + tt))
                    with act.Fori(0, BATCHES // 2) as i:
                        for j in range(2):
                            for half in range(2):
                                act.wait_ge(onehot_used, 2 + s * NT * BATCHES + tt * BATCHES + 2 * i + j + 1)
                                act.activation(g_tile[:, :, bass.ds(2 * BATCH * i + BATCH * j + 4 * half, 4)].rearrange("p i t -> p t i"),
                                               ps[:, 4 + 2 * j + half, :].rearrange("p (t i) -> p t i", t=4), ACT.Copy).then_inc(g_copied, 1)

                e0 = s * EXPERT_TILES
                mu = base + LAYER_TILES

                def acts(n, first, q, last):
                    for e in range(GROUP):
                        if e < GROUP - 1:
                            split_w(mu + n + e + 1, (mu + first + e + 1) % 2)
                        act.wait_ge(w_used, made(mu + n + e))
                        act.wait_ge(ga_made, e0 + n + e + 1)
                        act.activation(act_t[:, e % 2, :], ps[:, e % 2, :], ACT.Gelu).then_inc(act_made, 1)
                        act.wait_ge(ga_made, e0 + n + e + 3)
                        if e == 0:
                            act.wait_ge(outs_ps, (s * GROUPS) * OUTS + n * 2 + OUTS)
                        act.activation(a_hi[:, q, e, :], ga[:, e % 2, :], ACT.Copy).then_inc(a_hi_made, 1)

                def split_v(n, q):
                    for e in range(GROUP):
                        act.wait_ge(v_in[e % 2], landed(e0 + n + e, e % 2))
                        if e == 0:
                            act.wait_ge(outs_ps, (s * GROUPS) * OUTS + n * 2 + OUTS)
                        act.activation(vw_hi[:, q, e, :], vw_raw[:, e % 2, :], ACT.Copy).then_inc(v_hi_made, 1)

                def group(n, q, last=False):
                    acts(n, 0, q, last)
                    split_v(n, q)
                    if not last or s + 1 < SEQS:
                        split_w(mu + n + GROUP, mu % 2)

                group(0, 0)
                with act.Fori(0, GROUPS // 2 - 1) as i:
                    for j in range(2):
                        group(2 * GROUP * i + GROUP * (1 + j), (1 + j) % 2)
                group(EXPERT_TILES - GROUP, 1, last=True)
                norm(3 * s + 2)

        @block.vector
        def _(dve):
            dve.sem_inc(w_lo_made, 2)
            dve.sem_inc(m_lo_made, 2)
            dve.sem_inc(key_copied, 2)
            dve.sem_inc(ga_made, 2)
            dve.sem_inc(v_lo_made, 2)
            dve.sem_inc(outs_added, 4)

            def split_w(m, slot):
                dve.wait_ge(w_hi_made, m + 1)
                dve.tensor_tensor(w_lo[:, slot, :], w_raw[:, slot, :], w_hi[:, slot, :].bitcast(F32), ALU.subtract).then_inc(w_lo_made, 1)

            def norm(use, s, from_dram):
                for tt in range(NT):
                    if from_dram:
                        dve.wait_ge(x_in[tt], 16 * (s + 1))
                    for half in range(2):
                        dve.bn_stats(bn[:, tt, half, :], resid[:, tt, half * T:(half + 1) * T])
                dve.drain()
                for tt in range(NT):
                    dve.bn_aggr(mv[:, tt, :], bn[:, tt, :, :].rearrange("p a b -> p (a b)"))
                dve.drain()
                dve.tensor_scalar(var_eps[:], mv[:, :, 1], LN_EPS, None, ALU.add).then_inc(var_made, 1)
                dve.wait_ge(std_made, use + 1)
                dve.reciprocal(rstd[:], std[:])
                dve.drain()
                dve.wait_ge(gb_in, 32 * (use + 1))
                for tt in range(NT):
                    dve.tensor_scalar(resid[:, tt, :], resid[:, tt, :], mv[:, tt, 0:1], rstd[:, tt:tt + 1], ALU.subtract, ALU.mult)
                    dve.drain()
                    dve.tensor_tensor(resid[:, tt, :], resid[:, tt, :], ln_gb[:, 0, :], ALU.mult)
                    dve.drain()
                    dve.tensor_tensor(resid[:, tt, :], resid[:, tt, :], ln_gb[:, 1, :], ALU.add).then_inc(ln_done, 1)

            def turn(use):
                for n in range(2 * NT):
                    dve.wait_ge(xt_hi_made, 2 * NT * use + n + 1)
                    there = (slice(None), slice(4 * (n % 2), 4 * (n % 2) + 4), cols_of(n // 2))
                    dve.tensor_tensor(xt_lo[there], ps[:, n % 4, :].rearrange("p (k t) -> p k t", k=4),
                                      xt_hi[there].bitcast(F32), ALU.subtract).then_inc(xt_lo_made, 1)

            dve.wait_ge(consts_in, 48)
            dve.tensor_copy(iota_bf[:], iota[:])
            for s in range(SEQS):
                base = s * STREAM
                if s == 0:
                    split_w(0, 0)
                norm(3 * s, s, True)
                turn(2 * s)
                with dve.Fori(0, FQK_TILES // 2) as i:
                    for j in range(2):
                        m = base + j
                        split_w(2 * i + m + 1, (m + 1) % 2)
                split_w(base + V_TILE + 1, (base + V_TILE + 1) % 2)
                dve.wait_ge(w_used, made(base + V_TILE))
                for dup in range(2):
                    dve.tensor_copy(v_dup[:, :, :, dup, :], ps[:, 6, :].rearrange("p (t g d) -> p t g d", t=NT, g=KV_HEADS)).then_inc(v_copied, 1)
                for c in range(FT):
                    dve.wait_ge(fm_hi_made, FT * s + c + 1)
                    dve.tensor_tensor(fm_lo[:, c, :], ps[:, 4 + c % 2, :], fm_hi[:, c, :].bitcast(F32), ALU.subtract).then_inc(fm_lo_made, 1)

                def scores(u):
                    g, blk = u % 2, u // 2
                    w = P * len(key_tiles(blk))
                    at = 0 if blk else P
                    dve.wait_ge(sc_ps, UNITS * s + u + 1)
                    if u >= 2:
                        dve.wait_ge(pt_ps, UNITS * s + u - 1)
                    dve.scalar_tensor_tensor(out=probs[:, u % 2, :, 0:w], in0=ps[:, 0:4, 0:w], scalar=HEAD_DIM ** -0.5,
                                             in1=bias[:, Q_GROUP * g:Q_GROUP * g + Q_GROUP, at:at + w],
                                             op0=ALU.mult, op1=ALU.add).then_inc(sc_copied, 1)
                    dve.drain()
                    dve.tensor_reduce(row_max[:, u % 2, :], probs[:, u % 2, :, 0:w], AX_X, ALU.max)
                    dve.drain()
                    sk = sinks[:, Q_GROUP * g:Q_GROUP * g + Q_GROUP]
                    dve.tensor_tensor(row_max[:, u % 2, :], row_max[:, u % 2, :], sk, ALU.max)
                    dve.drain()
                    dve.tensor_scalar(neg_max[:, u % 2, :], row_max[:, u % 2, :], -1.0, None, ALU.mult)
                    dve.tensor_tensor(sink_ex[:, u % 2, :], sk, row_max[:, u % 2, :], ALU.subtract).then_inc(max_made, 1)

                def normalise(u):
                    w = P * len(key_tiles(u // 2))
                    dve.wait_ge(exp_made, UNITS * s + u + 1)
                    dve.tensor_tensor(row_inv[:, u % 2, :], row_sum[:, u % 2, :], sink_ex[:, u % 2, :], ALU.add)
                    dve.drain()
                    dve.reciprocal(row_inv[:, u % 2, :], row_inv[:, u % 2, :])
                    dve.drain()
                    for h in range(Q_GROUP):
                        d = dve.tensor_scalar(probs[:, u % 2, h, 0:w], probs[:, u % 2, h, 0:w], row_inv[:, u % 2, h:h + 1], None, ALU.mult)
                    d.then_inc(probs_made, 1)

                def outputs_lo(u):
                    g, blk = u % 2, u // 2
                    dve.wait_ge(o_hi_made, 2 * (UNITS * s + u + 1))
                    for half in range(2):
                        rows = slice(64 * half, 64 * half + 64)
                        dve.tensor_tensor(o_lo[rows, 2 * g:2 * g + 2, cols_of(blk)],
                                          ps[rows, 7, :].rearrange("p (a b q) -> p a b q", a=2, b=2)[:, :, half, :],
                                          o_hi[rows, 2 * g:2 * g + 2, cols_of(blk)].bitcast(F32), ALU.subtract).then_inc(o_lo_made, 1)

                dve.wait_ge(mix_in, 48 * (s + 1))
                scores(0)
                for u in range(UNITS):
                    if u + 1 < UNITS:
                        scores(u + 1)
                    normalise(u)
                    outputs_lo(u)

                with dve.Fori(0, KD // 2) as i:
                    for j in range(2):
                        m = base + MERGE_AT + 3 * j
                        for k in range(3):
                            split_w(6 * i + m + k + 1, (m + k + 1) % 2)
                        dve.wait_ge(w_used, made(6 * i + m + 2))
                        dve.wait_ge(sig_made, 2 * KD * s + 4 * i + 2 * j + 2)
                        for gate in range(2):
                            dve.tensor_tensor(gated[:, j, gate, :], ps[:, 4 * j + 2 + gate, :], sig[:, j, gate, :], ALU.mult)
                        dve.drain()
                        dve.tensor_tensor(merged[:, j, :], gated[:, j, 0, :], gated[:, j, 1, :], ALU.add).then_inc(merged_made, 1)
                        dve.wait_ge(m_hi_made, KD * s + 2 * i + j + 1)
                        there = m_hi[:, bass.ds(2 * i + j, 1), :].rearrange("p a t -> p (a t)")
                        dve.tensor_tensor(m_lo[:, bass.ds(2 * i + j, 1), :].rearrange("p a t -> p (a t)"), merged[:, j, :],
                                          there.bitcast(F32), ALU.subtract).then_inc(m_lo_made, 1)
                for half in range(2):
                    for k in range(4):
                        m = base + OUT_AT + 4 * half + k
                        split_w(m + 1, (m + 1) % 2)
                    dve.wait_ge(w_used, made(base + OUT_AT + 4 * half + 3))
                    for tt in range(NT):
                        there = resid[:, tt, half * T:(half + 1) * T]
                        dve.scalar_tensor_tensor(out=there, in0=there, scalar=ALPHA, in1=ps[:, 4 * half + tt, :],
                                                 op0=ALU.mult, op1=ALU.add).then_inc(mixed, 1)
                dve.drain()
                norm(3 * s + 1, s, False)
                turn(2 * s + 1)
                for tt in range(NT):
                    dve.tensor_scalar(resid[:, tt, :], resid[:, tt, :], ALPHA, None, ALU.mult)

                def scores_out(n, j):
                    dve.wait_ge(key_ps, 2 + SIDES * s + n + j + 1)
                    dve.tensor_copy(score[:, :, bass.ds(n + j, 1), :].rearrange("p t a n -> p t (a n)"),
                                    ps[:, 6 + j, :].rearrange("p (t n) -> p t n", t=NT)).then_inc(key_copied, 1)

                m = base + QUERY_AT
                dve.wait_ge(keys_in, 16 * (s + 1))
                split_w(m + 1, (m + 1) % 2)
                with dve.Fori(0, SIDES // 2 - 1) as i:
                    for j in range(2):
                        split_w(2 * i + m + 2 + j, (m + j) % 2)
                        scores_out(2 * i, j)
                split_w(m + SIDES, (m + SIDES) % 2)
                scores_out(SIDES - 2, 0)
                scores_out(SIDES - 2, 1)

                dve.wait_ge(pt_hi_made, s + 1)
                dve.tensor_tensor(pt_lo[:], pt_raw[:], pt_hi[:].bitcast(F32), ALU.subtract).then_inc(pt_lo_made, 1)
                for half in range(2):
                    m = base + PLE_AT + 5 * half
                    for k in range(5):
                        split_w(m + k + 1, (m + k + 1) % 2)
                    dve.wait_ge(w_used, made(m + 4))
                    dve.wait_ge(sig_p_made, 2 * s + half + 1)
                    for tt in range(NT):
                        dve.tensor_tensor(ple_t[:, tt, :], sig_p[:, tt, :], ps[:, 4 + tt, :], ALU.mult)
                    dve.drain()
                    there = resid[:, :, half * T:(half + 1) * T]
                    dve.tensor_tensor(there, there, ple_t[:], ALU.add).then_inc(ple_added, 1)
                dve.wait_ge(ple_added, 2 * (s + 1))

                for tt in range(NT):
                    dve.wait_ge(tile_copied, NT * s + tt + 1)
                    if tt:
                        dve.wait_ge(chosen_ps, NT * s + tt)
                    for r in range(SIDES):
                        dve.max(out=top_v[:, r, 0:8], in_=tile_sc[:, r, :])
                    dve.drain()
                    for r in range(SIDES):
                        dve.max_index(out=top_i[:, r, 0:8], in_max=top_v[:, r, 0:8], in_values=tile_sc[:, r, :])
                        dve.match_replace(out=rest_sc[:, r, :], in_to_replace=top_v[:, r, 0:8], in_values=tile_sc[:, r, :], imm_value=LOWEST)
                    dve.drain()
                    for r in range(SIDES):
                        dve.max(out=top_v[:, r, 8:16], in_=rest_sc[:, r, :])
                    dve.drain()
                    for r in range(SIDES):
                        dve.max_index(out=top_i[:, r, 8:16], in_max=top_v[:, r, 8:16], in_values=rest_sc[:, r, :])
                    pairs = top_v[:, :, :].rearrange("p (h c) k -> p h c k", c=2)
                    dve.tensor_tensor(pair_sc[:].rearrange("p h (a b) -> p h a b", a=TOPK),
                                      pairs[:, :, 0, :].unsqueeze(3).to_broadcast([P, PEER_HEADS, TOPK, TOPK]),
                                      pairs[:, :, 1, :].unsqueeze(2).to_broadcast([P, PEER_HEADS, TOPK, TOPK]), ALU.add)
                    dve.drain()
                    dve.tensor_copy(top_f[:], top_i[:])
                    rest_pairs = rest_sc[:].rearrange("p (h a) n -> p h (a n)", a=2)
                    for h in range(PEER_HEADS):
                        dve.max(out=fin_v[:, h, 0:8], in_=pair_sc[:, h, :])
                    dve.drain()
                    for h in range(PEER_HEADS):
                        dve.max_index(out=fin_i[:, 16 * h:16 * h + 8], in_max=fin_v[:, h, 0:8], in_values=pair_sc[:, h, :])
                        dve.match_replace(out=rest_pairs[:, h, :], in_to_replace=fin_v[:, h, 0:8], in_values=pair_sc[:, h, :], imm_value=LOWEST)
                    dve.drain()
                    for h in range(PEER_HEADS):
                        dve.max(out=fin_v[:, h, 8:16], in_=rest_pairs[:, h, :])
                    dve.drain()
                    for h in range(PEER_HEADS):
                        dve.max_index(out=fin_i[:, 16 * h + 8:16 * h + 16], in_max=fin_v[:, h, 8:16], in_values=rest_pairs[:, h, :])
                    dve.tensor_tensor(gate_x[:], fin_v[:], fin_v[:, :, 0:1].to_broadcast([P, PEER_HEADS, TOPK]), ALU.subtract).then_inc(gate_x_made, 1)
                    dve.drain()
                    dve.tensor_scalar(pos_i[:, 0, :], fin_i[:], 4, None, ALU.logical_shift_right)
                    dve.tensor_scalar(pos_i[:, 1, :], fin_i[:], TOPK - 1, None, ALU.bitwise_and)
                    dve.drain()
                    dve.tensor_copy(pos_f[:], pos_i[:])
                    dve.drain()
                    for c in range(2):
                        hot = pair_sc[:] if c == 0 else rest_pairs
                        hot3 = hot.rearrange("p h (k a) -> p (h k) a", a=TOPK)
                        hot4 = hot.rearrange("p h (k a) -> p h k a", a=TOPK)
                        numbers = top_f[:, :, :].rearrange("p (h c) k -> p h c k", c=2)[:, :, c, :]
                        dve.tensor_tensor(hot3, pos_f[:, c, :].unsqueeze(2).to_broadcast([P, HK, TOPK]),
                                          iota[:, 0:TOPK].unsqueeze(1).to_broadcast([P, HK, TOPK]), ALU.is_equal)
                        dve.drain()
                        dve.tensor_tensor(hot4, hot4, numbers.unsqueeze(2).to_broadcast([P, PEER_HEADS, TOPK, TOPK]), ALU.mult)
                        dve.drain()
                        dve.tensor_reduce(chosen[:, c, :], hot3, AX_X, ALU.add)
                    dve.wait_ge(gate_e_made, NT * s + tt + 1)
                    dve.tensor_reduce(gate_s[:], gate_e[:], AX_X, ALU.add)
                    dve.drain()
                    dve.reciprocal(gate_r[:], gate_s[:])
                    dve.drain()
                    dve.tensor_tensor(chosen[:, 2, :].rearrange("p (h k) -> p h k", k=TOPK), gate_e[:],
                                      gate_r[:].unsqueeze(2).to_broadcast([P, PEER_HEADS, TOPK]), ALU.mult).then_inc(chosen_made, 1)
                    dve.drain()
                    dve.sem_inc(tile_done, 1)
                    dve.wait_ge(chosen_ps, NT * s + tt + 1)
                    dve.tensor_copy(all_t[:, :, cols_of(tt)], ps[:, 0, 0:3 * P].rearrange("p (a t) -> p a t", a=3)).then_inc(chosen_copied, 1)
                dve.drain()
                gate = all_t[:, 2, :]
                for k in range(3):
                    dve.tensor_copy(gate_bf[:, k, :], gate if k == 0 else part[:])
                    dve.drain()
                    dve.tensor_copy(gate_parts[:, k, :], gate_bf[:, k, :])
                    dve.drain()
                    if k < 2:
                        dve.tensor_tensor(part[:], gate if k == 0 else part[:], gate_parts[:, k, :], ALU.subtract)
                        dve.drain()
                for tt in range(NT):
                    with dve.Fori(0, BATCHES // 2) as i:
                        for j in range(2):
                            t0 = 2 * BATCH * i + tt * P + BATCH * j
                            dve.wait_ge(onehot_used, s * NT * BATCHES + tt * BATCHES + 2 * i + j + 1)
                            dve.tensor_copy(cols[:, j, 0:2, :], all_t[:, 0:2, bass.ds(t0, BATCH)])
                            dve.tensor_copy(cols[:, j, 2:5, :], gate_parts[:, :, bass.ds(t0, BATCH)])
                            dve.drain()
                            for b in range(BATCH):
                                dve.tensor_scalar(onehot[:, j, b, 0, :], iota_bf[:], cols[:, j, 1, b:b + 1], None, ALU.is_equal)
                                for k in range(3):
                                    d = dve.tensor_scalar(onehot[:, j, b, 1 + k, :], iota_bf[:], cols[:, j, 0, b:b + 1],
                                                          cols[:, j, 2 + k, b:b + 1], ALU.is_equal, ALU.mult)
                            d.then_inc(onehot_made, 1)

                e0 = s * EXPERT_TILES
                mu = base + LAYER_TILES

                def acts(n, q):
                    for e in range(GROUP):
                        if e < GROUP - 1:
                            split_w(mu + n + e + 1, (mu + e + 1) % 2)
                        dve.wait_ge(act_made, 2 + e0 + n + e + 1)
                        dve.wait_ge(g_in_sem[e % 2], landed(e0 + n + e, e % 2))
                        dve.tensor_tensor(ga[:, e % 2, :], act_t[:, e % 2, :], g_in[:, e % 2, :], ALU.mult).then_inc(ga_made, 1)
                        dve.wait_ge(a_hi_made, e0 + n + e + 1)
                        dve.tensor_tensor(a_lo[:, q, e, :], ga[:, e % 2, :], a_hi[:, q, e, :].bitcast(F32), ALU.subtract).then_inc(a_lo_made, 1)

                def split_v(n, q, e):
                    dve.wait_ge(v_hi_made, e0 + n + e + 1)
                    dve.tensor_tensor(vw_lo[:, q, e, :], vw_raw[:, e % 2, :], vw_hi[:, q, e, :].bitcast(F32), ALU.subtract).then_inc(v_lo_made, 1)

                def add_out(g, o):
                    tt, half = o // 2, o % 2
                    there = resid[:, tt, half * T:(half + 1) * T]
                    dve.wait_ge(outs_ps, 2 * OUTS + s * GROUPS * OUTS + g * OUTS + o + 1)
                    dve.tensor_tensor(there, ps[:, 2 + o % 4, :], there, ALU.add).then_inc(outs_added, 1)

                def group(g, q, first=False, last=False):
                    acts(g * GROUP, q)
                    for e in range(GROUP):
                        split_v(g * GROUP, q, e)
                        if not first:
                            add_out(g - 1, 2 * e)
                            add_out(g - 1, 2 * e + 1)
                    if not last or s + 1 < SEQS:
                        split_w(mu + g * GROUP + GROUP, mu % 2)

                group(0, 0, first=True)
                with dve.Fori(0, GROUPS // 2 - 1) as i:
                    for j in range(2):
                        group(2 * i + 1 + j, (1 + j) % 2)
                group(GROUPS - 1, 1, last=True)
                for o in range(OUTS):
                    add_out(GROUPS - 1, o)
                dve.drain()
                norm(3 * s + 2, s, False)

        @block.tensor
        def _(pe):
            pe.sem_inc(w_used, 2)
            pe.sem_inc(key_ps, 2)
            pe.sem_inc(onehot_used, 2)
            pe.sem_inc(outs_ps, 2 * OUTS)

            def three(where, lh, ll, rh, rl, first, last):
                pe.matmul(where, lh, rh, start=first, stop=False)
                pe.matmul(where, lh, rl, start=False, stop=False)
                return pe.matmul(where, ll, rh, start=False, stop=last)

            def columns(where, slot, act_hi, act_lo, k0=0, kn=KD):
                for k in range(kn):
                    w = slice((k0 + k) * P, (k0 + k + 1) * P)
                    mm = three(where, w_hi[:, slot, w], w_lo[:, slot, w], act_hi[:, k, :], act_lo[:, k, :], k == 0, k == kn - 1)
                return mm

            def rows(bank, slot, act_hi, act_lo, k0, first, last):
                for k in range(2):
                    for tt in range(NT):
                        w = slice(k * T, (k + 1) * T)
                        mm = three(ps[:, bank + tt, :], act_hi[:, k0 + k, cols_of(tt)], act_lo[:, k0 + k, cols_of(tt)],
                                   w_hi[:, slot, w], w_lo[:, slot, w], first and k == 0, last and k == 1)
                return mm

            def turn(use, s):
                for tt in range(NT):
                    pe.wait_ge(ln_done, NT * (3 * (use // 2) + use % 2) + tt + 1)
                    for half in range(2):
                        n = 2 * tt + half
                        if n >= 4:
                            pe.wait_ge(xt_lo_made, 2 * NT * use + n - 3)
                        for k in range(4):
                            mm = pe.transpose(ps[:, n % 4, k * P:(k + 1) * P], resid[:, tt, (4 * half + k) * P:(4 * half + k + 1) * P], ident[:])
                        mm.then_inc(xt_ps, 1)
                pe.wait_ge(xt_lo_made, 2 * NT * (use + 1))

            pe.wait_ge(consts_in, 48)
            for s in range(SEQS):
                base = s * STREAM
                turn(2 * s, s)
                with pe.Fori(0, FQK_TILES // 2) as i:
                    for j in range(2):
                        m = base + j
                        pe.wait_ge(w_lo_made, made(2 * i + m))
                        pe.wait_ge(fqk_copied, FQK_TILES * s + 2 * i + j + 1)
                        columns(ps[:, 4 + j, :], m % 2, xt_hi, xt_lo).then_inc(w_used, 1)
                m = base + V_TILE
                pe.wait_ge(w_lo_made, made(m))
                for tt in range(NT):
                    for k in range(KD):
                        w = slice(k * P, (k + 1) * P)
                        mm = three(ps[:, 6, cols_of(tt)], xt_hi[:, k, cols_of(tt)], xt_lo[:, k, cols_of(tt)],
                                   w_hi[:, m % 2, w], w_lo[:, m % 2, w], k == 0, k == KD - 1)
                mm.then_inc(w_used, 1)

                pe.wait_ge(mix_in, 48 * (s + 1))
                pe.wait_ge(fqk_copied, 2 + FQK_TILES * (s + 1))
                for n in range(2 * NT):
                    tt, ch = n // 2, n % 2
                    if n >= 4:
                        pe.wait_ge(pq_copied, 2 * NT * s + n - 3)
                    for c in range(2):
                        mm = pe.matmul(ps[:, n % 4, c * 2 * P:(c + 1) * 2 * P], fqk[:, 2 * ch + c, cols_of(tt)], gdft[:], start=True, stop=True)
                    mm.then_inc(pq_ps, 1)
                pe.wait_ge(pq_copied, 2 * NT * (s + 1))
                for c in range(FT):
                    if c >= 2:
                        pe.wait_ge(fm_lo_made, FT * s + c - 1)
                    for part_ in range(2):
                        for tt in range(NT):
                            mm = pe.matmul(ps[:, 4 + c % 2, :], pq[:, tt, part_, cols_of(c)], dft[:, part_, tt, :],
                                           start=(part_ == 0 and tt == 0), stop=(part_ == 1 and tt == NT - 1))
                    mm.then_inc(fm_ps, 1)

                def scores(u):
                    g, blk = u % 2, u // 2
                    seen = key_tiles(blk)
                    if u:
                        pe.wait_ge(sc_copied, UNITS * s + u)
                    for h in range(Q_GROUP):
                        head = Q_GROUP * g + h
                        half = slice(64 * (head % 2), 64 * (head % 2) + 64)
                        mm = pe.matmul(ps[:, h, 0:P * len(seen)], fqk[half, FT + head // 2, cols_of(blk)],
                                       fqk[half, 2 * FT + g, seen[0] * P:(seen[-1] + 1) * P], start=True, stop=True)
                    mm.then_inc(sc_ps, 1)

                pe.wait_ge(v_copied, 2 * (s + 1))
                pe.wait_ge(fm_lo_made, FT * (s + 1))
                scores(0)
                for u in range(UNITS):
                    if u + 1 < UNITS:
                        scores(u + 1)
                    g, seen = u % 2, key_tiles(u // 2)
                    pe.wait_ge(probs_made, UNITS * s + u + 1)
                    if u:
                        pe.wait_ge(pt_copied, UNITS * s + u)
                    for k in range(len(seen)):
                        for h in range(Q_GROUP):
                            mm = pe.transpose(ps[:, 4 + k, cols_of(h)], probs[:, u % 2, h, k * P:(k + 1) * P], ident[:])
                    mm.then_inc(pt_ps, 1)
                    pe.wait_ge(pt_copied, UNITS * s + u + 1)
                    if u:
                        pe.wait_ge(o_lo_made, 2 * (UNITS * s + u))
                    for k, b in enumerate(seen):
                        mm = pe.matmul(ps[:, 7, :], v_dup[:, b, g, :, :].rearrange("p a d -> p (a d)"), probs_t[:, k, :],
                                       start=(k == 0), stop=(k == len(seen) - 1))
                    mm.then_inc(o_ps, 1)
                pe.wait_ge(o_lo_made, 2 * UNITS * (s + 1))

                with pe.Fori(0, KD // 2) as i:
                    for j in range(2):
                        m = base + MERGE_AT + 3 * j
                        pe.wait_ge(m_lo_made, KD * s + 2 * i + j + 1)
                        for gate in range(2):
                            pe.wait_ge(w_lo_made, made(6 * i + m + gate))
                            columns(ps[:, 4 * j + gate, :], (m + gate) % 2, xt_hi, xt_lo).then_inc(w_used, 1)
                        pe.wait_ge(w_lo_made, made(6 * i + m + 2))
                        columns(ps[:, 4 * j + 2, :], (m + 2) % 2, fm_hi, fm_lo, 0, FT)
                        columns(ps[:, 4 * j + 3, :], (m + 2) % 2, o_hi, o_lo, FT, FT).then_inc(w_used, 1)
                pe.wait_ge(m_lo_made, 2 + KD * (s + 1))
                for half in range(2):
                    for k in range(4):
                        m = base + OUT_AT + 4 * half + k
                        pe.wait_ge(w_lo_made, made(m))
                        rows(4 * half, m % 2, m_hi, m_lo, 2 * k, k == 0, k == 3).then_inc(w_used, 1)
                turn(2 * s + 1, s)

                def query(n, j):
                    m = base + QUERY_AT + j
                    pe.wait_ge(w_lo_made, made(m + n))
                    pe.wait_ge(q_copied, SIDES * s + n + j + 1)
                    columns(ps[:, 4 + j, :], m % 2, xt_hi, xt_lo).then_inc(w_used, 1)

                def key_scores(n, j):
                    pe.wait_ge(q_copied, 2 + SIDES * s + n + j + 1)
                    pe.wait_ge(key_copied, SIDES * s + n + j + 1)
                    for tt in range(NT):
                        mm = pe.matmul(ps[:, 6 + j, cols_of(tt)], q_t[:, j, cols_of(tt)],
                                       keys[:, bass.ds(n + j, 1), :].rearrange("p a n -> p (a n)"), start=True, stop=True)
                    mm.then_inc(key_ps, 1)

                pe.wait_ge(keys_in, 16 * (s + 1))
                query(0, 0)
                with pe.Fori(0, SIDES // 2 - 1) as i:
                    query(2 * i, 1)
                    key_scores(2 * i, 0)
                    query(2 * i + 2, 0)
                    key_scores(2 * i, 1)
                query(SIDES - 2, 1)
                key_scores(SIDES - 2, 0)
                key_scores(SIDES - 2, 1)

                pe.wait_ge(pt_lo_made, s + 1)
                pe.wait_ge(key_copied, 2 + SIDES * (s + 1))
                for half in range(2):
                    m = base + PLE_AT + 5 * half
                    if half:
                        pe.wait_ge(ple_added, 2 * s + 1)
                    for k in range(4):
                        pe.wait_ge(w_lo_made, made(m + k))
                        rows(0, (m + k) % 2, xt_hi, xt_lo, 2 * k, k == 0, k == 3).then_inc(w_used, 1)
                    pe.wait_ge(w_lo_made, made(m + 4))
                    rows(4, (m + 4) % 2, pt_hi, pt_lo, 0, True, True).then_inc(w_used, 1)

                pe.wait_ge(ple_added, 2 * (s + 1))
                for tt in range(NT):
                    pe.wait_ge(chosen_made, NT * s + tt + 1)
                    if tt:
                        pe.wait_ge(chosen_copied, NT * s + tt)
                    for k in range(3):
                        mm = pe.transpose(ps[:, 0, cols_of(k)], chosen[:, k, :], ident[:])
                    mm.then_inc(chosen_ps, 1)

                for tt in range(NT):
                    with pe.Fori(0, BATCHES // 2) as i:
                        for j in range(2):
                            done = s * NT * BATCHES + tt * BATCHES
                            pe.wait_ge(onehot_made, 2 * i + done + j + 1)
                            pe.wait_ge(g_copied, 2 * (2 * i + done + j) + 2)
                            for b in range(BATCH):
                                for k in range(3):
                                    mm = pe.matmul(ps[:, 4 + 2 * j + b // 4, cols_of(b % 4)], onehot[:, j, b, 0, :], onehot[:, j, b, 1 + k, :],
                                                   start=(k == 0), stop=(k == 2))
                            mm.then_inc(onehot_used, 1)

                e0 = s * EXPERT_TILES
                mu = base + LAYER_TILES
                pe.wait_ge(g_stored, 16 * NT * (s + 1))

                def up(n):
                    for e in range(GROUP):
                        pe.wait_ge(w_lo_made, made(mu + n + e))
                        pe.wait_ge(act_made, e0 + n + e + 1)
                        columns(ps[:, e % 2, :], (mu + e) % 2, xt_hi, xt_lo).then_inc(w_used, 1)

                def down(g, q):
                    pe.wait_ge(a_lo_made, e0 + g * GROUP + GROUP)
                    pe.wait_ge(v_lo_made, 2 + e0 + g * GROUP + GROUP)
                    for o in range(OUTS):
                        tt, half = o // 2, slice((o % 2) * T, (o % 2 + 1) * T)
                        pe.wait_ge(outs_added, s * GROUPS * OUTS + g * OUTS + o + 1)
                        for e in range(GROUP):
                            mm = three(ps[:, 2 + o % 4, :], a_hi[:, q, e, cols_of(tt)], a_lo[:, q, e, cols_of(tt)],
                                       vw_hi[:, q, e, half], vw_lo[:, q, e, half], e == 0, e == GROUP - 1)
                        mm.then_inc(outs_ps, 1)

                up(0)
                with pe.Fori(0, GROUPS // 2 - 1) as i:
                    for j in range(2):
                        up(2 * GROUP * i + GROUP * (1 + j))
                        down(2 * i + j, j)
                up(EXPERT_TILES - GROUP)
                down(GROUPS - 2, 0)
                down(GROUPS - 1, 1)


def _column_tile(np, w, columns):
    k = w.shape[0] // P
    return w[:, columns].reshape(k, P, -1).transpose(1, 0, 2).reshape(P, -1)


def _row_tile(np, w, k, half):
    return w[2 * k * P:2 * (k + 1) * P, half * T:(half + 1) * T].reshape(2, P, T).transpose(1, 0, 2).reshape(P, -1)


def _weight_stream(np, w_in, w_fo, w_ao, w_out, w_q, w_gate, w_proj):
    q0, k0, v0, g0 = FOURIER, 2 * FOURIER, 2 * FOURIER + KV_HEADS * HEAD_DIM, 2 * FOURIER + 2 * KV_HEADS * HEAD_DIM
    tiles = [_column_tile(np, w_in, np.arange(c * P, (c + 1) * P)) for c in range(2 * FT)]
    for g in range(KV_HEADS):
        head = np.arange(k0 + g * HEAD_DIM, k0 + (g + 1) * HEAD_DIM)
        tiles.append(_column_tile(np, w_in, np.concatenate([head, head])))
    tiles.append(_column_tile(np, w_in, np.arange(v0, g0)))
    for m in range(KD):
        here = np.arange(m * P, (m + 1) * P)
        tiles.append(_column_tile(np, w_in, g0 + here))
        tiles.append(_column_tile(np, w_in, g0 + D + here))
        tiles.append(np.concatenate([_column_tile(np, w_fo, here), _column_tile(np, w_ao, here)], axis=1))
    tiles += [_row_tile(np, w_out, k, half) for half in range(2) for k in range(KD // 2)]
    tiles += [_column_tile(np, w_q, np.arange(n * P, (n + 1) * P)) for n in range(SIDES)]
    for half in range(2):
        tiles += [_row_tile(np, w_gate, k, half) for k in range(KD // 2)]
        tiles.append(_row_tile(np, w_proj, 0, half))
    return np.stack(tiles)


def _constants(np):
    group = np.arange(GROUP_DIM)
    angle = 2 * np.pi * (np.outer(group, group) % GROUP_DIM) / GROUP_DIM
    norm = 1.0 / np.sqrt(T * GROUP_DIM)
    group_dft = np.zeros((P, 2 * P))
    for b in range(P // GROUP_DIM):
        at = slice(b * GROUP_DIM, (b + 1) * GROUP_DIM)
        group_dft[at, at] = np.cos(angle) * norm
        group_dft[at, P + b * GROUP_DIM:P + (b + 1) * GROUP_DIM] = np.sin(angle) * norm
    token = np.arange(T)
    angle = 2 * np.pi * (np.outer(token, token) % T) / T
    token_dft = np.stack([np.cos(angle), -np.sin(angle)])
    rel = np.abs(np.arange(P)[:, None] + P - np.arange(3 * P)[None, :])
    slopes = 2.0 ** (-8.0 * np.arange(1, HEADS + 1) / HEADS)
    bias = np.where(rel[:, None, :] <= WINDOW, -slopes[None, :, None] * rel[:, None, :], NEG_INF)
    iota = np.broadcast_to(np.arange(P), (P, P))
    return [a.astype(np.float32) for a in (np.eye(P), iota, group_dft, token_dft, bias)]


def kernel(x_prompt, x_sample, p_prompt, p_sample, emb_ln_g, emb_ln_b, w_in, attn_sink, w_fourier_out, w_attn_out,
           w_out, ln1_g, ln1_b, peer_w_q, peer_keys, peer_u, peer_v, ple_w_gate, ple_w_proj, ln2_g, ln2_b):
    import numpy as np
    import concourse.bacc as bacc
    from concourse.bass_utils import run_bass_kernel_spmd

    identity, key_iota, group_dft, token_dft, attn_bias = _constants(np)
    p_both = np.stack([np.asarray(p_prompt)[0, 0], np.asarray(p_sample)[0, 0]])
    ins = {
        "x": np.stack([np.asarray(x_prompt)[0], np.asarray(x_sample)[0]]),
        "p_t": p_both.reshape(SEQS, T, PLE // P, P).transpose(0, 3, 2, 1),
        "weights": _weight_stream(np, *(np.asarray(w)[0] for w in (w_in, w_fourier_out, w_attn_out, w_out, peer_w_q, ple_w_gate, ple_w_proj))),
        "u_t": np.asarray(peer_u)[0].reshape(NKEYS, P, KD, P).transpose(0, 3, 2, 1).reshape(NKEYS, P, D),
        "v_rows": np.asarray(peer_v)[0],
        "keys_t": np.asarray(peer_keys)[0].reshape(SIDES, NKEYS, P).transpose(2, 0, 1),
        "sink": np.asarray(attn_sink),
        "emb_g": np.asarray(emb_ln_g), "emb_b": np.asarray(emb_ln_b),
        "ln1_g": np.asarray(ln1_g)[0], "ln1_b": np.asarray(ln1_b)[0],
        "ln2_g": np.asarray(ln2_g)[0], "ln2_b": np.asarray(ln2_b)[0],
        "identity": identity, "key_iota": key_iota, "group_dft": group_dft, "token_dft": token_dft, "attn_bias": attn_bias,
    }
    nc = bacc.Bacc("TRN2", target_bir_lowering=False, num_devices=1)
    arrays = {f"in_{name}": np.ascontiguousarray(a) for name, a in ins.items()}
    args = [nc.dram_tensor(name, a.shape, mybir.dt.from_np(a.dtype), kind="ExternalInput").ap() for name, a in arrays.items()]
    out = nc.dram_tensor("out_y", (SEQS, T, D), F32, kind="ExternalOutput").ap()
    encoder(nc, *args, out)
    y = run_bass_kernel_spmd(nc, [arrays], core_ids=[0]).results[0]["out_y"]
    return y[0:1], y[1:2]
```

```python
from contextlib import ExitStack

import concourse.bass as bass
from concourse import mybir

F32 = mybir.dt.float32
F32R = mybir.dt.float32r
U32 = mybir.dt.uint32
ALU = mybir.AluOpType
ACT = mybir.ActivationFunctionType
AX_X = mybir.AxisListType.X

P = 128
SEQS = 2
T = 512
NT = T // P
D = 1024
KD = D // P
HEADS, KV_HEADS, HEAD_DIM = 8, 2, 64
Q_GROUP = HEADS // KV_HEADS
WINDOW = 128
FOURIER = 512
FT = FOURIER // P
GROUP_DIM = 64
PEER_HEADS, NKEYS, TOPK = 8, 128, 16
SIDES = 2 * PEER_HEADS
HK = PEER_HEADS * TOPK
PLE = 256
ALPHA = 2 ** 0.25
LN_EPS = 1e-5
NEG_INF = -1e30
LOWEST = -3.0e38

FQK_TILES = FT + FT + KV_HEADS
V_TILE = FQK_TILES
MERGE_AT = V_TILE + 1
OUT_AT = MERGE_AT + 3 * KD
QUERY_AT = OUT_AT + KD
PLE_AT = QUERY_AT + SIDES
LAYER_TILES = PLE_AT + 2 * (KD // 2 + 1)
EXPERT_TILES = NKEYS
STREAM = LAYER_TILES + EXPERT_TILES

OUTS = NT * 2

CHOICE_TILES = 8
LOOP_TILES, LOOP_BATCHES = 10, 8
UNITS = NT * KV_HEADS
BATCH = 8
BATCHES = P // BATCH
STEPS = BATCHES // LOOP_BATCHES
SETTLE_TILES = 4
SPREAD_AT = NT * CHOICE_TILES + SETTLE_TILES
LAST_AT = SPREAD_AT + NT * STEPS * LOOP_TILES
ORDER = ([("tile", e) for e in range(5)]
         + [("batch", 0), ("tile", 5), ("batch", 1), ("batch", 2), ("tile", 6), ("batch", 3), ("tile", 7),
            ("batch", 4), ("batch", 5), ("tile", 8), ("batch", 6), ("tile", 9), ("batch", 7)])
assert len(ORDER) == LOOP_TILES + LOOP_BATCHES
assert LAST_AT < EXPERT_TILES and (EXPERT_TILES - LAST_AT) % 2 == 0


def key_tiles(blk):
    return [b for b in (blk - 1, blk, blk + 1) if 0 <= b < NT]


def encoder(nc, x, p_t, weights, u_t, v_rows, keys_t, sink, emb_g, emb_b, ln1_g, ln1_b, ln2_g, ln2_b,
            identity, key_iota, group_dft, token_dft, attn_bias, out):
    ln_params = [(emb_g, emb_b), (ln1_g, ln1_b), (ln2_g, ln2_b)]
    with ExitStack() as ctx:
        def sb(name, shape, dt=F32, scope=ctx):
            return scope.enter_context(nc.sbuf_tensor(name, shape, dt))

        def sem(name):
            return ctx.enter_context(nc.semaphore(name))

        act_dram = nc.dram_tensor("act_dram", (SEQS, NKEYS, P, T), F32, kind="Internal").ap()
        g_dram = nc.dram_tensor("g_dram", (SEQS, NKEYS, P, T), F32, kind="Internal").ap()

        ident = sb("ident", [P, P])
        iota = sb("iota", [P, P])
        sinks = sb("sinks", [P, HEADS])
        resid = sb("resid", [P, NT, D])
        ln_gb = sb("ln_gb", [P, 2, D])
        w_raw = sb("w_raw", [P, 2, D])
        w_hi = sb("w_hi", [P, 2, D], F32R)
        w_lo = sb("w_lo", [P, 2, D], F32R)
        xt_hi = sb("xt_hi", [P, KD, T], F32R)
        xt_lo = sb("xt_lo", [P, KD, T], F32R)
        bn = sb("bn", [P, NT, 2, 6])
        mv = sb("mv", [P, NT, 2])
        var_eps = sb("var_eps", [P, NT])
        std = sb("std", [P, NT])
        rstd = sb("rstd", [P, NT])

        with ExitStack() as mix:
            fm_hi = sb("fm_hi", [P, FT, T], F32R, mix)
            fm_lo = sb("fm_lo", [P, FT, T], F32R, mix)
            o_hi = sb("o_hi", [P, FT, T], F32R, mix)
            o_lo = sb("o_lo", [P, FT, T], F32R, mix)
            with ExitStack() as four:
                pq = sb("pq", [P, NT, 2, FOURIER], F32, four)
                dft = sb("dft", [P, 2, NT, T], F32, four)
            m_hi = sb("m_hi", [P, KD, T], F32R, mix)
            m_lo = sb("m_lo", [P, KD, T], F32R, mix)
            gdft = sb("gdft", [P, 2 * P], F32, mix)
            with ExitStack() as att:
                fqk = sb("fqk", [P, FQK_TILES, T], F32, att)
                v_dup = sb("v_dup", [P, NT, KV_HEADS, 2, HEAD_DIM], F32, att)
                bias = sb("bias", [P, HEADS, 3 * P], F32, att)
                probs = sb("probs", [P, 2, Q_GROUP, 3 * P], F32, att)
                probs_t = sb("probs_t", [P, 3, Q_GROUP * P], F32, att)
                row_max = sb("row_max", [P, 2, Q_GROUP], F32, att)
                neg_max = sb("neg_max", [P, 2, Q_GROUP], F32, att)
                sink_ex = sb("sink_ex", [P, 2, Q_GROUP], F32, att)
                row_sum = sb("row_sum", [P, 2, Q_GROUP], F32, att)
                row_inv = sb("row_inv", [P, 2, Q_GROUP], F32, att)
            with ExitStack() as mrg:
                sig = sb("sig", [P, 2, 2, T], F32, mrg)
                gated = sb("gated", [P, 2, 2, T], F32, mrg)
                merged = sb("merged", [P, 2, T], F32, mrg)

        with ExitStack() as route:
            act_t = sb("act_t", [P, 2, T], F32, route)
            all_t = sb("all_t", [P, 3, T], F32, route)
            gate_hi = sb("gate_hi", [P, T], F32R, route)
            gate_lo = sb("gate_lo", [P, T], F32, route)
            with ExitStack() as choice:
                score = sb("score", [P, NT, SIDES, NKEYS], F32, choice)
                with ExitStack() as query:
                    keys = sb("keys", [P, SIDES, NKEYS], F32, query)
                    q_t = sb("q_t", [P, 2, T], F32, query)
                    pt_raw = sb("pt_raw", [P, 2, T], F32, query)
                    pt_hi = sb("pt_hi", [P, 2, T], F32R, query)
                    pt_lo = sb("pt_lo", [P, 2, T], F32R, query)
                    sig_p = sb("sig_p", [P, NT, T], F32, query)
                    ple_t = sb("ple_t", [P, NT, T], F32, query)
                with ExitStack() as pick:
                    tile_sc = sb("tile_sc", [P, SIDES, NKEYS], F32, pick)
                    rest_sc = sb("rest_sc", [P, SIDES, NKEYS], F32, pick)
                    pair_sc = sb("pair_sc", [P, PEER_HEADS, TOPK * TOPK], F32, pick)
                    chosen = sb("chosen", [P, 3, HK], F32, pick)
                    top_v = sb("top_v", [P, SIDES, TOPK], F32, pick)
                    top_i = sb("top_i", [P, SIDES, TOPK], U32, pick)
                    top_f = sb("top_f", [P, SIDES, TOPK], F32, pick)
                    fin_v = sb("fin_v", [P, PEER_HEADS, TOPK], F32, pick)
                    fin_i = sb("fin_i", [P, HK], U32, pick)
                    pos_i = sb("pos_i", [P, 2, HK], U32, pick)
                    pos_f = sb("pos_f", [P, 2, HK], F32, pick)
                    gate_x = sb("gate_x", [P, PEER_HEADS, TOPK], F32, pick)
                    gate_e = sb("gate_e", [P, PEER_HEADS, TOPK], F32, pick)
                    gate_s = sb("gate_s", [P, PEER_HEADS], F32, pick)
                    gate_r = sb("gate_r", [P, PEER_HEADS], F32, pick)
            with ExitStack() as spread:
                g_tile = sb("g_tile", [P, NKEYS, P], F32, spread)
                hot_col = sb("hot_col", [P, 2, BATCH, P], F32R, spread)
                hot_row = sb("hot_row", [P, 2, BATCH, P], F32, spread)
                gated_hi = sb("gated_hi", [P, 2, BATCH, P], F32R, spread)
                gated_lo = sb("gated_lo", [P, 2, BATCH, P], F32R, spread)

        with ExitStack() as second:
            v_raw = sb("v_raw", [P, 2, D], F32, second)
            v_hi = sb("v_hi", [P, 2, D], F32R, second)
            v_lo = sb("v_lo", [P, 2, D], F32R, second)
            act_in = sb("act_in", [P, 2, T], F32, second)
            g_in = sb("g_in", [P, 2, T], F32, second)
            ga = sb("ga", [P, 2, T], F32, second)
            a_hi = sb("a_hi", [P, 2, T], F32R, second)
            a_lo = sb("a_lo", [P, 2, T], F32R, second)

        ps = ctx.enter_context(nc.psum_tensor("ps", [P, 8, T], F32))

        consts_in, mix_in, keys_in, pt_in = sem("consts_in"), sem("mix_in"), sem("keys_in"), sem("pt_in")
        x_in = [sem(f"x_in{tt}") for tt in range(NT)]
        gb_in = sem("gb_in")
        stored = [sem(f"stored{tt}") for tt in range(NT)]
        w_in = [sem(f"w_in{k}") for k in range(2)]
        w_hi_made = sem("w_hi_made")
        w_lo_made = sem("w_lo_made")
        w_used = sem("w_used")
        var_made, std_made, ln_done, scaled = sem("var_made"), sem("std_made"), sem("ln_done"), sem("scaled")
        xt_ps, xt_hi_made, xt_lo_made = sem("xt_ps"), sem("xt_hi_made"), sem("xt_lo_made")
        fqk_copied = sem("fqk_copied")
        v_copied = sem("v_copied")
        pq_ps, pq_copied, fm_ps, fm_hi_made, fm_lo_made = (
            sem("pq_ps"), sem("pq_copied"), sem("fm_ps"), sem("fm_hi_made"), sem("fm_lo_made"))
        sc_ps, sc_copied, max_made, exp_made, probs_made = (
            sem("sc_ps"), sem("sc_copied"), sem("max_made"), sem("exp_made"), sem("probs_made"))
        pt_ps, pt_copied, o_ps, o_hi_made, o_lo_made = (
            sem("pt_ps"), sem("pt_copied"), sem("o_ps"), sem("o_hi_made"), sem("o_lo_made"))
        sig_made, merged_made, m_hi_made = sem("sig_made"), sem("merged_made"), sem("m_hi_made")
        m_lo_made = sem("m_lo_made")
        mixed = sem("mixed")
        q_copied = sem("q_copied")
        key_ps = sem("key_ps")
        key_copied = sem("key_copied")
        pt_hi_made, pt_lo_made, sig_p_made, ple_added = (
            sem("pt_hi_made"), sem("pt_lo_made"), sem("sig_p_made"), sem("ple_added"))
        tile_copied, tile_read = sem("tile_copied"), sem("tile_read")
        gate_x_made, gate_e_made, chosen_made = sem("gate_x_made"), sem("gate_e_made"), sem("chosen_made")
        chosen_ps, chosen_copied = sem("chosen_ps"), sem("chosen_copied")
        hot_made = sem("hot_made")
        hot_used = sem("hot_used")
        g_copied = sem("g_copied")
        g_stored = sem("g_stored")
        act_made = sem("act_made")
        act_stored = [sem(f"act_stored{k}") for k in range(2)]
        v_in, act_back, g_back = ([sem(f"{n}{k}") for k in range(2)] for n in ("v_in", "act_back", "g_back"))
        ga_made = sem("ga_made")
        a_hi_made, a_lo_made = sem("a_hi_made"), sem("a_lo_made")
        v_hi_made = sem("v_hi_made")
        v_lo_made = sem("v_lo_made")
        down_done = sem("down_done")
        outs_added = sem("outs_added")

        block = ctx.enter_context(nc.Block())

        def cols_of(tt):
            return slice(tt * P, (tt + 1) * P)

        def slot_free(m):
            return m + 1

        def made(m):
            return m + 3

        def landed(m, slot):
            return 8 * (m - slot) + 16

        def slot_left(m, slot):
            return 8 * (m - slot) + 16

        @block.sync
        def _(sp):
            def load_w(m, slot, source):
                sp.wait_ge(w_lo_made, slot_free(m))
                sp.dma_start(w_raw[:, slot, :], source).then_inc(w_in[slot], 16)

            def load_layer(s, first, last):
                pairs = (last - first) // 2
                with sp.Fori(0, pairs) as i:
                    for j in range(2):
                        m = s * STREAM + first + j
                        load_w(2 * i + m, m % 2, weights[bass.ds(2 * i + first + j, 1), :, :].rearrange("a p n -> (a p) n"))
                if (last - first) % 2:
                    m = s * STREAM + last - 1
                    load_w(m, m % 2, weights[last - 1])

            def load_ln(s, which):
                use = 3 * s + which
                if use:
                    sp.wait_ge(ln_done, NT * use)
                g, b = ln_params[which]
                for k, row in enumerate((g, b)):
                    sp.dma_start(ln_gb[:, k, :], row.rearrange("(a n) -> a n", a=1).to_broadcast([P, D])).then_inc(gb_in, 16)

            def load_u(s, n, slot):
                load_w(s * STREAM + LAYER_TILES + n, slot, u_t[bass.ds(n, 1), :, :].rearrange("a p n -> (a p) n"))

            def store_act(s, n, slot):
                sp.wait_ge(act_made, 2 + s * EXPERT_TILES + n + 1)
                sp.dma_start(act_dram[s, bass.ds(n, 1), :, :].rearrange("a p n -> (a p) n"), act_t[:, slot, :]).then_inc(act_stored[slot], 16)

            def first_pass(s, n, count):
                mu = s * STREAM + LAYER_TILES
                for e in range(count):
                    load_u(s, n + e + 2, (mu + e) % 2)
                    store_act(s, n + e, e % 2)

            def store_gates(s, tt):
                sp.wait_ge(g_copied, 4 + 2 * BATCHES * (s * NT + tt + 1))
                sp.dma_start(g_dram[s, :, :, bass.ds(tt * P, P)].rearrange("i j t -> j i t"), g_tile[:]).then_inc(g_stored, 16)

            def second_pass(s, n, slot):
                e0 = s * EXPERT_TILES
                sp.wait_ge(v_lo_made, e0 + n + 1)
                sp.dma_start(v_raw[:, slot, :], v_rows[bass.ds(n * P, P), :]).then_inc(v_in[slot], 16)
                sp.wait_ge(ga_made, e0 + n + 1)
                sp.wait_ge(act_stored[slot], 16 + landed(e0 + n, slot))
                sp.dma_start(act_in[:, slot, :], act_dram[s, bass.ds(n, 1), :, :].rearrange("a p n -> (a p) n")).then_inc(act_back[slot], 16)
                sp.dma_start(g_in[:, slot, :], g_dram[s, bass.ds(n, 1), :, :].rearrange("a p n -> (a p) n")).then_inc(g_back[slot], 16)

            sp.sem_inc(g_stored, 16)
            for slot in range(2):
                sp.sem_inc(act_stored[slot], 16)
            sp.dma_start(ident[:], identity).then_inc(consts_in, 16)
            sp.dma_start(iota[:], key_iota).then_inc(consts_in, 16)
            sp.dma_start(sinks[:], sink.to_broadcast([P, HEADS])).then_inc(consts_in, 16)
            for s in range(SEQS):
                base = s * STREAM
                for tt in range(NT):
                    if s:
                        sp.wait_ge(stored[tt], 16 * s)
                    sp.dma_start(resid[:, tt, :], x[s, cols_of(tt), :]).then_inc(x_in[tt], 16)
                load_ln(s, 0)
                load_layer(s, 2 if s else 0, 4)
                if s:
                    sp.wait_ge(outs_added, s * OUTS)
                sp.dma_start(gdft[:], group_dft).then_inc(mix_in, 16)
                sp.dma_start(dft[:], token_dft.rearrange("c (t p) n -> p c t n", p=P)).then_inc(mix_in, 16)
                sp.dma_start(bias[:], attn_bias).then_inc(mix_in, 16)
                load_layer(s, 4, MERGE_AT)
                load_ln(s, 1)
                load_layer(s, MERGE_AT, QUERY_AT + 2)
                sp.wait_ge(w_used, made(base + QUERY_AT - 1))
                sp.wait_ge(m_lo_made, 2 + KD * (s + 1))
                sp.dma_start(keys[:], keys_t).then_inc(keys_in, 16)
                sp.dma_start(pt_raw[:], p_t[s]).then_inc(pt_in, 16)
                load_layer(s, QUERY_AT + 2, LAYER_TILES)
                load_u(s, 0, (base + LAYER_TILES) % 2)
                load_ln(s, 2)
                load_u(s, 1, (base + LAYER_TILES + 1) % 2)
                with sp.Fori(0, SPREAD_AT // 2) as i:
                    first_pass(s, 2 * i, 2)
                with sp.Fori(0, NT) as tt:
                    with sp.Fori(0, STEPS) as i:
                        first_pass(s, SPREAD_AT + STEPS * LOOP_TILES * tt + LOOP_TILES * i, LOOP_TILES)
                    store_gates(s, tt)
                with sp.Fori(0, (EXPERT_TILES - LAST_AT) // 2 - 1) as i:
                    first_pass(s, LAST_AT + 2 * i, 2)
                if s + 1 < SEQS:
                    for e in range(2):
                        m = base + STREAM + e
                        load_w(m, m % 2, weights[e])
                for e in range(2):
                    store_act(s, EXPERT_TILES - 2 + e, e)
                sp.wait_ge(g_stored, 16 + 16 * NT * (s + 1))
                sp.wait_ge(hot_used, 2 + NT * BATCHES * (s + 1))
                for slot in range(2):
                    sp.wait_ge(act_stored[slot], 16 + landed((s + 1) * EXPERT_TILES - 2 + slot, slot))
                with sp.Fori(0, EXPERT_TILES // 2) as i:
                    for slot in range(2):
                        second_pass(s, 2 * i + slot, slot)
                for tt in range(NT):
                    sp.wait_ge(ln_done, NT * (3 * s + 2) + tt + 1)
                    sp.dma_start(out[s, cols_of(tt), :], resid[:, tt, :]).then_inc(stored[tt], 16)
            for tt in range(NT):
                sp.wait_ge(stored[tt], 16 * SEQS)

        @block.scalar
        def _(act):
            act.sem_inc(fqk_copied, 2)
            act.sem_inc(q_copied, 2)
            act.sem_inc(g_copied, 4)
            act.sem_inc(act_made, 2)

            def split_w(m, slot):
                act.wait_ge(w_in[slot], landed(m, slot))
                act.wait_ge(w_used, slot_free(m))
                act.activation(w_hi[:, slot, :], w_raw[:, slot, :], ACT.Copy).then_inc(w_hi_made, 1)

            def norm(use):
                act.wait_ge(var_made, use + 1)
                act.activation(std[:], var_eps[:], ACT.Sqrt).then_inc(std_made, 1)

            def turn(use):
                for n in range(2 * NT):
                    act.wait_ge(xt_ps, 2 * NT * use + n + 1)
                    act.activation(xt_hi[:, 4 * (n % 2):4 * (n % 2) + 4, cols_of(n // 2)],
                                   ps[:, n % 4, :].rearrange("p (k t) -> p k t", k=4), ACT.Copy).then_inc(xt_hi_made, 1)

            for s in range(SEQS):
                base = s * STREAM
                if s == 0:
                    split_w(0, 0)
                norm(3 * s)
                turn(2 * s)
                with act.Fori(0, FQK_TILES // 2) as i:
                    for j in range(2):
                        m = base + j
                        split_w(2 * i + m + 1, (m + 1) % 2)
                        act.wait_ge(w_used, made(2 * i + m))
                        act.activation(fqk[:, bass.ds(2 * i + j, 1), :].rearrange("p a t -> p (a t)"), ps[:, 4 + j, :], ACT.Copy).then_inc(fqk_copied, 1)
                split_w(base + V_TILE + 1, (base + V_TILE + 1) % 2)
                for n in range(2 * NT):
                    tt, ch = n // 2, n % 2
                    act.wait_ge(pq_ps, 2 * NT * s + n + 1)
                    act.activation(pq[:, tt, :, 256 * ch:256 * ch + 256].rearrange("p q (c f) -> p c q f", c=2),
                                   ps[:, n % 4, :].rearrange("p (c q f) -> p c q f", c=2, q=2), ACT.Copy).then_inc(pq_copied, 1)
                for c in range(FT):
                    act.wait_ge(fm_ps, FT * s + c + 1)
                    act.activation(fm_hi[:, c, :], ps[:, 4 + c % 2, :], ACT.Copy).then_inc(fm_hi_made, 1)

                def exps(u):
                    w = P * len(key_tiles(u // 2))
                    act.wait_ge(max_made, UNITS * s + u + 1)
                    for h in range(Q_GROUP):
                        act.activation(probs[:, u % 2, h, 0:w], probs[:, u % 2, h, 0:w], ACT.Exp,
                                       bias=neg_max[:, u % 2, h:h + 1], accum_out=row_sum[:, u % 2, h:h + 1])
                    act.activation(sink_ex[:, u % 2, :], sink_ex[:, u % 2, :], ACT.Exp).then_inc(exp_made, 1)

                def outputs_hi(u):
                    g, blk = u % 2, u // 2
                    act.wait_ge(o_ps, UNITS * s + u + 1)
                    for half in range(2):
                        rows = slice(64 * half, 64 * half + 64)
                        act.activation(o_hi[rows, 2 * g:2 * g + 2, cols_of(blk)],
                                       ps[rows, 7, :].rearrange("p (a b q) -> p a b q", a=2, b=2)[:, :, half, :], ACT.Copy).then_inc(o_hi_made, 1)

                exps(0)
                for u in range(UNITS):
                    if u + 1 < UNITS:
                        exps(u + 1)
                    act.wait_ge(pt_ps, UNITS * s + u + 1)
                    if u:
                        act.wait_ge(o_ps, UNITS * s + u)
                    nk = len(key_tiles(u // 2))
                    for k in range(nk):
                        a = act.activation(probs_t[:, k, :], ps[:, 4 + k, :], ACT.Copy)
                    a.then_inc(pt_copied, 1)
                    outputs_hi(u)

                with act.Fori(0, KD // 2) as i:
                    for j in range(2):
                        m = base + MERGE_AT + 3 * j
                        for gate in range(2):
                            split_w(6 * i + m + gate + 1, (m + gate + 1) % 2)
                            act.wait_ge(w_used, made(6 * i + m + gate))
                            if gate == 0:
                                act.wait_ge(m_lo_made, s * KD + 2 * i + j + 1)
                            act.activation(sig[:, j, gate, :], ps[:, 4 * j + gate, :], ACT.Sigmoid).then_inc(sig_made, 1)
                        split_w(6 * i + m + 3, (m + 3) % 2)
                        act.wait_ge(merged_made, s * KD + 2 * i + j + 1)
                        act.activation(m_hi[:, bass.ds(2 * i + j, 1), :].rearrange("p a t -> p (a t)"), merged[:, j, :], ACT.Copy).then_inc(m_hi_made, 1)
                for m in range(base + OUT_AT, base + QUERY_AT):
                    split_w(m + 1, (m + 1) % 2)
                norm(3 * s + 1)
                turn(2 * s + 1)

                def query(n, j):
                    m = base + QUERY_AT + j
                    split_w(m + 1 + n, (m + 1) % 2)
                    act.wait_ge(w_used, made(m + n))
                    act.wait_ge(key_ps, SIDES * s + n + j + 1)
                    act.activation(q_t[:, j, :], ps[:, 4 + j, :], ACT.Copy).then_inc(q_copied, 1)
                act.wait_ge(keys_in, 16 * (s + 1))
                with act.Fori(0, SIDES // 2) as i:
                    for j in range(2):
                        query(2 * i, j)
                act.wait_ge(pt_in, 16 * (s + 1))
                act.activation(pt_hi[:], pt_raw[:], ACT.Copy).then_inc(pt_hi_made, 1)
                for half in range(2):
                    m = base + PLE_AT + 5 * half
                    for k in range(5):
                        split_w(m + k + 1, (m + k + 1) % 2)
                        if k == 3:
                            act.wait_ge(w_used, made(m + k))
                            if half:
                                act.wait_ge(ple_added, 2 * s + half)
                            act.activation(sig_p[:], ps[:, 0:4, :], ACT.Sigmoid).then_inc(sig_p_made, 1)
                e0 = s * EXPERT_TILES
                mu = base + LAYER_TILES

                def first_pass(n, e, last=False):
                    if not last or s + 1 < SEQS:
                        split_w(mu + n + e + 1, (mu + e + 1) % 2)
                    act.wait_ge(w_used, made(mu + n + e))
                    act.wait_ge(act_stored[e % 2], slot_left(e0 + n + e, e % 2))
                    act.activation(act_t[:, e % 2, :], ps[:, e % 2, :], ACT.Gelu).then_inc(act_made, 1)

                def take_tile(tt):
                    act.wait_ge(key_copied, 2 + SIDES * (s + 1))
                    if s or tt:
                        act.wait_ge(tile_read, NT * s + tt)
                    act.activation(tile_sc[:], score[:, tt, :, :], ACT.Copy).then_inc(tile_copied, 1)

                def chosen_out(tt):
                    act.wait_ge(chosen_ps, NT * s + tt + 1)
                    act.activation(all_t[:, :, cols_of(tt)], ps[:, 2, 0:3 * P].rearrange("p (a t) -> p a t", a=3), ACT.Copy).then_inc(chosen_copied, 1)

                act.wait_ge(ple_added, 2 * (s + 1))
                take_tile(0)
                for tt in range(NT):
                    for half in range(2):
                        with act.Fori(0, CHOICE_TILES // 4) as i:
                            for e in range(2):
                                first_pass(CHOICE_TILES * tt + CHOICE_TILES // 2 * half + 2 * i, e)
                        if half == 0:
                            if tt:
                                chosen_out(tt - 1)
                            if tt + 1 < NT:
                                take_tile(tt + 1)
                    act.wait_ge(gate_x_made, NT * s + tt + 1)
                    act.activation(gate_e[:], gate_x[:], ACT.Exp).then_inc(gate_e_made, 1)
                with act.Fori(0, SETTLE_TILES // 2) as i:
                    for e in range(2):
                        first_pass(NT * CHOICE_TILES + 2 * i, e)
                chosen_out(NT - 1)
                with act.Fori(0, NT) as tt:
                    with act.Fori(0, STEPS) as i:
                        n = SPREAD_AT + STEPS * LOOP_TILES * tt + LOOP_TILES * i
                        for kind, at in ORDER:
                            if kind == "tile":
                                first_pass(n, at)
                                continue
                            done = NT * BATCHES * s + BATCHES * tt + LOOP_BATCHES * i + at
                            act.wait_ge(hot_used, 2 + done + 1)
                            act.wait_ge(g_stored, 16 * (NT * s + tt) + 16)
                            for half in range(2):
                                t0 = BATCH * LOOP_BATCHES * i + BATCH * at + 4 * half
                                act.activation(g_tile[:, :, bass.ds(t0, 4)].rearrange("p i t -> p t i"),
                                               ps[:, 4 + 2 * (at % 2) + half, :].rearrange("p (t i) -> p t i", t=4), ACT.Copy).then_inc(g_copied, 1)
                with act.Fori(0, (EXPERT_TILES - LAST_AT) // 2 - 1) as i:
                    for e in range(2):
                        first_pass(LAST_AT + 2 * i, e)
                first_pass(EXPERT_TILES - 2, 0)
                first_pass(EXPERT_TILES - 2, 1, last=True)

                def second_pass(n, slot):
                    act.wait_ge(v_in[slot], landed(e0 + n, slot))
                    act.wait_ge(down_done, e0 + n + 1)
                    act.activation(v_hi[:, slot, :], v_raw[:, slot, :], ACT.Copy).then_inc(v_hi_made, 1)
                    act.wait_ge(ga_made, 2 + e0 + n + 1)
                    act.activation(a_hi[:, slot, :], ga[:, slot, :], ACT.Copy).then_inc(a_hi_made, 1)
                with act.Fori(0, EXPERT_TILES // 2) as i:
                    for slot in range(2):
                        second_pass(2 * i + slot, slot)
                norm(3 * s + 2)

        @block.gpsimd
        def _(pool):
            pool.sem_inc(w_lo_made, 2)
            pool.sem_inc(v_lo_made, 2)

            def split_w(m, slot):
                pool.wait_ge(w_hi_made, m + 1)
                pool.tensor_tensor(w_lo[:, slot, :], w_raw[:, slot, :], w_hi[:, slot, :].bitcast(F32), ALU.subtract).then_inc(w_lo_made, 1)

            def split_v(n, slot):
                pool.wait_ge(v_hi_made, n + 1)
                pool.tensor_tensor(v_lo[:, slot, :], v_raw[:, slot, :], v_hi[:, slot, :].bitcast(F32), ALU.subtract).then_inc(v_lo_made, 1)

            for s in range(SEQS):
                first, last = s * STREAM + (1 if s else 0), s * STREAM + STREAM + (1 if s + 1 < SEQS else 0)
                with pool.Fori(0, (last - first) // 2) as i:
                    for j in range(2):
                        split_w(2 * i + first + j, (first + j) % 2)
                if (last - first) % 2:
                    split_w(last - 1, (last - 1) % 2)
                with pool.Fori(0, EXPERT_TILES // 2) as i:
                    for slot in range(2):
                        split_v(2 * i + s * EXPERT_TILES + slot, slot)

        @block.vector
        def _(dve):
            dve.sem_inc(m_lo_made, 2)
            dve.sem_inc(key_copied, 2)
            dve.sem_inc(ga_made, 2)

            def norm(use, s, from_dram):
                for tt in range(NT):
                    if from_dram:
                        dve.wait_ge(x_in[tt], 16 * (s + 1))
                    for half in range(2):
                        dve.bn_stats(bn[:, tt, half, :], resid[:, tt, half * T:(half + 1) * T])
                dve.drain()
                for tt in range(NT):
                    dve.bn_aggr(mv[:, tt, :], bn[:, tt, :, :].rearrange("p a b -> p (a b)"))
                dve.drain()
                dve.tensor_scalar(var_eps[:], mv[:, :, 1], LN_EPS, None, ALU.add).then_inc(var_made, 1)
                dve.wait_ge(std_made, use + 1)
                dve.reciprocal(rstd[:], std[:])
                dve.drain()
                dve.wait_ge(gb_in, 32 * (use + 1))
                for tt in range(NT):
                    dve.tensor_scalar(resid[:, tt, :], resid[:, tt, :], mv[:, tt, 0:1], rstd[:, tt:tt + 1], ALU.subtract, ALU.mult)
                    dve.drain()
                    dve.tensor_tensor(resid[:, tt, :], resid[:, tt, :], ln_gb[:, 0, :], ALU.mult)
                    dve.drain()
                    dve.tensor_tensor(resid[:, tt, :], resid[:, tt, :], ln_gb[:, 1, :], ALU.add).then_inc(ln_done, 1)

            def turn(use):
                for n in range(2 * NT):
                    dve.wait_ge(xt_hi_made, 2 * NT * use + n + 1)
                    there = (slice(None), slice(4 * (n % 2), 4 * (n % 2) + 4), cols_of(n // 2))
                    dve.tensor_tensor(xt_lo[there], ps[:, n % 4, :].rearrange("p (k t) -> p k t", k=4),
                                      xt_hi[there].bitcast(F32), ALU.subtract).then_inc(xt_lo_made, 1)

            dve.wait_ge(consts_in, 48)
            for s in range(SEQS):
                base = s * STREAM
                norm(3 * s, s, True)
                turn(2 * s)
                dve.wait_ge(w_used, made(base + V_TILE))
                for dup in range(2):
                    dve.tensor_copy(v_dup[:, :, :, dup, :], ps[:, 6, :].rearrange("p (t g d) -> p t g d", t=NT, g=KV_HEADS)).then_inc(v_copied, 1)
                for c in range(FT):
                    dve.wait_ge(fm_hi_made, FT * s + c + 1)
                    dve.tensor_tensor(fm_lo[:, c, :], ps[:, 4 + c % 2, :], fm_hi[:, c, :].bitcast(F32), ALU.subtract).then_inc(fm_lo_made, 1)

                def scores(u):
                    g, blk = u % 2, u // 2
                    w = P * len(key_tiles(blk))
                    at = 0 if blk else P
                    dve.wait_ge(sc_ps, UNITS * s + u + 1)
                    if u >= 2:
                        dve.wait_ge(pt_ps, UNITS * s + u - 1)
                    dve.scalar_tensor_tensor(out=probs[:, u % 2, :, 0:w], in0=ps[:, 0:4, 0:w], scalar=HEAD_DIM ** -0.5,
                                             in1=bias[:, Q_GROUP * g:Q_GROUP * g + Q_GROUP, at:at + w],
                                             op0=ALU.mult, op1=ALU.add).then_inc(sc_copied, 1)
                    dve.drain()
                    dve.tensor_reduce(row_max[:, u % 2, :], probs[:, u % 2, :, 0:w], AX_X, ALU.max)
                    dve.drain()
                    sk = sinks[:, Q_GROUP * g:Q_GROUP * g + Q_GROUP]
                    dve.tensor_tensor(row_max[:, u % 2, :], row_max[:, u % 2, :], sk, ALU.max)
                    dve.drain()
                    dve.tensor_scalar(neg_max[:, u % 2, :], row_max[:, u % 2, :], -1.0, None, ALU.mult)
                    dve.tensor_tensor(sink_ex[:, u % 2, :], sk, row_max[:, u % 2, :], ALU.subtract).then_inc(max_made, 1)

                def normalise(u):
                    w = P * len(key_tiles(u // 2))
                    dve.wait_ge(exp_made, UNITS * s + u + 1)
                    dve.tensor_tensor(row_inv[:, u % 2, :], row_sum[:, u % 2, :], sink_ex[:, u % 2, :], ALU.add)
                    dve.drain()
                    dve.reciprocal(row_inv[:, u % 2, :], row_inv[:, u % 2, :])
                    dve.drain()
                    for h in range(Q_GROUP):
                        d = dve.tensor_scalar(probs[:, u % 2, h, 0:w], probs[:, u % 2, h, 0:w], row_inv[:, u % 2, h:h + 1], None, ALU.mult)
                    d.then_inc(probs_made, 1)

                def outputs_lo(u):
                    g, blk = u % 2, u // 2
                    dve.wait_ge(o_hi_made, 2 * (UNITS * s + u + 1))
                    for half in range(2):
                        rows = slice(64 * half, 64 * half + 64)
                        dve.tensor_tensor(o_lo[rows, 2 * g:2 * g + 2, cols_of(blk)],
                                          ps[rows, 7, :].rearrange("p (a b q) -> p a b q", a=2, b=2)[:, :, half, :],
                                          o_hi[rows, 2 * g:2 * g + 2, cols_of(blk)].bitcast(F32), ALU.subtract).then_inc(o_lo_made, 1)

                dve.wait_ge(mix_in, 48 * (s + 1))
                scores(0)
                for u in range(UNITS):
                    if u + 1 < UNITS:
                        scores(u + 1)
                    normalise(u)
                    outputs_lo(u)

                with dve.Fori(0, KD // 2) as i:
                    for j in range(2):
                        m = base + MERGE_AT + 3 * j
                        dve.wait_ge(w_used, made(6 * i + m + 2))
                        dve.wait_ge(sig_made, 2 * KD * s + 4 * i + 2 * j + 2)
                        for gate in range(2):
                            dve.tensor_tensor(gated[:, j, gate, :], ps[:, 4 * j + 2 + gate, :], sig[:, j, gate, :], ALU.mult)
                        dve.drain()
                        dve.tensor_tensor(merged[:, j, :], gated[:, j, 0, :], gated[:, j, 1, :], ALU.add).then_inc(merged_made, 1)
                        dve.wait_ge(m_hi_made, KD * s + 2 * i + j + 1)
                        there = m_hi[:, bass.ds(2 * i + j, 1), :].rearrange("p a t -> p (a t)")
                        dve.tensor_tensor(m_lo[:, bass.ds(2 * i + j, 1), :].rearrange("p a t -> p (a t)"), merged[:, j, :],
                                          there.bitcast(F32), ALU.subtract).then_inc(m_lo_made, 1)
                for half in range(2):
                    dve.wait_ge(w_used, made(base + OUT_AT + 4 * half + 3))
                    for tt in range(NT):
                        there = resid[:, tt, half * T:(half + 1) * T]
                        dve.scalar_tensor_tensor(out=there, in0=there, scalar=ALPHA, in1=ps[:, 4 * half + tt, :],
                                                 op0=ALU.mult, op1=ALU.add).then_inc(mixed, 1)
                dve.drain()
                norm(3 * s + 1, s, False)
                turn(2 * s + 1)
                for tt in range(NT):
                    dve.tensor_scalar(resid[:, tt, :], resid[:, tt, :], ALPHA, None, ALU.mult)

                def scores_out(n, j):
                    dve.wait_ge(key_ps, 2 + SIDES * s + n + j + 1)
                    dve.tensor_copy(score[:, :, bass.ds(n + j, 1), :].rearrange("p t a n -> p t (a n)"),
                                    ps[:, 6 + j, :].rearrange("p (t n) -> p t n", t=NT)).then_inc(key_copied, 1)

                dve.wait_ge(keys_in, 16 * (s + 1))
                with dve.Fori(0, SIDES // 2) as i:
                    for j in range(2):
                        scores_out(2 * i, j)

                dve.wait_ge(pt_hi_made, s + 1)
                dve.tensor_tensor(pt_lo[:], pt_raw[:], pt_hi[:].bitcast(F32), ALU.subtract).then_inc(pt_lo_made, 1)
                for half in range(2):
                    m = base + PLE_AT + 5 * half
                    dve.wait_ge(w_used, made(m + 4))
                    dve.wait_ge(sig_p_made, 2 * s + half + 1)
                    for tt in range(NT):
                        dve.tensor_tensor(ple_t[:, tt, :], sig_p[:, tt, :], ps[:, 4 + tt, :], ALU.mult)
                    dve.drain()
                    there = resid[:, :, half * T:(half + 1) * T]
                    dve.tensor_tensor(there, there, ple_t[:], ALU.add).then_inc(ple_added, 1)
                dve.wait_ge(ple_added, 2 * (s + 1))

                for tt in range(NT):
                    dve.wait_ge(tile_copied, NT * s + tt + 1)
                    for r in range(SIDES):
                        dve.max(out=top_v[:, r, 0:8], in_=tile_sc[:, r, :])
                    dve.drain()
                    for r in range(SIDES):
                        dve.max_index(out=top_i[:, r, 0:8], in_max=top_v[:, r, 0:8], in_values=tile_sc[:, r, :])
                        d = dve.match_replace(out=rest_sc[:, r, :], in_to_replace=top_v[:, r, 0:8], in_values=tile_sc[:, r, :], imm_value=LOWEST)
                    d.then_inc(tile_read, 1)
                    dve.drain()
                    for r in range(SIDES):
                        dve.max(out=top_v[:, r, 8:16], in_=rest_sc[:, r, :])
                    dve.drain()
                    for r in range(SIDES):
                        dve.max_index(out=top_i[:, r, 8:16], in_max=top_v[:, r, 8:16], in_values=rest_sc[:, r, :])
                    pairs = top_v[:, :, :].rearrange("p (h c) k -> p h c k", c=2)
                    dve.tensor_tensor(pair_sc[:].rearrange("p h (a b) -> p h a b", a=TOPK),
                                      pairs[:, :, 0, :].unsqueeze(3).to_broadcast([P, PEER_HEADS, TOPK, TOPK]),
                                      pairs[:, :, 1, :].unsqueeze(2).to_broadcast([P, PEER_HEADS, TOPK, TOPK]), ALU.add)
                    dve.drain()
                    dve.tensor_copy(top_f[:], top_i[:])
                    rest_pairs = rest_sc[:].rearrange("p (h a) n -> p h (a n)", a=2)
                    for h in range(PEER_HEADS):
                        dve.max(out=fin_v[:, h, 0:8], in_=pair_sc[:, h, :])
                    dve.drain()
                    for h in range(PEER_HEADS):
                        dve.max_index(out=fin_i[:, 16 * h:16 * h + 8], in_max=fin_v[:, h, 0:8], in_values=pair_sc[:, h, :])
                        dve.match_replace(out=rest_pairs[:, h, :], in_to_replace=fin_v[:, h, 0:8], in_values=pair_sc[:, h, :], imm_value=LOWEST)
                    dve.drain()
                    for h in range(PEER_HEADS):
                        dve.max(out=fin_v[:, h, 8:16], in_=rest_pairs[:, h, :])
                    dve.drain()
                    for h in range(PEER_HEADS):
                        dve.max_index(out=fin_i[:, 16 * h + 8:16 * h + 16], in_max=fin_v[:, h, 8:16], in_values=rest_pairs[:, h, :])
                    dve.tensor_tensor(gate_x[:], fin_v[:], fin_v[:, :, 0:1].to_broadcast([P, PEER_HEADS, TOPK]), ALU.subtract).then_inc(gate_x_made, 1)
                    dve.drain()
                    dve.tensor_scalar(pos_i[:, 0, :], fin_i[:], 4, None, ALU.logical_shift_right)
                    dve.tensor_scalar(pos_i[:, 1, :], fin_i[:], TOPK - 1, None, ALU.bitwise_and)
                    dve.drain()
                    dve.tensor_copy(pos_f[:], pos_i[:])
                    dve.drain()
                    if tt:
                        dve.wait_ge(chosen_ps, NT * s + tt)
                    for c in range(2):
                        hot = pair_sc[:] if c == 0 else rest_pairs
                        hot3 = hot.rearrange("p h (k a) -> p (h k) a", a=TOPK)
                        hot4 = hot.rearrange("p h (k a) -> p h k a", a=TOPK)
                        numbers = top_f[:, :, :].rearrange("p (h c) k -> p h c k", c=2)[:, :, c, :]
                        dve.tensor_tensor(hot3, pos_f[:, c, :].unsqueeze(2).to_broadcast([P, HK, TOPK]),
                                          iota[:, 0:TOPK].unsqueeze(1).to_broadcast([P, HK, TOPK]), ALU.is_equal)
                        dve.drain()
                        dve.tensor_tensor(hot4, hot4, numbers.unsqueeze(2).to_broadcast([P, PEER_HEADS, TOPK, TOPK]), ALU.mult)
                        dve.drain()
                        dve.tensor_reduce(chosen[:, c, :], hot3, AX_X, ALU.add)
                    dve.wait_ge(gate_e_made, NT * s + tt + 1)
                    dve.tensor_reduce(gate_s[:], gate_e[:], AX_X, ALU.add)
                    dve.drain()
                    dve.reciprocal(gate_r[:], gate_s[:])
                    dve.drain()
                    dve.tensor_tensor(chosen[:, 2, :].rearrange("p (h k) -> p h k", k=TOPK), gate_e[:],
                                      gate_r[:].unsqueeze(2).to_broadcast([P, PEER_HEADS, TOPK]), ALU.mult).then_inc(chosen_made, 1)
                dve.wait_ge(chosen_copied, NT * (s + 1))
                dve.tensor_copy(gate_hi[:], all_t[:, 2, :])
                dve.drain()
                dve.tensor_tensor(gate_lo[:], all_t[:, 2, :], gate_hi[:].bitcast(F32), ALU.subtract)
                dve.drain()
                with dve.Fori(0, NT * BATCHES // 2) as i:
                    for j in range(2):
                        def spread_out(values):
                            return values.unsqueeze(2).to_broadcast([P, BATCH, P])
                        t0 = 2 * BATCH * i + BATCH * j
                        numbers = iota[:].unsqueeze(1).to_broadcast([P, BATCH, P])
                        dve.wait_ge(hot_used, s * NT * BATCHES + 2 * i + j + 1)
                        dve.tensor_tensor(hot_row[:, j], spread_out(all_t[:, 0, bass.ds(t0, BATCH)]), numbers, ALU.is_equal)
                        dve.tensor_tensor(hot_col[:, j], spread_out(all_t[:, 1, bass.ds(t0, BATCH)]), numbers, ALU.is_equal)
                        dve.drain()
                        dve.tensor_tensor(gated_hi[:, j], hot_row[:, j], spread_out(gate_hi[:, bass.ds(t0, BATCH)].bitcast(F32)), ALU.mult)
                        dve.tensor_tensor(gated_lo[:, j], hot_row[:, j], spread_out(gate_lo[:, bass.ds(t0, BATCH)]), ALU.mult).then_inc(hot_made, 1)

                e0 = s * EXPERT_TILES

                def second_pass(n, slot):
                    dve.wait_ge(act_back[slot], landed(e0 + n, slot))
                    dve.wait_ge(g_back[slot], landed(e0 + n, slot))
                    dve.tensor_tensor(ga[:, slot, :], act_in[:, slot, :], g_in[:, slot, :], ALU.mult).then_inc(ga_made, 1)
                    dve.wait_ge(a_hi_made, e0 + n + 1)
                    dve.tensor_tensor(a_lo[:, slot, :], ga[:, slot, :], a_hi[:, slot, :].bitcast(F32), ALU.subtract).then_inc(a_lo_made, 1)
                with dve.Fori(0, EXPERT_TILES // 2) as i:
                    for slot in range(2):
                        second_pass(2 * i + slot, slot)
                dve.wait_ge(down_done, 2 + e0 + EXPERT_TILES)
                for o in range(OUTS):
                    there = resid[:, o // 2, (o % 2) * T:(o % 2 + 1) * T]
                    dve.tensor_tensor(there, ps[:, o, :], there, ALU.add).then_inc(outs_added, 1)
                dve.drain()
                norm(3 * s + 2, s, False)

        @block.tensor
        def _(pe):
            pe.sem_inc(w_used, 2)
            pe.sem_inc(key_ps, 2)
            pe.sem_inc(hot_used, 2)
            pe.sem_inc(down_done, 2)

            def three(where, lh, ll, rh, rl, first, last):
                pe.matmul(where, lh, rh, start=first, stop=False)
                pe.matmul(where, lh, rl, start=False, stop=False)
                return pe.matmul(where, ll, rh, start=False, stop=last)

            def columns(where, slot, act_hi, act_lo, k0=0, kn=KD):
                for k in range(kn):
                    w = slice((k0 + k) * P, (k0 + k + 1) * P)
                    mm = three(where, w_hi[:, slot, w], w_lo[:, slot, w], act_hi[:, k, :], act_lo[:, k, :], k == 0, k == kn - 1)
                return mm

            def rows(bank, slot, act_hi, act_lo, k0, first, last):
                for k in range(2):
                    for tt in range(NT):
                        w = slice(k * T, (k + 1) * T)
                        mm = three(ps[:, bank + tt, :], act_hi[:, k0 + k, cols_of(tt)], act_lo[:, k0 + k, cols_of(tt)],
                                   w_hi[:, slot, w], w_lo[:, slot, w], first and k == 0, last and k == 1)
                return mm

            def turn(use, s):
                for tt in range(NT):
                    pe.wait_ge(ln_done, NT * (3 * (use // 2) + use % 2) + tt + 1)
                    for half in range(2):
                        n = 2 * tt + half
                        if n >= 4:
                            pe.wait_ge(xt_lo_made, 2 * NT * use + n - 3)
                        for k in range(4):
                            mm = pe.transpose(ps[:, n % 4, k * P:(k + 1) * P], resid[:, tt, (4 * half + k) * P:(4 * half + k + 1) * P], ident[:])
                        mm.then_inc(xt_ps, 1)
                pe.wait_ge(xt_lo_made, 2 * NT * (use + 1))

            pe.wait_ge(consts_in, 48)
            for s in range(SEQS):
                base = s * STREAM
                if s:
                    pe.wait_ge(outs_added, OUTS * s)
                turn(2 * s, s)
                with pe.Fori(0, FQK_TILES // 2) as i:
                    for j in range(2):
                        m = base + j
                        pe.wait_ge(w_lo_made, made(2 * i + m))
                        pe.wait_ge(fqk_copied, FQK_TILES * s + 2 * i + j + 1)
                        columns(ps[:, 4 + j, :], m % 2, xt_hi, xt_lo).then_inc(w_used, 1)
                m = base + V_TILE
                pe.wait_ge(w_lo_made, made(m))
                for tt in range(NT):
                    for k in range(KD):
                        w = slice(k * P, (k + 1) * P)
                        mm = three(ps[:, 6, cols_of(tt)], xt_hi[:, k, cols_of(tt)], xt_lo[:, k, cols_of(tt)],
                                   w_hi[:, m % 2, w], w_lo[:, m % 2, w], k == 0, k == KD - 1)
                mm.then_inc(w_used, 1)

                pe.wait_ge(mix_in, 48 * (s + 1))
                pe.wait_ge(fqk_copied, 2 + FQK_TILES * (s + 1))
                for n in range(2 * NT):
                    tt, ch = n // 2, n % 2
                    if n >= 4:
                        pe.wait_ge(pq_copied, 2 * NT * s + n - 3)
                    for c in range(2):
                        mm = pe.matmul(ps[:, n % 4, c * 2 * P:(c + 1) * 2 * P], fqk[:, 2 * ch + c, cols_of(tt)], gdft[:], start=True, stop=True)
                    mm.then_inc(pq_ps, 1)
                pe.wait_ge(pq_copied, 2 * NT * (s + 1))
                for c in range(FT):
                    if c >= 2:
                        pe.wait_ge(fm_lo_made, FT * s + c - 1)
                    for part_ in range(2):
                        for tt in range(NT):
                            mm = pe.matmul(ps[:, 4 + c % 2, :], pq[:, tt, part_, cols_of(c)], dft[:, part_, tt, :],
                                           start=(part_ == 0 and tt == 0), stop=(part_ == 1 and tt == NT - 1))
                    mm.then_inc(fm_ps, 1)

                def scores(u):
                    g, blk = u % 2, u // 2
                    seen = key_tiles(blk)
                    if u:
                        pe.wait_ge(sc_copied, UNITS * s + u)
                    for h in range(Q_GROUP):
                        head = Q_GROUP * g + h
                        half = slice(64 * (head % 2), 64 * (head % 2) + 64)
                        mm = pe.matmul(ps[:, h, 0:P * len(seen)], fqk[half, FT + head // 2, cols_of(blk)],
                                       fqk[half, 2 * FT + g, seen[0] * P:(seen[-1] + 1) * P], start=True, stop=True)
                    mm.then_inc(sc_ps, 1)

                pe.wait_ge(v_copied, 2 * (s + 1))
                pe.wait_ge(fm_lo_made, FT * (s + 1))
                scores(0)
                for u in range(UNITS):
                    if u + 1 < UNITS:
                        scores(u + 1)
                    g, seen = u % 2, key_tiles(u // 2)
                    pe.wait_ge(probs_made, UNITS * s + u + 1)
                    if u:
                        pe.wait_ge(pt_copied, UNITS * s + u)
                    for k in range(len(seen)):
                        for h in range(Q_GROUP):
                            mm = pe.transpose(ps[:, 4 + k, cols_of(h)], probs[:, u % 2, h, k * P:(k + 1) * P], ident[:])
                    mm.then_inc(pt_ps, 1)
                    pe.wait_ge(pt_copied, UNITS * s + u + 1)
                    if u:
                        pe.wait_ge(o_lo_made, 2 * (UNITS * s + u))
                    for k, b in enumerate(seen):
                        mm = pe.matmul(ps[:, 7, :], v_dup[:, b, g, :, :].rearrange("p a d -> p (a d)"), probs_t[:, k, :],
                                       start=(k == 0), stop=(k == len(seen) - 1))
                    mm.then_inc(o_ps, 1)
                pe.wait_ge(o_lo_made, 2 * UNITS * (s + 1))

                with pe.Fori(0, KD // 2) as i:
                    for j in range(2):
                        m = base + MERGE_AT + 3 * j
                        pe.wait_ge(m_lo_made, KD * s + 2 * i + j + 1)
                        for gate in range(2):
                            pe.wait_ge(w_lo_made, made(6 * i + m + gate))
                            columns(ps[:, 4 * j + gate, :], (m + gate) % 2, xt_hi, xt_lo).then_inc(w_used, 1)
                        pe.wait_ge(w_lo_made, made(6 * i + m + 2))
                        columns(ps[:, 4 * j + 2, :], (m + 2) % 2, fm_hi, fm_lo, 0, FT)
                        columns(ps[:, 4 * j + 3, :], (m + 2) % 2, o_hi, o_lo, FT, FT).then_inc(w_used, 1)
                pe.wait_ge(m_lo_made, 2 + KD * (s + 1))
                for half in range(2):
                    for k in range(4):
                        m = base + OUT_AT + 4 * half + k
                        pe.wait_ge(w_lo_made, made(m))
                        rows(4 * half, m % 2, m_hi, m_lo, 2 * k, k == 0, k == 3).then_inc(w_used, 1)
                turn(2 * s + 1, s)

                def query(n, j):
                    m = base + QUERY_AT + j
                    pe.wait_ge(w_lo_made, made(m + n))
                    pe.wait_ge(q_copied, SIDES * s + n + j + 1)
                    columns(ps[:, 4 + j, :], m % 2, xt_hi, xt_lo).then_inc(w_used, 1)

                def key_scores(n, j):
                    pe.wait_ge(q_copied, 2 + SIDES * s + n + j + 1)
                    pe.wait_ge(key_copied, SIDES * s + n + j + 1)
                    for tt in range(NT):
                        mm = pe.matmul(ps[:, 6 + j, cols_of(tt)], q_t[:, j, cols_of(tt)],
                                       keys[:, bass.ds(n + j, 1), :].rearrange("p a n -> p (a n)"), start=True, stop=True)
                    mm.then_inc(key_ps, 1)

                pe.wait_ge(keys_in, 16 * (s + 1))
                query(0, 0)
                with pe.Fori(0, SIDES // 2 - 1) as i:
                    query(2 * i, 1)
                    key_scores(2 * i, 0)
                    query(2 * i + 2, 0)
                    key_scores(2 * i, 1)
                query(SIDES - 2, 1)
                key_scores(SIDES - 2, 0)
                key_scores(SIDES - 2, 1)

                pe.wait_ge(pt_lo_made, s + 1)
                pe.wait_ge(key_copied, 2 + SIDES * (s + 1))
                for half in range(2):
                    m = base + PLE_AT + 5 * half
                    if half:
                        pe.wait_ge(ple_added, 2 * s + 1)
                    for k in range(4):
                        pe.wait_ge(w_lo_made, made(m + k))
                        rows(0, (m + k) % 2, xt_hi, xt_lo, 2 * k, k == 0, k == 3).then_inc(w_used, 1)
                    pe.wait_ge(w_lo_made, made(m + 4))
                    rows(4, (m + 4) % 2, pt_hi, pt_lo, 0, True, True).then_inc(w_used, 1)

                e0 = s * EXPERT_TILES
                mu = base + LAYER_TILES
                pe.wait_ge(ple_added, 2 * (s + 1))

                def first_pass(n, e):
                    pe.wait_ge(w_lo_made, made(mu + n + e))
                    pe.wait_ge(act_made, e0 + n + e + 1)
                    columns(ps[:, e % 2, :], (mu + e) % 2, xt_hi, xt_lo).then_inc(w_used, 1)

                def turn_chosen(tt):
                    pe.wait_ge(chosen_made, NT * s + tt + 1)
                    if tt:
                        pe.wait_ge(chosen_copied, NT * s + tt)
                    for k in range(3):
                        mm = pe.transpose(ps[:, 2, cols_of(k)], chosen[:, k, :], ident[:])
                    mm.then_inc(chosen_ps, 1)

                for tt in range(NT):
                    for half in range(2):
                        with pe.Fori(0, CHOICE_TILES // 4) as i:
                            for e in range(2):
                                first_pass(CHOICE_TILES * tt + CHOICE_TILES // 2 * half + 2 * i, e)
                        if half == 0 and tt:
                            turn_chosen(tt - 1)
                with pe.Fori(0, SETTLE_TILES // 2) as i:
                    for e in range(2):
                        first_pass(NT * CHOICE_TILES + 2 * i, e)
                turn_chosen(NT - 1)
                with pe.Fori(0, NT) as tt:
                    with pe.Fori(0, STEPS) as i:
                        n = SPREAD_AT + STEPS * LOOP_TILES * tt + LOOP_TILES * i
                        for kind, at in ORDER:
                            if kind == "tile":
                                first_pass(n, at)
                                continue
                            done = NT * BATCHES * s + BATCHES * tt + LOOP_BATCHES * i + at
                            pe.wait_ge(hot_made, done + 1)
                            pe.wait_ge(g_copied, 2 * done + 2)
                            for b in range(BATCH):
                                where = ps[:, 4 + 2 * (at % 2) + b // 4, cols_of(b % 4)]
                                pe.matmul(where, hot_col[:, at % 2, b, :], gated_hi[:, at % 2, b, :], start=True, stop=False)
                                mm = pe.matmul(where, hot_col[:, at % 2, b, :], gated_lo[:, at % 2, b, :], start=False, stop=True)
                            mm.then_inc(hot_used, 1)
                with pe.Fori(0, (EXPERT_TILES - LAST_AT) // 2) as i:
                    for e in range(2):
                        first_pass(LAST_AT + 2 * i, e)

                pe.wait_ge(act_made, 2 + e0 + EXPERT_TILES)
                pe.wait_ge(g_copied, 4 + 2 * NT * BATCHES * (s + 1))

                def second_pass(n, slot, first=False, last=False):
                    pe.wait_ge(a_lo_made, e0 + n + 1)
                    pe.wait_ge(v_lo_made, 2 + e0 + n + 1)
                    for o in range(OUTS):
                        tt, half = o // 2, slice((o % 2) * T, (o % 2 + 1) * T)
                        mm = three(ps[:, o, :], a_hi[:, slot, cols_of(tt)], a_lo[:, slot, cols_of(tt)],
                                   v_hi[:, slot, half], v_lo[:, slot, half], first, last)
                    mm.then_inc(down_done, 1)

                second_pass(0, 0, first=True)
                second_pass(1, 1)
                with pe.Fori(0, EXPERT_TILES // 2 - 2) as i:
                    for slot in range(2):
                        second_pass(2 * i + 2 + slot, slot)
                second_pass(EXPERT_TILES - 2, 0)
                second_pass(EXPERT_TILES - 1, 1, last=True)


def _column_tile(np, w, columns):
    k = w.shape[0] // P
    return w[:, columns].reshape(k, P, -1).transpose(1, 0, 2).reshape(P, -1)


def _row_tile(np, w, k, half):
    return w[2 * k * P:2 * (k + 1) * P, half * T:(half + 1) * T].reshape(2, P, T).transpose(1, 0, 2).reshape(P, -1)


def _weight_stream(np, w_in, w_fo, w_ao, w_out, w_q, w_gate, w_proj):
    q0, k0, v0, g0 = FOURIER, 2 * FOURIER, 2 * FOURIER + KV_HEADS * HEAD_DIM, 2 * FOURIER + 2 * KV_HEADS * HEAD_DIM
    tiles = [_column_tile(np, w_in, np.arange(c * P, (c + 1) * P)) for c in range(2 * FT)]
    for g in range(KV_HEADS):
        head = np.arange(k0 + g * HEAD_DIM, k0 + (g + 1) * HEAD_DIM)
        tiles.append(_column_tile(np, w_in, np.concatenate([head, head])))
    tiles.append(_column_tile(np, w_in, np.arange(v0, g0)))
    for m in range(KD):
        here = np.arange(m * P, (m + 1) * P)
        tiles.append(_column_tile(np, w_in, g0 + here))
        tiles.append(_column_tile(np, w_in, g0 + D + here))
        tiles.append(np.concatenate([_column_tile(np, w_fo, here), _column_tile(np, w_ao, here)], axis=1))
    tiles += [_row_tile(np, w_out, k, half) for half in range(2) for k in range(KD // 2)]
    tiles += [_column_tile(np, w_q, np.arange(n * P, (n + 1) * P)) for n in range(SIDES)]
    for half in range(2):
        tiles += [_row_tile(np, w_gate, k, half) for k in range(KD // 2)]
        tiles.append(_row_tile(np, w_proj, 0, half))
    return np.stack(tiles)


def _constants(np):
    group = np.arange(GROUP_DIM)
    angle = 2 * np.pi * (np.outer(group, group) % GROUP_DIM) / GROUP_DIM
    norm = 1.0 / np.sqrt(T * GROUP_DIM)
    group_dft = np.zeros((P, 2 * P))
    for b in range(P // GROUP_DIM):
        at = slice(b * GROUP_DIM, (b + 1) * GROUP_DIM)
        group_dft[at, at] = np.cos(angle) * norm
        group_dft[at, P + b * GROUP_DIM:P + (b + 1) * GROUP_DIM] = np.sin(angle) * norm
    token = np.arange(T)
    angle = 2 * np.pi * (np.outer(token, token) % T) / T
    token_dft = np.stack([np.cos(angle), -np.sin(angle)])
    rel = np.abs(np.arange(P)[:, None] + P - np.arange(3 * P)[None, :])
    slopes = 2.0 ** (-8.0 * np.arange(1, HEADS + 1) / HEADS)
    bias = np.where(rel[:, None, :] <= WINDOW, -slopes[None, :, None] * rel[:, None, :], NEG_INF)
    iota = np.broadcast_to(np.arange(P), (P, P))
    return [a.astype(np.float32) for a in (np.eye(P), iota, group_dft, token_dft, bias)]


def kernel(x_prompt, x_sample, p_prompt, p_sample, emb_ln_g, emb_ln_b, w_in, attn_sink, w_fourier_out, w_attn_out,
           w_out, ln1_g, ln1_b, peer_w_q, peer_keys, peer_u, peer_v, ple_w_gate, ple_w_proj, ln2_g, ln2_b):
    import numpy as np
    import concourse.bacc as bacc
    from concourse.bass_utils import run_bass_kernel_spmd

    identity, key_iota, group_dft, token_dft, attn_bias = _constants(np)
    p_both = np.stack([np.asarray(p_prompt)[0, 0], np.asarray(p_sample)[0, 0]])
    ins = {
        "x": np.stack([np.asarray(x_prompt)[0], np.asarray(x_sample)[0]]),
        "p_t": p_both.reshape(SEQS, T, PLE // P, P).transpose(0, 3, 2, 1),
        "weights": _weight_stream(np, *(np.asarray(w)[0] for w in (w_in, w_fourier_out, w_attn_out, w_out, peer_w_q, ple_w_gate, ple_w_proj))),
        "u_t": np.asarray(peer_u)[0].reshape(NKEYS, P, KD, P).transpose(0, 3, 2, 1).reshape(NKEYS, P, D),
        "v_rows": np.asarray(peer_v)[0],
        "keys_t": np.asarray(peer_keys)[0].reshape(SIDES, NKEYS, P).transpose(2, 0, 1),
        "sink": np.asarray(attn_sink),
        "emb_g": np.asarray(emb_ln_g), "emb_b": np.asarray(emb_ln_b),
        "ln1_g": np.asarray(ln1_g)[0], "ln1_b": np.asarray(ln1_b)[0],
        "ln2_g": np.asarray(ln2_g)[0], "ln2_b": np.asarray(ln2_b)[0],
        "identity": identity, "key_iota": key_iota, "group_dft": group_dft, "token_dft": token_dft, "attn_bias": attn_bias,
    }
    nc = bacc.Bacc("TRN2", target_bir_lowering=False, num_devices=1)
    arrays = {f"in_{name}": np.ascontiguousarray(a) for name, a in ins.items()}
    args = [nc.dram_tensor(name, a.shape, mybir.dt.from_np(a.dtype), kind="ExternalInput").ap() for name, a in arrays.items()]
    out = nc.dram_tensor("out_y", (SEQS, T, D), F32, kind="ExternalOutput").ap()
    encoder(nc, *args, out)
    y = run_bass_kernel_spmd(nc, [arrays], core_ids=[0]).results[0]["out_y"]
    return y[0:1], y[1:2]
```

```python
from contextlib import ExitStack

import concourse.bass as bass
from concourse import mybir

F32 = mybir.dt.float32
F32R = mybir.dt.float32r
U32 = mybir.dt.uint32
ALU = mybir.AluOpType
ACT = mybir.ActivationFunctionType
AX_X = mybir.AxisListType.X

P = 128
SEQS = 2
T = 512
NT = T // P
D = 1024
KD = D // P
HEADS, KV_HEADS, HEAD_DIM = 8, 2, 64
Q_GROUP = HEADS // KV_HEADS
WINDOW = 128
FOURIER = 512
FT = FOURIER // P
GROUP_DIM = 64
PEER_HEADS, NKEYS, TOPK = 8, 128, 16
SIDES = 2 * PEER_HEADS
HK = PEER_HEADS * TOPK
PLE = 256
ALPHA = 2 ** 0.25
LN_EPS = 1e-5
NEG_INF = -1e30
LOWEST = -3.0e38

FQK_TILES = FT + FT + KV_HEADS
V_TILE = FQK_TILES
MERGE_AT = V_TILE + 1
OUT_AT = MERGE_AT + 3 * KD
QUERY_AT = OUT_AT + KD
PLE_AT = QUERY_AT + SIDES
LAYER_TILES = PLE_AT + 2 * (KD // 2 + 1)
EXPERT_TILES = NKEYS
STREAM = LAYER_TILES + EXPERT_TILES

OUTS = NT * 2

CHOICE_TILES = 10
LOOP_TILES = 20
CHOICE_PAIRS = [(0, 2), (2, 4), (4, CHOICE_TILES // 2)]
UNITS = NT * KV_HEADS
BATCH = 8
BATCHES = P // BATCH
SETTLE_TILES = 4
SPREAD_AT = NT * CHOICE_TILES + SETTLE_TILES
LAST_AT = SPREAD_AT + NT * LOOP_TILES
ALONE = 8
MIXED = LOOP_TILES - ALONE
GROUP_TILES, GROUP_BATCHES = 3, 4
GROUPS = MIXED // GROUP_TILES
SPAN = GROUP_TILES * KD // GROUP_BATCHES
G_PIECES = 8
assert G_PIECES <= ALONE and GROUPS * GROUP_TILES == MIXED and GROUPS * GROUP_BATCHES == BATCHES

NORMS = [(0, 0), (0, 1), (1, 0), (0, 2), (1, 1), (1, 2)]
DEEP = 4
AHEAD = 6
EARLY_AT = EXPERT_TILES // 2
assert SEQS == 2 and all(n % DEEP == 0 for n in (EARLY_AT, 2 * NT, SPREAD_AT, LOOP_TILES)) and EXPERT_TILES - LAST_AT == DEEP


def nth_norm(s, which):
    return NORMS.index((s, which))


def key_tiles(blk):
    return [b for b in (blk - 1, blk, blk + 1) if 0 <= b < NT]


def encoder(nc, x, p_t, weights, u_t, v_rows, keys_t, sink, emb_g, emb_b, ln1_g, ln1_b, ln2_g, ln2_b,
            identity, key_iota, group_dft, token_dft, attn_bias, out):
    ln_params = [(emb_g, emb_b), (ln1_g, ln1_b), (ln2_g, ln2_b)]
    with ExitStack() as ctx:
        def sb(name, shape, dt=F32, scope=ctx):
            return scope.enter_context(nc.sbuf_tensor(name, shape, dt))

        def sem(name):
            return ctx.enter_context(nc.semaphore(name))

        act_dram = nc.dram_tensor("act_dram", (SEQS, NKEYS, P, T), F32, kind="Internal").ap()
        g_dram = nc.dram_tensor("g_dram", (SEQS, NKEYS, P, T), F32, kind="Internal").ap()

        ident = sb("ident", [P, P])
        iota = sb("iota", [P, P])
        sinks = sb("sinks", [P, HEADS])
        resid = sb("resid", [P, NT, D])
        ln_gb = sb("ln_gb", [P, 2, D])
        w_hi = sb("w_hi", [P, 2, D], F32R)
        w_lo = sb("w_lo", [P, 2, D], F32R)
        xt_hi = sb("xt_hi", [P, KD, T], F32R)
        xt_lo = sb("xt_lo", [P, KD, T], F32R)
        bn = sb("bn", [P, NT, 2, 6])
        mv = sb("mv", [P, NT, 2])
        var_eps = sb("var_eps", [P, NT])
        std = sb("std", [P, NT])
        rstd = sb("rstd", [P, NT])

        with ExitStack() as layer:
            w_raw = sb("w_raw", [P, 2, D], F32, layer)
        act_t = sb("act_t", [P, DEEP, T])

        with ExitStack() as mix:
            fm_hi = sb("fm_hi", [P, FT, T], F32R, mix)
            fm_lo = sb("fm_lo", [P, FT, T], F32R, mix)
            o_hi = sb("o_hi", [P, FT, T], F32R, mix)
            o_lo = sb("o_lo", [P, FT, T], F32R, mix)
            with ExitStack() as four:
                pq = sb("pq", [P, NT, 2, FOURIER], F32, four)
                dft = sb("dft", [P, 2, NT, T], F32, four)
            m_hi = sb("m_hi", [P, KD, T], F32R, mix)
            m_lo = sb("m_lo", [P, KD, T], F32R, mix)
            gdft = sb("gdft", [P, 2 * P], F32, mix)
            with ExitStack() as att:
                fqk = sb("fqk", [P, 2 * FT, T], F32, att)
                k_half = sb("k_half", [P, KV_HEADS, 2, T], F32, att)
                v_t = sb("v_t", [P, T], F32, att)
                v_dup = sb("v_dup", [P, NT, KV_HEADS, 2, HEAD_DIM], F32, att)
                bias = sb("bias", [P, HEADS, 3 * P], F32, att)
                probs = sb("probs", [P, 2, Q_GROUP, 3 * P], F32, att)
                probs_t = sb("probs_t", [P, 3, Q_GROUP * P], F32, att)
                row_max = sb("row_max", [P, 2, Q_GROUP], F32, att)
                neg_max = sb("neg_max", [P, 2, Q_GROUP], F32, att)
                sink_ex = sb("sink_ex", [P, 2, Q_GROUP], F32, att)
                row_sum = sb("row_sum", [P, 2, Q_GROUP], F32, att)
                row_inv = sb("row_inv", [P, 2, Q_GROUP], F32, att)
            with ExitStack() as mrg:
                sig = sb("sig", [P, 2, 2, T], F32, mrg)
                gated = sb("gated", [P, 2, 2, T], F32, mrg)
                merged = sb("merged", [P, 2, T], F32, mrg)

        experts = ctx.enter_context(ExitStack())
        u_raw = sb("u_raw", [P, DEEP, D], F32, experts)
        with ExitStack() as route:
            all_t = sb("all_t", [P, 3, T], F32, route)
            gate_hi = sb("gate_hi", [P, T], F32R, route)
            gate_lo = sb("gate_lo", [P, T], F32, route)
            with ExitStack() as choice:
                score = sb("score", [P, NT, SIDES, NKEYS], F32, choice)
                with ExitStack() as query:
                    keys = sb("keys", [P, SIDES, NKEYS], F32, query)
                    q_t = sb("q_t", [P, 2, T], F32, query)
                    pt_raw = sb("pt_raw", [P, 2, T], F32, query)
                    pt_hi = sb("pt_hi", [P, 2, T], F32R, query)
                    pt_lo = sb("pt_lo", [P, 2, T], F32R, query)
                    sig_p = sb("sig_p", [P, NT, T], F32, query)
                    ple_t = sb("ple_t", [P, NT, T], F32, query)
                with ExitStack() as pick:
                    tile_sc = sb("tile_sc", [P, SIDES, NKEYS], F32, pick)
                    rest_sc = sb("rest_sc", [P, SIDES, NKEYS], F32, pick)
                    pair_sc = sb("pair_sc", [P, PEER_HEADS, TOPK * TOPK], F32, pick)
                    chosen = sb("chosen", [P, 3, HK], F32, pick)
                    top_v = sb("top_v", [P, SIDES, TOPK], F32, pick)
                    top_i = sb("top_i", [P, SIDES, TOPK], U32, pick)
                    top_f = sb("top_f", [P, SIDES, TOPK], F32, pick)
                    fin_v = sb("fin_v", [P, PEER_HEADS, TOPK], F32, pick)
                    fin_i = sb("fin_i", [P, HK], U32, pick)
                    pos_i = sb("pos_i", [P, 2, HK], U32, pick)
                    pos_f = sb("pos_f", [P, 2, HK], F32, pick)
                    gate_x = sb("gate_x", [P, PEER_HEADS, TOPK], F32, pick)
                    gate_e = sb("gate_e", [P, PEER_HEADS, TOPK], F32, pick)
                    gate_s = sb("gate_s", [P, PEER_HEADS], F32, pick)
                    gate_r = sb("gate_r", [P, PEER_HEADS], F32, pick)
            with ExitStack() as spread:
                hot_col = sb("hot_col", [P, 2, BATCH, P], F32R, spread)
                hot_row = sb("hot_row", [P, 2, BATCH, P], F32, spread)
                gated_hi = sb("gated_hi", [P, 2, BATCH, P], F32R, spread)
                gated_lo = sb("gated_lo", [P, 2, BATCH, P], F32R, spread)
                g_tile = sb("g_tile", [P, NKEYS, P], F32, spread)

        with ExitStack() as second:
            early = sb("early", [P, NT, D], F32, second)
            v_raw = sb("v_raw", [P, DEEP, D], F32, second)
            act_in = sb("act_in", [P, DEEP, T], F32, second)
            g_in = sb("g_in", [P, DEEP, T], F32, second)
            v_hi = sb("v_hi", [P, 2, D], F32R, second)
            v_lo = sb("v_lo", [P, 2, D], F32R, second)
            ga = sb("ga", [P, 2, T], F32, second)
            a_hi = sb("a_hi", [P, 2, T], F32R, second)
            a_lo = sb("a_lo", [P, 2, T], F32R, second)

        experts.close()
        ps = ctx.enter_context(nc.psum_tensor("ps", [P, 8, T], F32))

        consts_in, mix_in, keys_in, pt_in = sem("consts_in"), sem("mix_in"), sem("keys_in"), sem("pt_in")
        x_in = [sem(f"x_in{tt}") for tt in range(NT)]
        gb_in = sem("gb_in")
        stored = [sem(f"stored{tt}") for tt in range(NT)]
        w_in = [sem(f"w_in{k}") for k in range(2)]
        w_hi_made = sem("w_hi_made")
        w_lo_made = [sem(f"w_lo_made{h}") for h in range(2)]
        w_used = sem("w_used")
        var_made, std_made, ln_done = sem("var_made"), sem("std_made"), sem("ln_done")
        xt_ps, xt_hi_made, xt_lo_made = sem("xt_ps"), sem("xt_hi_made"), sem("xt_lo_made")
        fqk_copied = sem("fqk_copied")
        k_zeroed = sem("k_zeroed")
        v_t_copied, v_ps = sem("v_t_copied"), sem("v_ps")
        dft_in, early_moved = sem("dft_in"), sem("early_moved")
        v_copied = sem("v_copied")
        pq_ps, pq_copied, fm_ps, fm_hi_made, fm_lo_made = (
            sem("pq_ps"), sem("pq_copied"), sem("fm_ps"), sem("fm_hi_made"), sem("fm_lo_made"))
        sc_ps, sc_copied, max_made, exp_made, probs_made = (
            sem("sc_ps"), sem("sc_copied"), sem("max_made"), sem("exp_made"), sem("probs_made"))
        pt_ps, pt_copied, o_ps, o_hi_made, o_lo_made = (
            sem("pt_ps"), sem("pt_copied"), sem("o_ps"), sem("o_hi_made"), sem("o_lo_made"))
        sig_made, merged_made, m_hi_made = sem("sig_made"), sem("merged_made"), sem("m_hi_made")
        m_lo_made = sem("m_lo_made")
        q_copied = sem("q_copied")
        key_ps = sem("key_ps")
        key_copied = sem("key_copied")
        pt_hi_made, pt_lo_made, sig_p_made, ple_read, ple_added = (
            sem("pt_hi_made"), sem("pt_lo_made"), sem("sig_p_made"), sem("ple_read"), sem("ple_added"))
        tile_copied, tile_read = sem("tile_copied"), sem("tile_read")
        gate_x_made, gate_e_made, chosen_made = sem("gate_x_made"), sem("gate_e_made"), sem("chosen_made")
        chosen_ps, chosen_copied = sem("chosen_ps"), sem("chosen_copied")
        hot_made = sem("hot_made")
        hot_used = sem("hot_used")
        g_copied = sem("g_copied")
        g_stored = sem("g_stored")
        act_made = sem("act_made")
        act_stored = [sem(f"act_stored{k}") for k in range(DEEP)]
        u_in, v_in, act_back, g_back = ([sem(f"{n}{k}") for k in range(DEEP)] for n in ("u_in", "v_in", "act_back", "g_back"))
        ga_made = sem("ga_made")
        a_hi_made, a_lo_made = sem("a_hi_made"), sem("a_lo_made")
        v_hi_made = sem("v_hi_made")
        v_lo_made = [sem(f"v_lo_made{h}") for h in range(2)]
        down_done = sem("down_done")
        out_ps, outs_added = sem("out_ps"), sem("outs_added")

        block = ctx.enter_context(nc.Block())

        def cols_of(tt):
            return slice(tt * P, (tt + 1) * P)

        def slot_free(m):
            return m + 1

        def made(m):
            return m + 3

        def landed(m, slot):
            return 8 * (m - slot) + 16

        def deep_landed(n, slot):
            return 16 // DEEP * (n - slot) + 16

        def slot_left(n, slot):
            return 16 // DEEP * (n - slot) + 16

        @block.sync
        def _(sp):
            def load_w(m, slot, source):
                sp.wait_ge(w_lo_made[1], slot_free(m))
                sp.dma_start(w_raw[:, slot, :], source).then_inc(w_in[slot], 16)

            def load_layer(s, first, last):
                pairs = (last - first) // 2
                with sp.Fori(0, pairs) as i:
                    for j in range(2):
                        m = s * STREAM + first + j
                        load_w(2 * i + m, m % 2, weights[bass.ds(2 * i + first + j, 1), :, :].rearrange("a p n -> (a p) n"))
                if (last - first) % 2:
                    m = s * STREAM + last - 1
                    load_w(m, m % 2, weights[last - 1])

            def load_ln(s, which):
                use = nth_norm(s, which)
                if use:
                    sp.wait_ge(ln_done, NT * use)
                g, b = ln_params[which]
                for k, row in enumerate((g, b)):
                    sp.dma_start(ln_gb[:, k, :], row.rearrange("(a n) -> a n", a=1).to_broadcast([P, D])).then_inc(gb_in, 16)

            def load_u(s, n, slot):
                sp.wait_ge(w_lo_made[1], made(s * STREAM + LAYER_TILES + n + slot - DEEP))
                sp.dma_start(u_raw[:, slot, :], u_t[bass.ds(n + slot, 1), :, :].rearrange("a p n -> (a p) n")).then_inc(u_in[slot], 16)

            def store_act(s, n, slot):
                sp.wait_ge(act_made, 2 + s * EXPERT_TILES + n + 1)
                sp.dma_start(act_dram[s, bass.ds(n, 1), :, :].rearrange("a p n -> (a p) n"), act_t[:, slot, :]).then_inc(act_stored[slot], 16)

            def first_pass(s, n, e):
                load_u(s, n + e - e % DEEP + DEEP, e % DEEP)
                store_act(s, n + e, e % DEEP)

            def store_gates(s, tt, piece):
                n = NKEYS // G_PIECES
                rows = slice(piece * n, (piece + 1) * n)
                sp.dma_start(g_dram[s, rows, :, bass.ds(tt * P, P)].rearrange("i j t -> j i t"), g_tile[:, rows, :]).then_inc(g_stored, 16)

            def second_pass(s, n, slot, first=False):
                e0 = s * EXPERT_TILES
                if not first:
                    sp.wait_ge(v_lo_made[1], 2 + e0 + n + slot - DEEP + 1)
                sp.dma_start(v_raw[:, slot, :], v_rows[bass.ds((n + slot) * P, P), :]).then_inc(v_in[slot], 16)
                if not first:
                    sp.wait_ge(ga_made, 2 + e0 + n + slot - DEEP + 1)
                sp.wait_ge(act_stored[slot], 16 + deep_landed(e0 + n + slot, slot))
                sp.dma_start(act_in[:, slot, :], act_dram[s, bass.ds(n + slot, 1), :, :].rearrange("a p n -> (a p) n")).then_inc(act_back[slot], 16)
                sp.dma_start(g_in[:, slot, :], g_dram[s, bass.ds(n + slot, 1), :, :].rearrange("a p n -> (a p) n")).then_inc(g_back[slot], 16)

            sp.sem_inc(g_stored, 16)
            for slot in range(DEEP):
                sp.sem_inc(act_stored[slot], 16)
            sp.dma_start(ident[:], identity).then_inc(consts_in, 16)
            sp.dma_start(iota[:], key_iota).then_inc(consts_in, 16)
            sp.dma_start(sinks[:], sink.to_broadcast([P, HEADS])).then_inc(consts_in, 16)
            for s in range(SEQS):
                base = s * STREAM
                if s == 0:
                    for tt in range(NT):
                        sp.dma_start(resid[:, tt, :], x[s, cols_of(tt), :]).then_inc(x_in[tt], 16)
                        if tt == 0:
                            load_ln(s, 0)
                load_layer(s, AHEAD if s else 0, 8)
                if s:
                    sp.wait_ge(outs_added, s * OUTS)
                sp.dma_start(gdft[:], group_dft).then_inc(mix_in, 16)
                sp.dma_start(bias[:], attn_bias).then_inc(mix_in, 16)
                load_layer(s, 8, MERGE_AT)
                sp.dma_start(dft[:], token_dft.rearrange("c (t p) n -> p c t n", p=P)).then_inc(dft_in, 16)
                load_ln(s, 1)
                load_layer(s, MERGE_AT, QUERY_AT + 2)
                sp.wait_ge(w_used, made(base + QUERY_AT - 1))
                sp.wait_ge(m_lo_made, 2 + KD * (s + 1))
                sp.dma_start(keys[:], keys_t).then_inc(keys_in, 16)
                sp.dma_start(pt_raw[:], p_t[s]).then_inc(pt_in, 16)
                load_layer(s, QUERY_AT + 2, LAYER_TILES)
                for slot in range(DEEP):
                    load_u(s, 0, slot)
                load_ln(*((1, 0) if s == 0 else (1, 2)))
                with sp.Fori(0, SPREAD_AT // DEEP) as i:
                    for e in range(DEEP):
                        first_pass(s, DEEP * i, e)
                with sp.Fori(0, NT) as tt:
                    n = SPREAD_AT + LOOP_TILES * tt
                    for e in range(LOOP_TILES):
                        if e == LOOP_TILES - ALONE:
                            sp.wait_ge(g_copied, 4 + 2 * BATCHES * (s * NT + tt + 1))
                        if 0 <= e - (LOOP_TILES - ALONE) < G_PIECES:
                            store_gates(s, tt, e - (LOOP_TILES - ALONE))
                        first_pass(s, n, e)
                sp.wait_ge(g_stored, 16 + 16 * G_PIECES * NT * (s + 1))
                sp.wait_ge(hot_used, 2 + NT * BATCHES * (s + 1))
                for slot in range(DEEP):
                    second_pass(s, 0, slot, first=True)
                for e in range(EXPERT_TILES - LAST_AT - 2):
                    store_act(s, LAST_AT + e, e % DEEP)
                for e in range(2):
                    store_act(s, EXPERT_TILES - 2 + e, DEEP - 2 + e)
                if s == 0:
                    for tt in range(NT):
                        sp.dma_start(early[:, tt, :], x[1, cols_of(tt), :]).then_inc(x_in[tt], 16)
                if s + 1 < SEQS:
                    for slot in range(DEEP):
                        sp.wait_ge(act_stored[slot], 16 + 16 // DEEP * EXPERT_TILES * (s + 1))
                    load_layer(s + 1, 0, 2)
                middle = (EARLY_AT + 2 * NT) // DEEP + 1
                with sp.Fori(1, middle) as i:
                    for slot in range(DEEP):
                        second_pass(s, DEEP * i, slot)
                if s == 0:
                    load_ln(0, 2)
                with sp.Fori(middle, EXPERT_TILES // DEEP) as i:
                    for slot in range(DEEP):
                        second_pass(s, DEEP * i, slot)
                if s + 1 < SEQS:
                    load_layer(s + 1, 2, AHEAD)
                for tt in range(NT):
                    sp.wait_ge(ln_done, NT * nth_norm(s, 2) + tt + 1)
                    sp.dma_start(out[s, cols_of(tt), :], resid[:, tt, :]).then_inc(stored[tt], 16)
            for tt in range(NT):
                sp.wait_ge(stored[tt], 16 * SEQS)

        @block.scalar
        def _(act):
            act.sem_inc(fqk_copied, 2)
            act.sem_inc(q_copied, 2)
            act.sem_inc(g_copied, 4)
            act.sem_inc(act_made, 2)

            def split_w(s, m, slot):
                act.wait_ge(w_in[slot], landed(m - s * EXPERT_TILES, slot))
                act.wait_ge(w_used, slot_free(m))
                act.activation(w_hi[:, slot, :], w_raw[:, slot, :], ACT.Copy).then_inc(w_hi_made, 1)

            def deviation(use, tt):
                act.wait_ge(var_made, NT * use + tt + 1)
                act.activation(std[:, tt:tt + 1], var_eps[:, tt:tt + 1], ACT.Sqrt).then_inc(std_made, 1)

            def turn(use, tt):
                for n in (2 * tt, 2 * tt + 1):
                    act.wait_ge(xt_ps, 2 * NT * use + n + 1)
                    act.activation(xt_hi[:, 4 * (n % 2):4 * (n % 2) + 4, cols_of(tt)],
                                   ps[:, n % 4, :].rearrange("p (k t) -> p k t", k=4), ACT.Copy).then_inc(xt_hi_made, 1)

            def norm(use, turns=None, splits=()):
                deviation(use, 0)
                for tt in range(NT):
                    if tt + 1 < NT:
                        deviation(use, tt + 1)
                    for at, s, m in splits:
                        if at == tt:
                            split_w(s, m, m % 2)
                    if turns is not None and tt:
                        turn(turns, tt - 1)
                if turns is not None:
                    turn(turns, NT - 1)

            for s in range(SEQS):
                base = s * STREAM
                if s == 0:
                    norm(nth_norm(0, 0), turns=0, splits=((1, 0, 0), (2, 0, 1)))
                else:
                    for tt in range(NT):
                        turn(2 * s, tt)
                        if tt == 1:
                            split_w(s, base + 1, (base + 1) % 2)
                def fqk_out(n, j):
                    m = base + j
                    if not isinstance(n, int) or n + j:
                        split_w(s, n + m + 1, (m + 1) % 2)
                    act.wait_ge(w_used, made(n + m))
                    act.activation(fqk[:, bass.ds(n + j, 1), :].rearrange("p a t -> p (a t)"), ps[:, 4 + j, :], ACT.Copy).then_inc(fqk_copied, 1)

                for j in range(2):
                    fqk_out(0, j)
                if s:
                    for tt in range(NT):
                        deviation(nth_norm(s - 1, 2), tt)
                with act.Fori(1, FT) as i:
                    for j in range(2):
                        fqk_out(2 * i, j)
                act.wait_ge(k_zeroed, s + 1)
                for g in range(KV_HEADS):
                    m = base + 2 * FT + g
                    split_w(s, m + 1, (m + 1) % 2)
                    act.wait_ge(w_used, made(m))
                    for odd in range(2):
                        rows = slice(64 * odd, 64 * odd + 64)
                        a = act.activation(k_half[rows, g, odd, :], ps[rows, 4 + g, :], ACT.Copy)
                    a.then_inc(fqk_copied, 1)
                split_w(s, base + V_TILE + 1, (base + V_TILE + 1) % 2)
                act.wait_ge(w_used, made(base + V_TILE))
                act.activation(v_t[:], ps[:, 3, :], ACT.Copy).then_inc(v_t_copied, 1)
                if s:
                    act.wait_ge(early_moved, NT)
                def exps(u):
                    w = P * len(key_tiles(u // 2))
                    act.wait_ge(max_made, UNITS * s + u + 1)
                    for h in range(Q_GROUP):
                        act.activation(probs[:, u % 2, h, 0:w], probs[:, u % 2, h, 0:w], ACT.Exp,
                                       bias=neg_max[:, u % 2, h:h + 1], accum_out=row_sum[:, u % 2, h:h + 1])
                    act.activation(sink_ex[:, u % 2, :], sink_ex[:, u % 2, :], ACT.Exp).then_inc(exp_made, 1)

                def outputs_hi(u):
                    g, blk = u % 2, u // 2
                    act.wait_ge(o_ps, UNITS * s + u + 1)
                    for half in range(2):
                        rows = slice(64 * half, 64 * half + 64)
                        act.activation(o_hi[rows, 2 * g:2 * g + 2, cols_of(blk)],
                                       ps[rows, 3, :].rearrange("p (a b q) -> p a b q", a=2, b=2)[:, :, half, :], ACT.Copy).then_inc(o_hi_made, 1)

                for n in range(2 * NT):
                    tt, ch = n // 2, n % 2
                    if n == 2 * NT - 2:
                        exps(0)
                    act.wait_ge(pq_ps, 2 * NT * s + n + 1)
                    act.activation(pq[:, tt, :, 256 * ch:256 * ch + 256].rearrange("p q (c f) -> p c q f", c=2),
                                   ps[:, 4 + n % 4, :].rearrange("p (c q f) -> p c q f", c=2, q=2), ACT.Copy).then_inc(pq_copied, 1)

                for u in range(UNITS):
                    act.wait_ge(pt_ps, UNITS * s + u + 1)
                    if u:
                        act.wait_ge(o_ps, UNITS * s + u)
                    nk = len(key_tiles(u // 2))
                    for k in range(nk):
                        a = act.activation(probs_t[:, k, :], ps[:, 4 + k, :], ACT.Copy)
                    a.then_inc(pt_copied, 1)
                    if u + 1 < UNITS:
                        exps(u + 1)
                    if u % 2:
                        c = u // 2
                        act.wait_ge(fm_ps, FT * s + c + 1)
                        act.activation(fm_hi[:, c, :], ps[:, 7, :], ACT.Copy).then_inc(fm_hi_made, 1)
                    outputs_hi(u)

                for i in range(KD // 2):
                    for j in range(2):
                        m = base + MERGE_AT + 3 * j
                        for gate in range(2):
                            split_w(s, 6 * i + m + gate + 1, (m + gate + 1) % 2)
                            act.wait_ge(w_used, made(6 * i + m + gate))
                            if gate == 0:
                                act.wait_ge(m_lo_made, s * KD + 2 * i + j + 1)
                            act.activation(sig[:, j, gate, :], ps[:, 4 * j + gate, :], ACT.Sigmoid).then_inc(sig_made, 1)
                        split_w(s, 6 * i + m + 3, (m + 3) % 2)
                        act.wait_ge(merged_made, s * KD + 2 * i + j + 1)
                        act.activation(m_hi[:, bass.ds(2 * i + j, 1), :].rearrange("p a t -> p (a t)"), merged[:, j, :], ACT.Copy).then_inc(m_hi_made, 1)
                for m in range(base + OUT_AT, base + QUERY_AT):
                    split_w(s, m + 1, (m + 1) % 2)
                norm(nth_norm(s, 1), turns=2 * s + 1, splits=((2, s, base + QUERY_AT + 1),))

                def query(n, j):
                    m = base + QUERY_AT + j
                    if not isinstance(n, int) or n + j:
                        split_w(s, m + 1 + n, (m + 1) % 2)
                    act.wait_ge(w_used, made(m + n))
                    act.wait_ge(key_ps, SIDES * s + n + j + 1)
                    act.activation(q_t[:, j, :], ps[:, 4 + j, :], ACT.Copy).then_inc(q_copied, 1)
                act.wait_ge(keys_in, 16 * (s + 1))
                for j in range(2):
                    query(0, j)
                with act.Fori(1, SIDES // 2) as i:
                    for j in range(2):
                        query(2 * i, j)
                act.wait_ge(pt_in, 16 * (s + 1))
                act.activation(pt_hi[:], pt_raw[:], ACT.Copy).then_inc(pt_hi_made, 1)
                e0 = s * EXPERT_TILES
                mu = base + LAYER_TILES

                def split_u(n, e):
                    act.wait_ge(u_in[e % DEEP], deep_landed(e0 + n + e, e % DEEP))
                    act.wait_ge(w_used, slot_free(mu + n + e))
                    act.activation(w_hi[:, (mu + e) % 2, :], u_raw[:, e % DEEP, :], ACT.Copy).then_inc(w_hi_made, 1)

                for half in range(2):
                    m = base + PLE_AT + 5 * half
                    for k in range(5):
                        if half and k == 4:
                            split_u(0, 0)
                        else:
                            split_w(s, m + k + 1, (m + k + 1) % 2)
                        if k == 4:
                            act.wait_ge(w_used, made(m + k - 1))
                            if half:
                                act.wait_ge(ple_read, 2 * s + 1)
                            act.activation(sig_p[:], ps[:, 0:4, :], ACT.Sigmoid).then_inc(sig_p_made, 1)
                def gelu(n, e):
                    act.wait_ge(w_used, made(mu + n + e))
                    act.wait_ge(act_stored[e % DEEP], slot_left(e0 + n + e, e % DEEP))
                    act.activation(act_t[:, e % DEEP, :], ps[:, e % 2, :], ACT.Gelu).then_inc(act_made, 1)

                def first_pass(n, e, last=False):
                    if not last:
                        split_u(n, e + 1)
                    gelu(n, e)

                def take_tile(tt):
                    act.wait_ge(key_copied, 2 + SIDES * (s + 1))
                    if s or tt:
                        act.wait_ge(tile_read, NT * s + tt)
                    act.activation(tile_sc[:], score[:, tt, :, :], ACT.Copy).then_inc(tile_copied, 1)

                def chosen_out(tt):
                    act.wait_ge(chosen_ps, NT * s + tt + 1)
                    act.activation(all_t[:, :, cols_of(tt)], ps[:, 2, 0:3 * P].rearrange("p (a t) -> p a t", a=3), ACT.Copy).then_inc(chosen_copied, 1)

                first_pass(0, 0)
                act.wait_ge(ple_added, 2 * (s + 1))
                take_tile(0)
                first_pass(0, 1)
                def gate_exps(tt):
                    act.wait_ge(gate_x_made, NT * s + tt + 1)
                    act.activation(gate_e[:], gate_x[:], ACT.Exp).then_inc(gate_e_made, 1)

                for tt in range(NT):
                    for part, (first, last) in enumerate(CHOICE_PAIRS):
                        for e in range(2 if tt == 0 and part == 0 else 2 * first, 2 * last):
                            first_pass(0, CHOICE_TILES * tt + e)
                        if part == 0 and tt:
                            chosen_out(tt - 1)
                        if part == 0 and tt + 1 < NT:
                            take_tile(tt + 1)
                        if part == 1:
                            gate_exps(tt)
                for e in range(SETTLE_TILES):
                    first_pass(NT * CHOICE_TILES, e)
                    if e == 1:
                        chosen_out(NT - 1)
                with act.Fori(0, NT) as tt:
                    n = SPREAD_AT + LOOP_TILES * tt

                    def gates_out(at):
                        done = NT * BATCHES * s + BATCHES * tt + at
                        act.wait_ge(hot_used, 2 + done + 1)
                        act.wait_ge(g_stored, 16 * G_PIECES * (NT * s + tt) + 16)
                        for half in range(2):
                            t0 = BATCH * at + 4 * half
                            act.activation(g_tile[:, :, t0:t0 + 4].rearrange("p i t -> p t i"),
                                           ps[:, 4 + 2 * (at % 2) + half, :].rearrange("p (t i) -> p t i", t=4), ACT.Copy).then_inc(g_copied, 1)

                    for group in range(GROUPS):
                        for e in range(GROUP_TILES):
                            split_u(n, GROUP_TILES * group + e + 1)
                            gates_out(GROUP_BATCHES * group + e)
                            gelu(n, GROUP_TILES * group + e)
                        gates_out(GROUP_BATCHES * group + GROUP_BATCHES - 1)
                    for e in range(MIXED, LOOP_TILES):
                        first_pass(n, e)
                for e in range(EXPERT_TILES - LAST_AT - 2):
                    first_pass(LAST_AT, e)

                def second_pass(n, k):
                    act.wait_ge(v_in[k % DEEP], deep_landed(e0 + n + k, k % DEEP))
                    act.wait_ge(down_done, e0 + n + k + 1)
                    act.activation(v_hi[:, k % 2, :], v_raw[:, k % DEEP, :], ACT.Copy).then_inc(v_hi_made, 1)
                    act.wait_ge(ga_made, 2 + e0 + n + k + 1)
                    act.activation(a_hi[:, k % 2, :], ga[:, k % 2, :], ACT.Copy).then_inc(a_hi_made, 1)

                first_pass(LAST_AT, EXPERT_TILES - LAST_AT - 2)
                second_pass(0, 0)
                first_pass(LAST_AT, EXPERT_TILES - LAST_AT - 1, last=True)
                for k in range(1, 2 * DEEP):
                    second_pass(0, k)
                if s + 1 < SEQS:
                    split_w(s + 1, base + STREAM, (base + STREAM) % 2)
                with act.Fori(2, EARLY_AT // DEEP) as i:
                    for k in range(DEEP):
                        second_pass(DEEP * i, k)
                for tt in range(NT):
                    second_pass(EARLY_AT, 2 * tt)
                    if s == 0:
                        deviation(nth_norm(1, 0), tt)
                    second_pass(EARLY_AT, 2 * tt + 1)
                with act.Fori((EARLY_AT + 2 * NT) // DEEP, EXPERT_TILES // DEEP) as i:
                    for k in range(DEEP):
                        second_pass(DEEP * i, k)
                if s == SEQS - 1:
                    norm(nth_norm(s, 2))

        @block.gpsimd
        def _(pool):
            for half in range(2):
                pool.sem_inc(w_lo_made[half], 2)
                pool.sem_inc(v_lo_made[half], 2)

            def split(where, lo, hi, raw, made_):
                for half in range(2):
                    here = slice(half * T, (half + 1) * T)
                    pool.tensor_tensor(lo[:, where, here], raw[:, here], hi[:, where, here].bitcast(F32), ALU.subtract).then_inc(made_[half], 1)

            def split_w(m, slot):
                pool.wait_ge(w_hi_made, m + 1)
                split(slot, w_lo, w_hi, w_raw[:, slot, :], w_lo_made)

            for s in range(SEQS):
                e0, first, mu = s * EXPERT_TILES, s * STREAM + (1 if s else 0), s * STREAM + LAYER_TILES
                with pool.Fori(0, (mu - first) // 2) as i:
                    for j in range(2):
                        split_w(2 * i + first + j, (first + j) % 2)
                if (mu - first) % 2:
                    split_w(mu - 1, (mu - 1) % 2)
                with pool.Fori(0, EXPERT_TILES // DEEP) as i:
                    for e in range(DEEP):
                        pool.wait_ge(w_hi_made, DEEP * i + mu + e + 1)
                        split((mu + e) % 2, w_lo, w_hi, u_raw[:, e, :], w_lo_made)

                def split_v(n, e):
                    pool.wait_ge(v_hi_made, n + e0 + e + 1)
                    split(e % 2, v_lo, v_hi, v_raw[:, e, :], v_lo_made)

                with pool.Fori(0, 2) as i:
                    for e in range(DEEP):
                        split_v(DEEP * i, e)
                if s + 1 < SEQS:
                    split_w(mu + EXPERT_TILES, (mu + EXPERT_TILES) % 2)
                with pool.Fori(2, EXPERT_TILES // DEEP) as i:
                    for e in range(DEEP):
                        split_v(DEEP * i, e)

        @block.vector
        def _(dve):
            dve.sem_inc(m_lo_made, 2)
            dve.sem_inc(key_copied, 2)
            dve.sem_inc(ga_made, 2)

            def statistics(tt, half, where=resid):
                dve.bn_stats(bn[:, tt, half, :], where[:, tt, half * T:(half + 1) * T])

            def variance(tt):
                dve.drain()
                dve.bn_aggr(mv[:, tt, :], bn[:, tt, :, :].rearrange("p a b -> p (a b)"))
                dve.drain()
                dve.tensor_scalar(var_eps[:, tt:tt + 1], mv[:, tt, 1:2], LN_EPS, None, ALU.add).then_inc(var_made, 1)

            def normalised(use, tt, where=resid):
                dve.wait_ge(std_made, NT * use + tt + 1)
                dve.reciprocal(rstd[:, tt:tt + 1], std[:, tt:tt + 1])
                dve.wait_ge(gb_in, 32 * (use + 1))
                there = where[:, tt, :]
                dve.scalar_tensor_tensor(out=there, in0=there, scalar=mv[:, tt, 0:1], in1=ln_gb[:, 0, :], op0=ALU.subtract, op1=ALU.mult)
                dve.drain()
                dve.scalar_tensor_tensor(out=there, in0=there, scalar=rstd[:, tt:tt + 1], in1=ln_gb[:, 1, :],
                                         op0=ALU.mult, op1=ALU.add).then_inc(ln_done, 1)

            def turn(use, tt):
                for n in (2 * tt, 2 * tt + 1):
                    dve.wait_ge(xt_hi_made, 2 * NT * use + n + 1)
                    there = (slice(None), slice(4 * (n % 2), 4 * (n % 2) + 4), cols_of(tt))
                    dve.tensor_tensor(xt_lo[there], ps[:, n % 4, :].rearrange("p (k t) -> p k t", k=4),
                                      xt_hi[there].bitcast(F32), ALU.subtract).then_inc(xt_lo_made, 1)

            def norm(use, prepare, turns=None):
                prepare(0)
                variance(0)
                for tt in range(NT):
                    if tt + 1 < NT:
                        prepare(tt + 1)
                        variance(tt + 1)
                    normalised(use, tt)
                    if turns is not None and tt:
                        turn(turns, tt - 1)
                if turns is not None:
                    turn(turns, NT - 1)

            for s in range(SEQS):
                base = s * STREAM

                def input_in(tt, where=resid):
                    dve.wait_ge(x_in[tt], 16 * (s + 1 if where is resid else s + 2))
                    for half in range(2):
                        statistics(tt, half, where)

                if s == 0:
                    norm(nth_norm(0, 0), input_in, turns=0)
                    dve.wait_ge(consts_in, 48)
                else:
                    for tt in range(NT):
                        turn(2 * s, tt)
                    for tt in range(NT):
                        for half in range(2):
                            statistics(tt, half)
                        variance(tt)
                    for tt in range(NT):
                        normalised(nth_norm(s - 1, 2), tt)
                    for tt in range(NT):
                        dve.wait_ge(stored[tt], 16 * s)
                        dve.tensor_copy(resid[:, tt, :], early[:, tt, :]).then_inc(early_moved, 1)
                for g in range(KV_HEADS):
                    dve.memset(k_half[64:128, g, 0, :], 0.0)
                    d = dve.memset(k_half[0:64, g, 1, :], 0.0)
                d.then_inc(k_zeroed, 1)

                def scores(u):
                    g, blk = u % 2, u // 2
                    w = P * len(key_tiles(blk))
                    at = 0 if blk else P
                    dve.wait_ge(sc_ps, UNITS * s + u + 1)
                    if u >= 2:
                        dve.wait_ge(pt_ps, UNITS * s + u - 1)
                    dve.scalar_tensor_tensor(out=probs[:, u % 2, :, 0:w], in0=ps[:, 0:3, :].rearrange("p b n -> p (b n)")[:, 0:Q_GROUP * w].rearrange("p (h n) -> p h n", h=Q_GROUP), scalar=HEAD_DIM ** -0.5,
                                             in1=bias[:, Q_GROUP * g:Q_GROUP * g + Q_GROUP, at:at + w],
                                             op0=ALU.mult, op1=ALU.add).then_inc(sc_copied, 1)
                    dve.drain()
                    dve.tensor_reduce(row_max[:, u % 2, :], probs[:, u % 2, :, 0:w], AX_X, ALU.max)
                    dve.drain()
                    sk = sinks[:, Q_GROUP * g:Q_GROUP * g + Q_GROUP]
                    dve.tensor_tensor(row_max[:, u % 2, :], row_max[:, u % 2, :], sk, ALU.max)
                    dve.drain()
                    dve.tensor_scalar(neg_max[:, u % 2, :], row_max[:, u % 2, :], -1.0, None, ALU.mult)
                    dve.tensor_tensor(sink_ex[:, u % 2, :], sk, row_max[:, u % 2, :], ALU.subtract).then_inc(max_made, 1)

                def normalise(u):
                    w = P * len(key_tiles(u // 2))
                    dve.wait_ge(exp_made, UNITS * s + u + 1)
                    dve.tensor_tensor(row_inv[:, u % 2, :], row_sum[:, u % 2, :], sink_ex[:, u % 2, :], ALU.add)
                    dve.drain()
                    dve.reciprocal(row_inv[:, u % 2, :], row_inv[:, u % 2, :])
                    dve.drain()
                    for h in range(Q_GROUP):
                        d = dve.tensor_scalar(probs[:, u % 2, h, 0:w], probs[:, u % 2, h, 0:w], row_inv[:, u % 2, h:h + 1], None, ALU.mult)
                    d.then_inc(probs_made, 1)

                def outputs_lo(u):
                    g, blk = u % 2, u // 2
                    dve.wait_ge(o_hi_made, 2 * (UNITS * s + u + 1))
                    for half in range(2):
                        rows = slice(64 * half, 64 * half + 64)
                        dve.tensor_tensor(o_lo[rows, 2 * g:2 * g + 2, cols_of(blk)],
                                          ps[rows, 3, :].rearrange("p (a b q) -> p a b q", a=2, b=2)[:, :, half, :],
                                          o_hi[rows, 2 * g:2 * g + 2, cols_of(blk)].bitcast(F32), ALU.subtract).then_inc(o_lo_made, 1)

                dve.wait_ge(mix_in, 32 * (s + 1))
                scores(0)
                dve.wait_ge(v_ps, s + 1)
                for dup in range(2):
                    dve.tensor_copy(v_dup[:, :, :, dup, :], ps[:, 3, :].rearrange("p (t g d) -> p t g d", t=NT, g=KV_HEADS)).then_inc(v_copied, 1)
                for u in range(UNITS):
                    normalise(u)
                    if u:
                        outputs_lo(u - 1)
                    if u + 1 < UNITS:
                        scores(u + 1)
                    if u % 2:
                        c = u // 2
                        dve.wait_ge(fm_hi_made, FT * s + c + 1)
                        dve.tensor_tensor(fm_lo[:, c, :], ps[:, 7, :], fm_hi[:, c, :].bitcast(F32), ALU.subtract).then_inc(fm_lo_made, 1)
                outputs_lo(UNITS - 1)

                with dve.Fori(0, KD // 2) as i:
                    for j in range(2):
                        m = base + MERGE_AT + 3 * j
                        dve.wait_ge(w_used, made(6 * i + m + 2))
                        dve.wait_ge(sig_made, 2 * KD * s + 4 * i + 2 * j + 2)
                        for gate in range(2):
                            dve.tensor_tensor(gated[:, j, gate, :], ps[:, 4 * j + 2 + gate, :], sig[:, j, gate, :], ALU.mult)
                        dve.drain()
                        dve.tensor_tensor(merged[:, j, :], gated[:, j, 0, :], gated[:, j, 1, :], ALU.add).then_inc(merged_made, 1)
                        dve.wait_ge(m_hi_made, KD * s + 2 * i + j + 1)
                        there = m_hi[:, bass.ds(2 * i + j, 1), :].rearrange("p a t -> p (a t)")
                        dve.tensor_tensor(m_lo[:, bass.ds(2 * i + j, 1), :].rearrange("p a t -> p (a t)"), merged[:, j, :],
                                          there.bitcast(F32), ALU.subtract).then_inc(m_lo_made, 1)
                def mixed_in(tt, half):
                    there = resid[:, tt, half * T:(half + 1) * T]
                    dve.scalar_tensor_tensor(out=there, in0=there, scalar=ALPHA, in1=ps[:, 4 * half + tt, :], op0=ALU.mult, op1=ALU.add)
                    dve.drain()
                    statistics(tt, half)

                dve.wait_ge(w_used, made(base + OUT_AT + 3))
                for tt in range(NT):
                    mixed_in(tt, 0)
                dve.wait_ge(w_used, made(base + OUT_AT + 7))
                norm(nth_norm(s, 1), lambda tt: mixed_in(tt, 1), turns=2 * s + 1)
                for tt in range(NT):
                    dve.tensor_scalar(resid[:, tt, :], resid[:, tt, :], ALPHA, None, ALU.mult)

                def scores_out(n, j):
                    dve.wait_ge(key_ps, 2 + SIDES * s + n + j + 1)
                    dve.tensor_copy(score[:, :, bass.ds(n + j, 1), :].rearrange("p t a n -> p t (a n)"),
                                    ps[:, 6 + j, :].rearrange("p (t n) -> p t n", t=NT)).then_inc(key_copied, 1)

                dve.wait_ge(keys_in, 16 * (s + 1))
                with dve.Fori(0, SIDES // 2) as i:
                    for j in range(2):
                        scores_out(2 * i, j)

                dve.wait_ge(pt_hi_made, s + 1)
                dve.tensor_tensor(pt_lo[:], pt_raw[:], pt_hi[:].bitcast(F32), ALU.subtract).then_inc(pt_lo_made, 1)
                for half in range(2):
                    m = base + PLE_AT + 5 * half
                    dve.wait_ge(w_used, made(m + 4))
                    dve.wait_ge(sig_p_made, 2 * s + half + 1)
                    for tt in range(NT):
                        d = dve.tensor_tensor(ple_t[:, tt, :], sig_p[:, tt, :], ps[:, 4 + tt, :], ALU.mult)
                    d.then_inc(ple_read, 1)
                    dve.drain()
                    there = resid[:, :, half * T:(half + 1) * T]
                    dve.tensor_tensor(there, there, ple_t[:], ALU.add).then_inc(ple_added, 1)
                    dve.drain()
                dve.wait_ge(ple_added, 2 * (s + 1))

                for tt in range(NT):
                    dve.wait_ge(tile_copied, NT * s + tt + 1)
                    for r in range(SIDES):
                        dve.max(out=top_v[:, r, 0:8], in_=tile_sc[:, r, :])
                    dve.drain()
                    for r in range(SIDES):
                        dve.max_index(out=top_i[:, r, 0:8], in_max=top_v[:, r, 0:8], in_values=tile_sc[:, r, :])
                        d = dve.match_replace(out=rest_sc[:, r, :], in_to_replace=top_v[:, r, 0:8], in_values=tile_sc[:, r, :], imm_value=LOWEST)
                    d.then_inc(tile_read, 1)
                    dve.drain()
                    for r in range(SIDES):
                        dve.max(out=top_v[:, r, 8:16], in_=rest_sc[:, r, :])
                    dve.drain()
                    for r in range(SIDES):
                        dve.max_index(out=top_i[:, r, 8:16], in_max=top_v[:, r, 8:16], in_values=rest_sc[:, r, :])
                    pairs = top_v[:, :, :].rearrange("p (h c) k -> p h c k", c=2)
                    dve.tensor_tensor(pair_sc[:].rearrange("p h (a b) -> p h a b", a=TOPK),
                                      pairs[:, :, 0, :].unsqueeze(3).to_broadcast([P, PEER_HEADS, TOPK, TOPK]),
                                      pairs[:, :, 1, :].unsqueeze(2).to_broadcast([P, PEER_HEADS, TOPK, TOPK]), ALU.add)
                    dve.drain()
                    dve.tensor_copy(top_f[:], top_i[:])
                    rest_pairs = rest_sc[:].rearrange("p (h a) n -> p h (a n)", a=2)
                    for h in range(PEER_HEADS):
                        dve.max(out=fin_v[:, h, 0:8], in_=pair_sc[:, h, :])
                    dve.drain()
                    for h in range(PEER_HEADS):
                        dve.max_index(out=fin_i[:, 16 * h:16 * h + 8], in_max=fin_v[:, h, 0:8], in_values=pair_sc[:, h, :])
                        dve.match_replace(out=rest_pairs[:, h, :], in_to_replace=fin_v[:, h, 0:8], in_values=pair_sc[:, h, :], imm_value=LOWEST)
                    dve.drain()
                    for h in range(PEER_HEADS):
                        dve.max(out=fin_v[:, h, 8:16], in_=rest_pairs[:, h, :])
                    dve.drain()
                    for h in range(PEER_HEADS):
                        dve.max_index(out=fin_i[:, 16 * h + 8:16 * h + 16], in_max=fin_v[:, h, 8:16], in_values=rest_pairs[:, h, :])
                    dve.tensor_tensor(gate_x[:], fin_v[:], fin_v[:, :, 0:1].to_broadcast([P, PEER_HEADS, TOPK]), ALU.subtract).then_inc(gate_x_made, 1)
                    dve.drain()
                    dve.tensor_scalar(pos_i[:, 0, :], fin_i[:], 4, None, ALU.logical_shift_right)
                    dve.tensor_scalar(pos_i[:, 1, :], fin_i[:], TOPK - 1, None, ALU.bitwise_and)
                    dve.drain()
                    dve.tensor_copy(pos_f[:], pos_i[:])
                    dve.drain()
                    if tt:
                        dve.wait_ge(chosen_ps, NT * s + tt)
                    for c in range(2):
                        hot = pair_sc[:] if c == 0 else rest_pairs
                        hot3 = hot.rearrange("p h (k a) -> p (h k) a", a=TOPK)
                        hot4 = hot.rearrange("p h (k a) -> p h k a", a=TOPK)
                        numbers = top_f[:, :, :].rearrange("p (h c) k -> p h c k", c=2)[:, :, c, :]
                        dve.tensor_tensor(hot3, pos_f[:, c, :].unsqueeze(2).to_broadcast([P, HK, TOPK]),
                                          iota[:, 0:TOPK].unsqueeze(1).to_broadcast([P, HK, TOPK]), ALU.is_equal)
                        dve.drain()
                        dve.tensor_tensor(hot4, hot4, numbers.unsqueeze(2).to_broadcast([P, PEER_HEADS, TOPK, TOPK]), ALU.mult)
                        dve.drain()
                        dve.tensor_reduce(chosen[:, c, :], hot3, AX_X, ALU.add)
                    dve.wait_ge(gate_e_made, NT * s + tt + 1)
                    dve.tensor_reduce(gate_s[:], gate_e[:], AX_X, ALU.add)
                    dve.drain()
                    dve.reciprocal(gate_r[:], gate_s[:])
                    dve.drain()
                    dve.tensor_tensor(chosen[:, 2, :].rearrange("p (h k) -> p h k", k=TOPK), gate_e[:],
                                      gate_r[:].unsqueeze(2).to_broadcast([P, PEER_HEADS, TOPK]), ALU.mult).then_inc(chosen_made, 1)
                dve.wait_ge(chosen_copied, NT * (s + 1))
                dve.tensor_copy(gate_hi[:], all_t[:, 2, :])
                dve.drain()
                dve.tensor_tensor(gate_lo[:], all_t[:, 2, :], gate_hi[:].bitcast(F32), ALU.subtract)
                dve.drain()
                with dve.Fori(0, NT * BATCHES // 2) as i:
                    for j in range(2):
                        def spread_out(values):
                            return values.unsqueeze(2).to_broadcast([P, BATCH, P])
                        t0 = 2 * BATCH * i + BATCH * j
                        numbers = iota[:].unsqueeze(1).to_broadcast([P, BATCH, P])
                        dve.wait_ge(hot_used, s * NT * BATCHES + 2 * i + j + 1)
                        dve.tensor_tensor(hot_row[:, j], spread_out(all_t[:, 0, bass.ds(t0, BATCH)]), numbers, ALU.is_equal)
                        dve.tensor_tensor(hot_col[:, j], spread_out(all_t[:, 1, bass.ds(t0, BATCH)]), numbers, ALU.is_equal)
                        dve.drain()
                        dve.tensor_tensor(gated_hi[:, j], hot_row[:, j], spread_out(gate_hi[:, bass.ds(t0, BATCH)].bitcast(F32)), ALU.mult)
                        dve.tensor_tensor(gated_lo[:, j], hot_row[:, j], spread_out(gate_lo[:, bass.ds(t0, BATCH)]), ALU.mult).then_inc(hot_made, 1)

                e0 = s * EXPERT_TILES

                def second_pass(n, k):
                    dve.wait_ge(act_back[k % DEEP], deep_landed(e0 + n + k, k % DEEP))
                    dve.wait_ge(g_back[k % DEEP], deep_landed(e0 + n + k, k % DEEP))
                    dve.tensor_tensor(ga[:, k % 2, :], act_in[:, k % DEEP, :], g_in[:, k % DEEP, :], ALU.mult).then_inc(ga_made, 1)
                    dve.wait_ge(a_hi_made, e0 + n + k + 1)
                    dve.tensor_tensor(a_lo[:, k % 2, :], ga[:, k % 2, :], a_hi[:, k % 2, :].bitcast(F32), ALU.subtract).then_inc(a_lo_made, 1)

                with dve.Fori(0, EARLY_AT // DEEP) as i:
                    for k in range(DEEP):
                        second_pass(DEEP * i, k)
                for tt in range(NT):
                    second_pass(EARLY_AT, 2 * tt)
                    if s == 0:
                        input_in(tt, early)
                        variance(tt)
                    second_pass(EARLY_AT, 2 * tt + 1)
                    if s == 0:
                        normalised(nth_norm(1, 0), tt, early)
                with dve.Fori((EARLY_AT + 2 * NT) // DEEP, EXPERT_TILES // DEEP) as i:
                    for k in range(DEEP):
                        second_pass(DEEP * i, k)

                def sums_in(tt):
                    for half in range(2):
                        o = 2 * tt + half
                        there = resid[:, tt, half * T:(half + 1) * T]
                        if o < OUTS - 1:
                            dve.wait_ge(out_ps, (OUTS - 1) * s + o + 1)
                        else:
                            dve.wait_ge(down_done, 2 + e0 + EXPERT_TILES)
                        dve.tensor_tensor(there, ps[:, o, :], there, ALU.add).then_inc(outs_added, 1)

                def experts_in(tt):
                    sums_in(tt)
                    dve.drain()
                    for half in range(2):
                        statistics(tt, half)

                if s == SEQS - 1:
                    norm(nth_norm(s, 2), experts_in)
                else:
                    for tt in range(NT):
                        sums_in(tt)

        @block.tensor
        def _(pe):
            pe.sem_inc(w_used, 2)
            pe.sem_inc(key_ps, 2)
            pe.sem_inc(hot_used, 2)
            pe.sem_inc(down_done, 2)

            def three(where, lh, ll, rh, rl, first, last):
                pe.matmul(where, lh, rh, start=first, stop=False)
                pe.matmul(where, lh, rl, start=False, stop=False)
                return pe.matmul(where, ll, rh, start=False, stop=last)

            def columns(where, m, slot, act_hi, act_lo, k0=0, kn=KD):
                for k in range(kn):
                    if k == 0 or k0 + k == KD // 2:
                        pe.wait_ge(w_lo_made[(k0 + k) // (KD // 2)], made(m))
                    w = slice((k0 + k) * P, (k0 + k + 1) * P)
                    mm = three(where, w_hi[:, slot, w], w_lo[:, slot, w], act_hi[:, k, :], act_lo[:, k, :], k == 0, k == kn - 1)
                return mm

            def rows(bank, m, slot, act_hi, act_lo, k0, first, last):
                for k in range(2):
                    pe.wait_ge(w_lo_made[k], made(m))
                    for tt in range(NT):
                        w = slice(k * T, (k + 1) * T)
                        mm = three(ps[:, bank + tt, :], act_hi[:, k0 + k, cols_of(tt)], act_lo[:, k0 + k, cols_of(tt)],
                                   w_hi[:, slot, w], w_lo[:, slot, w], first and k == 0, last and k == 1)
                return mm

            def half_columns(where, m, act_hi, act_lo, half):
                t = slice(half * T // 2, (half + 1) * T // 2)
                for k in range(KD):
                    if k % (KD // 2) == 0:
                        pe.wait_ge(w_lo_made[k // (KD // 2)], made(m))
                    w = slice(k * P, (k + 1) * P)
                    mm = three(where[:, t], w_hi[:, m % 2, w], w_lo[:, m % 2, w], act_hi[:, k, t], act_lo[:, k, t], k == 0, k == KD - 1)
                return mm

            def turn(use, nth, m, where=resid, last_sums=0):
                for tt in range(NT):
                    pe.wait_ge(ln_done, NT * nth + tt + 1)
                    for half in range(2):
                        n = 2 * tt + half
                        if n >= 4:
                            pe.wait_ge(xt_lo_made, 2 * NT * use + n - 3)
                        elif last_sums:
                            pe.wait_ge(outs_added, last_sums - OUTS + n + 1)
                        for k in range(4):
                            mm = pe.transpose(ps[:, n % 4, k * P:(k + 1) * P], where[:, tt, (4 * half + k) * P:(4 * half + k + 1) * P], ident[:])
                        mm.then_inc(xt_ps, 1)
                    if tt >= NT // 2:
                        if tt == NT // 2:
                            pe.wait_ge(xt_lo_made, 2 * NT * use + NT)
                            if last_sums:
                                pe.wait_ge(outs_added, last_sums)
                        j = tt - NT // 2
                        half_columns(ps[:, 4 + j, :], m + j, xt_hi, xt_lo, 0)
                pe.wait_ge(xt_lo_made, 2 * NT * (use + 1))
                for j in range(2):
                    half_columns(ps[:, 4 + j, :], m + j, xt_hi, xt_lo, 1).then_inc(w_used, 1)

            pe.wait_ge(consts_in, 48)
            for s in range(SEQS):
                base = s * STREAM
                if s == 0:
                    turn(0, nth_norm(0, 0), base)
                else:
                    turn(2 * s, nth_norm(s, 0), base, early, last_sums=OUTS * s)
                with pe.Fori(1, FQK_TILES // 2) as i:
                    for j in range(2):
                        m = base + j
                        pe.wait_ge(fqk_copied, FQK_TILES * s + 2 * i + j + 1)
                        columns(ps[:, 4 + j, :], 2 * i + m, m % 2, xt_hi, xt_lo).then_inc(w_used, 1)
                m = base + V_TILE
                columns(ps[:, 3, :], m, m % 2, xt_hi, xt_lo).then_inc(w_used, 1)

                def scores(u):
                    g, blk = u % 2, u // 2
                    seen = key_tiles(blk)
                    if u:
                        pe.wait_ge(sc_copied, UNITS * s + u)
                    for h in range(Q_GROUP):
                        head = Q_GROUP * g + h
                        at, end = h * P * len(seen), (h + 1) * P * len(seen)
                        key = seen[0] * P
                        while at < end:
                            n = min(end, (at // T + 1) * T) - at
                            mm = pe.matmul(ps[:, at // T, at % T:at % T + n], fqk[:, FT + head // 2, cols_of(blk)],
                                           k_half[:, g, head % 2, key:key + n], start=True, stop=True)
                            at, key = at + n, key + n
                    mm.then_inc(sc_ps, 1)

                def fourier_tokens(c, part):
                    if c == 0 and part == 0:
                        pe.wait_ge(dft_in, 16 * (s + 1))
                    if c and part == 0:
                        pe.wait_ge(fm_lo_made, FT * s + c)
                    for tt in range(NT):
                        mm = pe.matmul(ps[:, 7, :], pq[:, tt, part, cols_of(c)], dft[:, part, tt, :],
                                       start=(part == 0 and tt == 0), stop=(part == 1 and tt == NT - 1))
                    if part:
                        mm.then_inc(fm_ps, 1)

                pe.wait_ge(mix_in, 32 * (s + 1))
                pe.wait_ge(fqk_copied, 2 + FQK_TILES * (s + 1))
                scores(0)
                for n in range(2 * NT):
                    tt, ch = n // 2, n % 2
                    if n >= 4:
                        pe.wait_ge(pq_copied, 2 * NT * s + n - 3)
                    for c in range(2):
                        mm = pe.matmul(ps[:, 4 + n % 4, c * 2 * P:(c + 1) * 2 * P], fqk[:, 2 * ch + c, cols_of(tt)], gdft[:], start=True, stop=True)
                    mm.then_inc(pq_ps, 1)
                pe.wait_ge(v_t_copied, s + 1)
                for tt in range(NT):
                    mm = pe.transpose(ps[:, 3, cols_of(tt)], v_t[:, cols_of(tt)], ident[:])
                mm.then_inc(v_ps, 1)
                for u in range(UNITS):
                    if u + 1 < UNITS:
                        scores(u + 1)
                    if u == 0:
                        pe.wait_ge(pq_copied, 2 * NT * (s + 1))
                        pe.wait_ge(v_copied, 2 * (s + 1))
                    g, seen = u % 2, key_tiles(u // 2)
                    pe.wait_ge(probs_made, UNITS * s + u + 1)
                    if u:
                        pe.wait_ge(pt_copied, UNITS * s + u)
                    for k in range(len(seen)):
                        for h in range(Q_GROUP):
                            mm = pe.transpose(ps[:, 4 + k, cols_of(h)], probs[:, u % 2, h, k * P:(k + 1) * P], ident[:])
                    mm.then_inc(pt_ps, 1)
                    fourier_tokens(u // 2, u % 2)
                    pe.wait_ge(pt_copied, UNITS * s + u + 1)
                    if u:
                        pe.wait_ge(o_lo_made, 2 * (UNITS * s + u))
                    for k, b in enumerate(seen):
                        mm = pe.matmul(ps[:, 3, :], v_dup[:, b, g, :, :].rearrange("p a d -> p (a d)"), probs_t[:, k, :],
                                       start=(k == 0), stop=(k == len(seen) - 1))
                    mm.then_inc(o_ps, 1)

                with pe.Fori(0, KD // 2) as i:
                    for j in range(2):
                        m = base + MERGE_AT + 3 * j
                        pe.wait_ge(m_lo_made, KD * s + 2 * i + j + 1)
                        for gate in range(2):
                            columns(ps[:, 4 * j + gate, :], 6 * i + m + gate, (m + gate) % 2, xt_hi, xt_lo).then_inc(w_used, 1)
                        pe.wait_ge(fm_lo_made, FT * (s + 1))
                        pe.wait_ge(o_lo_made, 2 * UNITS * (s + 1))
                        columns(ps[:, 4 * j + 2, :], 6 * i + m + 2, (m + 2) % 2, fm_hi, fm_lo, 0, FT)
                        columns(ps[:, 4 * j + 3, :], 6 * i + m + 2, (m + 2) % 2, o_hi, o_lo, FT, FT).then_inc(w_used, 1)
                pe.wait_ge(m_lo_made, 2 + KD * (s + 1) - 1)
                for half in range(2):
                    for k in range(4):
                        m = base + OUT_AT + 4 * half + k
                        if half == 0 and k == 3:
                            pe.wait_ge(m_lo_made, 2 + KD * (s + 1))
                        rows(4 * half, m, m % 2, m_hi, m_lo, 2 * k, k == 0, k == 3).then_inc(w_used, 1)
                turn(2 * s + 1, nth_norm(s, 1), base + QUERY_AT)

                def query(n, j):
                    m = base + QUERY_AT + j
                    pe.wait_ge(q_copied, SIDES * s + n + j + 1)
                    columns(ps[:, 4 + j, :], m + n, m % 2, xt_hi, xt_lo).then_inc(w_used, 1)

                def key_scores(n, j):
                    pe.wait_ge(q_copied, 2 + SIDES * s + n + j + 1)
                    pe.wait_ge(key_copied, SIDES * s + n + j + 1)
                    for tt in range(NT):
                        mm = pe.matmul(ps[:, 6 + j, cols_of(tt)], q_t[:, j, cols_of(tt)],
                                       keys[:, bass.ds(n + j, 1), :].rearrange("p a n -> p (a n)"), start=True, stop=True)
                    mm.then_inc(key_ps, 1)

                pe.wait_ge(keys_in, 16 * (s + 1))
                key_scores(0, 0)
                query(2, 0)
                key_scores(0, 1)
                with pe.Fori(1, SIDES // 2 - 1) as i:
                    query(2 * i, 1)
                    key_scores(2 * i, 0)
                    query(2 * i + 2, 0)
                    key_scores(2 * i, 1)
                query(SIDES - 2, 1)
                key_scores(SIDES - 2, 0)
                key_scores(SIDES - 2, 1)

                pe.wait_ge(pt_lo_made, s + 1)
                pe.wait_ge(key_copied, 2 + SIDES * (s + 1))
                for half in range(2):
                    m = base + PLE_AT + 5 * half
                    if half:
                        pe.wait_ge(sig_p_made, 2 * s + 1)
                    for k in range(4):
                        rows(0, m + k, (m + k) % 2, xt_hi, xt_lo, 2 * k, k == 0, k == 3).then_inc(w_used, 1)
                    if half:
                        pe.wait_ge(ple_read, 2 * s + 1)
                    rows(4, m + 4, (m + 4) % 2, pt_hi, pt_lo, 0, True, True).then_inc(w_used, 1)

                e0 = s * EXPERT_TILES
                mu = base + LAYER_TILES
                pe.wait_ge(sig_p_made, 2 * (s + 1))

                def first_pass(n, e):
                    pe.wait_ge(act_made, e0 + n + e + 1)
                    columns(ps[:, e % 2, :], mu + n + e, (mu + e) % 2, xt_hi, xt_lo).then_inc(w_used, 1)

                def turn_chosen(tt):
                    pe.wait_ge(chosen_made, NT * s + tt + 1)
                    if tt:
                        pe.wait_ge(chosen_copied, NT * s + tt)
                    for k in range(3):
                        mm = pe.transpose(ps[:, 2, cols_of(k)], chosen[:, k, :], ident[:])
                    mm.then_inc(chosen_ps, 1)

                for tt in range(NT):
                    for part, (first, last) in enumerate(CHOICE_PAIRS):
                        with pe.Fori(first, last) as i:
                            for e in range(2):
                                first_pass(CHOICE_TILES * tt + 2 * i, e)
                        if part == 0 and tt:
                            turn_chosen(tt - 1)
                for n in range(0, SETTLE_TILES, 2):
                    for e in range(2):
                        first_pass(NT * CHOICE_TILES + n, e)
                    if n == 0:
                        turn_chosen(NT - 1)
                def mixed_group(n, done, group):
                    for step in range(GROUP_TILES * KD):
                        e, k = GROUP_TILES * group + step // KD, step % KD
                        at, nth = GROUP_BATCHES * group + step // SPAN, step % SPAN
                        if k == 0:
                            pe.wait_ge(act_made, e0 + n + e + 1)
                        if k % (KD // 2) == 0:
                            pe.wait_ge(w_lo_made[k // (KD // 2)], made(mu + n + e))
                        if nth == 0:
                            pe.wait_ge(hot_made, done + at + 1)
                            pe.wait_ge(g_copied, 2 * (done + at) + 2)
                        small = []
                        for b in range(nth * BATCH // SPAN, (nth + 1) * BATCH // SPAN):
                            where = ps[:, 4 + 2 * (at % 2) + b // 4, cols_of(b % 4)]
                            small.append((where, gated_hi[:, at % 2, b, :], b, True))
                            small.append((where, gated_lo[:, at % 2, b, :], b, False))
                        slot, w = (mu + e) % 2, slice(k * P, (k + 1) * P)
                        big = [(w_hi[:, slot, w], xt_hi[:, k, :]), (w_hi[:, slot, w], xt_lo[:, k, :]), (w_lo[:, slot, w], xt_hi[:, k, :])]
                        for p, (lhs, rhs) in enumerate(big):
                            mm = pe.matmul(ps[:, e % 2, :], lhs, rhs, start=(k == 0 and p == 0), stop=(k == KD - 1 and p == 2))
                            if k == KD - 1 and p == 2:
                                mm.then_inc(w_used, 1)
                            for where, rhs, b, hi in (small[p:p + 1] if p < 2 else small[2:]):
                                mm = pe.matmul(where, hot_col[:, at % 2, b, :], rhs, start=hi, stop=not hi)
                        if nth == SPAN - 1:
                            mm.then_inc(hot_used, 1)

                with pe.Fori(0, NT) as tt:
                    n = SPREAD_AT + LOOP_TILES * tt
                    for group in range(GROUPS):
                        mixed_group(n, NT * BATCHES * s + BATCHES * tt, group)
                    for e in range(MIXED, LOOP_TILES):
                        first_pass(n, e)
                with pe.Fori(0, (EXPERT_TILES - LAST_AT) // 2) as i:
                    for e in range(2):
                        first_pass(LAST_AT + 2 * i, e)

                pe.wait_ge(act_made, 2 + e0 + EXPERT_TILES)
                pe.wait_ge(g_copied, 4 + 2 * NT * BATCHES * (s + 1))

                def second_pass(n, slot, first=False, last=False):
                    pe.wait_ge(a_lo_made, e0 + n + 1)
                    if last:
                        pe.wait_ge(v_lo_made[1], 2 + e0 + n + 1)
                    for o in range(OUTS):
                        tt, half = (o // 2, o % 2) if last else (o % NT, o // NT)
                        if not last and o % NT == 0:
                            pe.wait_ge(v_lo_made[half], 2 + e0 + n + 1)
                        here = slice(half * T, (half + 1) * T)
                        mm = three(ps[:, 2 * tt + half, :], a_hi[:, slot, cols_of(tt)], a_lo[:, slot, cols_of(tt)],
                                   v_hi[:, slot, here], v_lo[:, slot, here], first, last)
                        if last and o < OUTS - 1:
                            mm.then_inc(out_ps, 1)
                    mm.then_inc(down_done, 1)

                second_pass(0, 0, first=True)
                second_pass(1, 1)
                with pe.Fori(0, EXPERT_TILES // 2 - 2) as i:
                    for slot in range(2):
                        second_pass(2 * i + 2 + slot, slot)
                second_pass(EXPERT_TILES - 2, 0)
                second_pass(EXPERT_TILES - 1, 1, last=True)


def _column_tile(np, w, columns):
    k = w.shape[0] // P
    return w[:, columns].reshape(k, P, -1).transpose(1, 0, 2).reshape(P, -1)


def _row_tile(np, w, k, half):
    return w[2 * k * P:2 * (k + 1) * P, half * T:(half + 1) * T].reshape(2, P, T).transpose(1, 0, 2).reshape(P, -1)


def _weight_stream(np, w_in, w_fo, w_ao, w_out, w_q, w_gate, w_proj):
    q0, k0, v0, g0 = FOURIER, 2 * FOURIER, 2 * FOURIER + KV_HEADS * HEAD_DIM, 2 * FOURIER + 2 * KV_HEADS * HEAD_DIM
    tiles = [_column_tile(np, w_in, np.arange(c * P, (c + 1) * P)) for c in range(2 * FT)]
    for g in range(KV_HEADS):
        head = np.arange(k0 + g * HEAD_DIM, k0 + (g + 1) * HEAD_DIM)
        tiles.append(_column_tile(np, w_in, np.concatenate([head, head])))
    tiles.append(_column_tile(np, w_in, np.arange(v0, g0)))
    for m in range(KD):
        here = np.arange(m * P, (m + 1) * P)
        tiles.append(_column_tile(np, w_in, g0 + here))
        tiles.append(_column_tile(np, w_in, g0 + D + here))
        tiles.append(np.concatenate([_column_tile(np, w_fo, here), _column_tile(np, w_ao, here)], axis=1))
    tiles += [_row_tile(np, w_out, k, half) for half in range(2) for k in range(KD // 2)]
    tiles += [_column_tile(np, w_q, np.arange(n * P, (n + 1) * P)) for n in range(SIDES)]
    for half in range(2):
        tiles += [_row_tile(np, w_gate, k, half) for k in range(KD // 2)]
        tiles.append(_row_tile(np, w_proj, 0, half))
    return np.stack(tiles)


def _constants(np):
    group = np.arange(GROUP_DIM)
    angle = 2 * np.pi * (np.outer(group, group) % GROUP_DIM) / GROUP_DIM
    norm = 1.0 / np.sqrt(T * GROUP_DIM)
    group_dft = np.zeros((P, 2 * P))
    for b in range(P // GROUP_DIM):
        at = slice(b * GROUP_DIM, (b + 1) * GROUP_DIM)
        group_dft[at, at] = np.cos(angle) * norm
        group_dft[at, P + b * GROUP_DIM:P + (b + 1) * GROUP_DIM] = np.sin(angle) * norm
    token = np.arange(T)
    angle = 2 * np.pi * (np.outer(token, token) % T) / T
    token_dft = np.stack([np.cos(angle), -np.sin(angle)])
    rel = np.abs(np.arange(P)[:, None] + P - np.arange(3 * P)[None, :])
    slopes = 2.0 ** (-8.0 * np.arange(1, HEADS + 1) / HEADS)
    bias = np.where(rel[:, None, :] <= WINDOW, -slopes[None, :, None] * rel[:, None, :], NEG_INF)
    iota = np.broadcast_to(np.arange(P), (P, P))
    return [a.astype(np.float32) for a in (np.eye(P), iota, group_dft, token_dft, bias)]


def kernel(x_prompt, x_sample, p_prompt, p_sample, emb_ln_g, emb_ln_b, w_in, attn_sink, w_fourier_out, w_attn_out,
           w_out, ln1_g, ln1_b, peer_w_q, peer_keys, peer_u, peer_v, ple_w_gate, ple_w_proj, ln2_g, ln2_b):
    import numpy as np
    import concourse.bacc as bacc
    from concourse.bass_utils import run_bass_kernel_spmd

    identity, key_iota, group_dft, token_dft, attn_bias = _constants(np)
    p_both = np.stack([np.asarray(p_prompt)[0, 0], np.asarray(p_sample)[0, 0]])
    ins = {
        "x": np.stack([np.asarray(x_prompt)[0], np.asarray(x_sample)[0]]),
        "p_t": p_both.reshape(SEQS, T, PLE // P, P).transpose(0, 3, 2, 1),
        "weights": _weight_stream(np, *(np.asarray(w)[0] for w in (w_in, w_fourier_out, w_attn_out, w_out, peer_w_q, ple_w_gate, ple_w_proj))),
        "u_t": np.asarray(peer_u)[0].reshape(NKEYS, P, KD, P).transpose(0, 3, 2, 1).reshape(NKEYS, P, D),
        "v_rows": np.asarray(peer_v)[0],
        "keys_t": np.asarray(peer_keys)[0].reshape(SIDES, NKEYS, P).transpose(2, 0, 1),
        "sink": np.asarray(attn_sink),
        "emb_g": np.asarray(emb_ln_g), "emb_b": np.asarray(emb_ln_b),
        "ln1_g": np.asarray(ln1_g)[0], "ln1_b": np.asarray(ln1_b)[0],
        "ln2_g": np.asarray(ln2_g)[0], "ln2_b": np.asarray(ln2_b)[0],
        "identity": identity, "key_iota": key_iota, "group_dft": group_dft, "token_dft": token_dft, "attn_bias": attn_bias,
    }
    nc = bacc.Bacc("TRN2", target_bir_lowering=False, num_devices=1)
    arrays = {f"in_{name}": np.ascontiguousarray(a) for name, a in ins.items()}
    args = [nc.dram_tensor(name, a.shape, mybir.dt.from_np(a.dtype), kind="ExternalInput").ap() for name, a in arrays.items()]
    out = nc.dram_tensor("out_y", (SEQS, T, D), F32, kind="ExternalOutput").ap()
    encoder(nc, *args, out)
    y = run_bass_kernel_spmd(nc, [arrays], core_ids=[0]).results[0]["out_y"]
    return y[0:1], y[1:2]
```
